# Optimizing a Trainium2 kernel written in Bass

```python
import jax, jax.numpy as jnp
from jax import lax
import numpy as np
import math

D_MODEL = 2048
BATCH = 1
SEQ = 256
DEPTH = 1

PLE_DIM = 256
A_HEADS = 16
A_KV_GROUPS = 4
A_REP = A_HEADS // A_KV_GROUPS
HEAD_DIM = 64
A_WIDTH = A_HEADS * HEAD_DIM
A_KV_WIDTH = A_KV_GROUPS * HEAD_DIM
CMP_LEN = 32
CMP_STRIDE = 16
CMP_RATIO = CMP_LEN // CMP_STRIDE
SEL_BLOCK = 64
SEL_TOP_N = 16
WINDOW = 512
Q_BLOCK = 128
FORCE_BONUS = 1000.0
B_WIDTH = D_MODEL // 2
B_GROUPS = 8
B_GROUP_DIM = B_WIDTH // B_GROUPS
B_CHUNK = 128
N_BRANCHES = 2
NEG = -1e30
EPS = 1e-6

IN_SPLITS = [A_WIDTH,
             6 * A_KV_WIDTH,
             3 * A_HEADS,
             A_WIDTH,
             2 * B_WIDTH,
             B_WIDTH,
             N_BRANCHES * D_MODEL]
IN_WIDTH = int(sum(IN_SPLITS))
SPLIT_IDX = [int(c) for c in np.cumsum(IN_SPLITS)[:-1]]


def rms_norm(x, g):
    xf = x.astype(jnp.float32)
    y = xf * lax.rsqrt(jnp.mean(xf * xf, axis=-1, keepdims=True) + EPS)
    return (y * g.astype(jnp.float32)).astype(x.dtype)

def layer_norm(x, g, b):
    xf = x.astype(jnp.float32)
    mu = jnp.mean(xf, axis=-1, keepdims=True)
    xc = xf - mu
    y = xc * lax.rsqrt(jnp.mean(xc * xc, axis=-1, keepdims=True) + EPS)
    return (y * g.astype(jnp.float32) + b.astype(jnp.float32)).astype(x.dtype)

def alibi_slopes():
    h = np.arange(1, A_HEADS + 1, dtype=np.float32)
    s = np.power(np.float32(2.0), -8.0 * h / A_HEADS).astype(np.float32)
    return jnp.asarray(s.reshape(A_KV_GROUPS, A_REP))

def compress(kv, pe, w1, w2):
    b, s, g, d = kv.shape
    ch = kv.reshape(b, s // CMP_STRIDE, CMP_STRIDE, g, d)
    nc = s // CMP_STRIDE - CMP_RATIO + 1
    blocks = jnp.concatenate([ch[:, r:nc + r] for r in range(CMP_RATIO)], axis=2)
    blocks = blocks + pe[None, None, :, None, :]
    hid = jax.nn.silu(jnp.einsum('bnlgd,lde->bnge', blocks, w1))
    return jnp.einsum('bnge,ef->bngf', hid, w2)

def nsa_attention(q, k_c, v_c, k_s, v_s, k_w, v_w, gate_logits,
                  pe_k, w1_k, w2_k, pe_v, w1_v, w2_v):
    b, s = q.shape[:2]
    q = q.reshape(b, s, A_KV_GROUPS, A_REP, HEAD_DIM)
    kc = compress(k_c, pe_k, w1_k, w2_k)
    vc = compress(v_c, pe_v, w1_v, w2_v)
    nc = kc.shape[1]
    c_end = jnp.arange(nc, dtype=jnp.int32) * CMP_STRIDE + (CMP_LEN - 1)
    ns = s // SEL_BLOCK
    n_top = min(SEL_TOP_N, ns)
    ci = np.arange(nc)[:, None]
    sj = np.arange(ns)[None, :]
    overlap = jnp.asarray(((CMP_STRIDE * ci < SEL_BLOCK * sj + SEL_BLOCK) &
                           (CMP_STRIDE * ci + CMP_LEN > SEL_BLOCK * sj)).astype(np.float32))
    kb = k_s.reshape(b, ns, SEL_BLOCK, A_KV_GROUPS, HEAD_DIM).transpose(0, 3, 1, 2, 4)
    vb = v_s.reshape(b, ns, SEL_BLOCK, A_KV_GROUPS, HEAD_DIM).transpose(0, 3, 1, 2, 4)
    kw = jnp.pad(k_w, ((0, 0), (WINDOW, 0), (0, 0), (0, 0)))
    vw = jnp.pad(v_w, ((0, 0), (WINDOW, 0), (0, 0), (0, 0)))
    slopes = alibi_slopes()
    gates = jax.nn.sigmoid(gate_logits.astype(jnp.float32)).reshape(b, s, 3, A_KV_GROUPS, A_REP)
    scale = HEAD_DIM ** -0.5
    gather = jax.vmap(jax.vmap(lambda blk, ix: blk[ix]))
    sel_off = jnp.arange(SEL_BLOCK, dtype=jnp.int32)
    win_off = jnp.arange(WINDOW + Q_BLOCK, dtype=jnp.int32)
    blk_ids = jnp.arange(ns, dtype=jnp.int32)

    def block_fn(i):
        q0 = i * Q_BLOCK
        qb = lax.dynamic_slice_in_dim(q, q0, Q_BLOCK, axis=1)
        gb = lax.dynamic_slice_in_dim(gates, q0, Q_BLOCK, axis=1)
        t = q0 + jnp.arange(Q_BLOCK, dtype=jnp.int32)
        dc = t[:, None] - c_end[None, :]
        vc_mask = dc >= 0
        sc = jnp.einsum('bqgrd,bngd->bgrqn', qb, kc).astype(jnp.float32) * scale
        sc = jnp.where(vc_mask, sc - slopes[:, :, None, None] * dc.astype(jnp.float32), NEG)
        p_c = jax.nn.softmax(sc, axis=-1) * vc_mask
        o_c = jnp.einsum('bgrqn,bngd->bqgrd', p_c.astype(vc.dtype), vc)
        imp = jnp.einsum('bgrqn,nj->bgqj', p_c, overlap)
        cur = t // SEL_BLOCK
        forced = ((blk_ids[None, :] == 0) | (blk_ids[None, :] == cur[:, None]) |
                  (blk_ids[None, :] == cur[:, None] - 1))
        causal = blk_ids[None, :] * SEL_BLOCK <= t[:, None]
        score = jnp.where(causal, imp + jnp.where(forced, FORCE_BONUS, 0.0), -1.0)
        _, idx = lax.top_k(score, n_top)
        ks = gather(kb, idx)
        vs = gather(vb, idx)
        pos = idx[..., None] * SEL_BLOCK + sel_off
        ds = (t[None, None, :, None, None] - pos)[:, :, None]
        ss = jnp.einsum('bqgrd,bgqnkd->bgrqnk', qb, ks).astype(jnp.float32) * scale
        ss = jnp.where(ds >= 0, ss - slopes[None, :, :, None, None, None] * ds.astype(jnp.float32), NEG)
        p_s = jax.nn.softmax(ss.reshape(b, A_KV_GROUPS, A_REP, Q_BLOCK, n_top * SEL_BLOCK), axis=-1)
        p_s = p_s.reshape(b, A_KV_GROUPS, A_REP, Q_BLOCK, n_top, SEL_BLOCK)
        o_s = jnp.einsum('bgrqnk,bgqnkd->bqgrd', p_s.astype(vs.dtype), vs)
        kwb = lax.dynamic_slice_in_dim(kw, q0, WINDOW + Q_BLOCK, axis=1)
        vwb = lax.dynamic_slice_in_dim(vw, q0, WINDOW + Q_BLOCK, axis=1)
        kp = q0 - WINDOW + win_off
        dw = t[:, None] - kp[None, :]
        vw_mask = (dw >= 0) & (dw < WINDOW) & (kp[None, :] >= 0)
        sw = jnp.einsum('bqgrd,bkgd->bgrqk', qb, kwb).astype(jnp.float32) * scale
        sw = jnp.where(vw_mask, sw - slopes[:, :, None, None] * dw.astype(jnp.float32), NEG)
        p_w = jax.nn.softmax(sw, axis=-1)
        o_w = jnp.einsum('bgrqk,bkgd->bqgrd', p_w.astype(vwb.dtype), vwb)
        o = (gb[:, :, 0, :, :, None] * o_c + gb[:, :, 1, :, :, None] * o_s +
             gb[:, :, 2, :, :, None] * o_w)
        return o.astype(q.dtype)

    out = lax.map(block_fn, jnp.arange(s // Q_BLOCK, dtype=jnp.int32))
    return out.transpose(1, 0, 2, 3, 4, 5).reshape(b, s, A_WIDTH)

def spatial_gating(uv, ln_g, ln_b, w_s, b_s):
    uv = jax.nn.gelu(uv)
    u, v = jnp.split(uv, 2, axis=-1)
    v = layer_norm(v, ln_g, ln_b)
    b, s, _ = v.shape
    v = v.reshape(b, s // B_CHUNK, B_CHUNK, B_GROUPS, B_GROUP_DIM)
    tril = jnp.tril(jnp.ones((B_CHUNK, B_CHUNK), dtype=w_s.dtype))
    sv = jnp.einsum('gts,bcsgd->bctgd', w_s * tril, v) + b_s.T[None, None, :, :, None]
    return u * sv.reshape(b, s, B_WIDTH)

def first_inputs(seed: int = 0) -> dict:
    key = jax.random.key(seed)
    ks = jax.random.split(key, 24)
    f32 = jnp.float32
    nrm = lambda k, shape, sc: jax.random.normal(k, shape, f32) * sc
    L = DEPTH
    return {
        "x": nrm(ks[0], (BATCH, SEQ, D_MODEL), 1.0),
        "p": nrm(ks[1], (DEPTH, BATCH, SEQ, PLE_DIM), 1.0),
        "norm_g": 1.0 + nrm(ks[2], (L, D_MODEL), 0.05),
        "w_in": nrm(ks[3], (L, D_MODEL, IN_WIDTH), D_MODEL ** -0.5),
        "cmp_pe_k": nrm(ks[4], (L, CMP_LEN, HEAD_DIM), 0.1),
        "cmp_w1_k": nrm(ks[5], (L, CMP_LEN, HEAD_DIM, HEAD_DIM), (CMP_LEN * HEAD_DIM) ** -0.5),
        "cmp_w2_k": nrm(ks[6], (L, HEAD_DIM, HEAD_DIM), HEAD_DIM ** -0.5),
        "cmp_pe_v": nrm(ks[7], (L, CMP_LEN, HEAD_DIM), 0.1),
        "cmp_w1_v": nrm(ks[8], (L, CMP_LEN, HEAD_DIM, HEAD_DIM), (CMP_LEN * HEAD_DIM) ** -0.5),
        "cmp_w2_v": nrm(ks[9], (L, HEAD_DIM, HEAD_DIM), HEAD_DIM ** -0.5),
        "ln_v_g": 1.0 + nrm(ks[10], (L, B_WIDTH), 0.05),
        "ln_v_b": nrm(ks[11], (L, B_WIDTH), 0.02),
        "sgu_w": nrm(ks[12], (L, B_GROUPS, B_CHUNK, B_CHUNK), B_CHUNK ** -0.5),
        "sgu_b": 1.0 + nrm(ks[13], (L, B_GROUPS, B_CHUNK), 0.05),
        "w_up_a": nrm(ks[14], (L, A_WIDTH, D_MODEL), A_WIDTH ** -0.5),
        "w_up_b": nrm(ks[15], (L, B_WIDTH, D_MODEL), B_WIDTH ** -0.5),
        "w_out": nrm(ks[16], (L, D_MODEL, D_MODEL), D_MODEL ** -0.5),
        "w_ple": nrm(ks[17], (L, PLE_DIM, D_MODEL), PLE_DIM ** -0.5),
        "w_ple_gate": nrm(ks[18], (L, D_MODEL, D_MODEL), D_MODEL ** -0.5),
        "final_g": 1.0 + nrm(ks[19], (D_MODEL,), 0.05),
    }

def first_block(x, p, norm_g, w_in, cmp_pe_k, cmp_w1_k, cmp_w2_k, cmp_pe_v, cmp_w1_v, cmp_w2_v,
              ln_v_g, ln_v_b, sgu_w, sgu_b, w_up_a, w_up_b, w_out, w_ple, w_ple_gate, final_g):
    b, s, _ = x.shape
    for l in range(DEPTH):
        h = rms_norm(x, norm_g[l])
        proj = h @ w_in[l]
        q, kv, g_logits, z_a, uv, z_b, merge_logits = jnp.split(proj, SPLIT_IDX, axis=-1)
        k_c, v_c, k_s, v_s, k_w, v_w = [t.reshape(b, s, A_KV_GROUPS, HEAD_DIM)
                                        for t in jnp.split(kv, 6, axis=-1)]
        o_a = nsa_attention(q, k_c, v_c, k_s, v_s, k_w, v_w, g_logits,
                            cmp_pe_k[l], cmp_w1_k[l], cmp_w2_k[l],
                            cmp_pe_v[l], cmp_w1_v[l], cmp_w2_v[l]) * jax.nn.silu(z_a)
        o_b = spatial_gating(uv, ln_v_g[l], ln_v_b[l], sgu_w[l], sgu_b[l]) * jax.nn.silu(z_b)
        g_a, g_b = jnp.split(jax.nn.sigmoid(merge_logits), 2, axis=-1)
        merged = g_a * (o_a @ w_up_a[l]) + g_b * (o_b @ w_up_b[l])
        x = x + merged @ w_out[l]
        x = x + jax.nn.sigmoid(x @ w_ple_gate[l]) * (p[l] @ w_ple[l])
    return rms_norm(x, final_g)


DEPTH_2 = 2

N_META = 16
GRID_W = 64
EPS_2 = 1e-5
N_EVEN = (DEPTH_2 + 1) // 2
N_ODD = DEPTH_2 // 2

SSD_HEAD_DIM = 64
SSD_WIDTH = D_MODEL
SSD_HEADS = SSD_WIDTH // SSD_HEAD_DIM
SSD_GROUPS = 8
SSD_STATE = 128
SSD_GN = SSD_GROUPS * SSD_STATE
SSD_CONV = 5
SSD_CONV_CH = SSD_WIDTH + 2 * SSD_GN
CHUNK = 128

CONV_WIDTH = D_MODEL
CONV_KERNEL = 31

IN_E_SIZES = (SSD_WIDTH,
              SSD_WIDTH,
              SSD_GN,
              SSD_GN,
              SSD_HEADS,
              SSD_HEADS,
              CONV_WIDTH,
              CONV_WIDTH,
              CONV_WIDTH)
IN_E = sum(IN_E_SIZES)
OUT_E = SSD_WIDTH + CONV_WIDTH

NA_HEAD_DIM = 64
NA_WIDTH = D_MODEL
NA_HEADS = NA_WIDTH // NA_HEAD_DIM
NA_KH = 8
NA_KW = 16
IN_O = 4 * NA_WIDTH


def split_cols(a, sizes):
    idx = [int(i) for i in np.cumsum(sizes)[:-1]]
    return jnp.split(a, idx, axis=-1)

def rmsnorm(x, g):
    xf = x.astype(jnp.float32)
    y = xf * lax.rsqrt(jnp.mean(xf * xf, axis=-1, keepdims=True) + EPS_2)
    return (y * g.astype(jnp.float32)).astype(x.dtype)

def layernorm(x, g, b):
    xf = x.astype(jnp.float32)
    mu = jnp.mean(xf, axis=-1, keepdims=True)
    var = jnp.mean(jnp.square(xf - mu), axis=-1, keepdims=True)
    y = (xf - mu) * lax.rsqrt(var + EPS_2)
    return (y * g.astype(jnp.float32) + b.astype(jnp.float32)).astype(x.dtype)

def depthwise_conv(x, w, b):
    y = lax.conv_general_dilated(
        x, w[:, None, :].astype(x.dtype), window_strides=(1,), padding="SAME",
        dimension_numbers=("NWC", "WIO", "NWC"), feature_group_count=x.shape[-1])
    return y + b.astype(x.dtype)

def ssd_scan(xdt, log_a, Bm, Cm):
    b, T, h, p = xdt.shape
    g, n = Bm.shape[2], Bm.shape[3]
    r = h // g
    c = T // CHUNK
    X = xdt.reshape(b, c, CHUNK, g, r, p)
    A = log_a.reshape(b, c, CHUNK, g, r).astype(jnp.float32)
    Bc = Bm.reshape(b, c, CHUNK, g, n)
    Cc = Cm.reshape(b, c, CHUNK, g, n)
    A_cs = jnp.cumsum(A, axis=2)
    tri = jnp.tril(jnp.ones((CHUNK, CHUNK), dtype=bool))[None, None, :, :, None, None]
    seg = A_cs[:, :, :, None] - A_cs[:, :, None, :]
    Lmat = jnp.exp(jnp.where(tri, seg, -jnp.inf))
    CB = jnp.einsum("bclgn,bcsgn->bclsg", Cc, Bc)
    Y_diag = jnp.einsum("bclsgr,bcsgrp->bclgrp", CB[..., None] * Lmat, X)
    Xd = X * jnp.exp(A_cs[:, :, -1:] - A_cs)[..., None]
    states = jnp.einsum("bclgn,bclgrp->bcgrpn", Bc, Xd)
    chunk_decay = jnp.exp(A_cs[:, :, -1])

    def step(carry, inp):
        st, dec = inp
        return carry * dec[..., None, None] + st, carry

    init = jnp.zeros((b, g, r, p, n), dtype=states.dtype)
    _, prev = lax.scan(step, init, (jnp.moveaxis(states, 1, 0), jnp.moveaxis(chunk_decay, 1, 0)))
    prev = jnp.moveaxis(prev, 0, 1)
    Y_off = jnp.einsum("bclgn,bcgrpn->bclgrp", Cc, prev) * jnp.exp(A_cs)[..., None]
    return (Y_diag + Y_off).reshape(b, T, h, p)

def ssd_mixer(xs, Bm, Cm, dt_f, dt_b, z, conv_w, conv_b, dt_bias, A_log, D_skip, norm_g):
    b, L, _ = xs.shape
    xbc = jax.nn.silu(depthwise_conv(jnp.concatenate([xs, Bm, Cm], axis=-1), conv_w, conv_b))
    xs, Bm, Cm = split_cols(xbc, (SSD_WIDTH, SSD_GN, SSD_GN))
    xh = xs.reshape(b, L, SSD_HEADS, SSD_HEAD_DIM)
    Bg = Bm.reshape(b, L, SSD_GROUPS, SSD_STATE)
    Cg = Cm.reshape(b, L, SSD_GROUPS, SSD_STATE)
    pad = (-L) % CHUNK

    def padl(a):
        return jnp.pad(a, [(0, 0), (pad, 0)] + [(0, 0)] * (a.ndim - 2))

    Bp, Cp = padl(Bg), padl(Cg)

    def direction(dt_raw, bias, a_log, reverse):
        dt = jax.nn.softplus(dt_raw.astype(jnp.float32) + bias.astype(jnp.float32))
        log_a = dt * (-jnp.exp(a_log.astype(jnp.float32)))
        xdt = xh.astype(jnp.float32) * dt[..., None]
        args = [padl(xdt), padl(log_a), Bp, Cp]
        if reverse:
            args = [jnp.flip(a, axis=1) for a in args]
        y = ssd_scan(*args)
        if reverse:
            y = jnp.flip(y, axis=1)
        return y[:, pad:]

    y = (direction(dt_f, dt_bias[0], A_log[0], False)
         + direction(dt_b, dt_bias[1], A_log[1], True)
         + D_skip.astype(jnp.float32)[:, None] * xh.astype(jnp.float32))
    y = y.reshape(b, L, SSD_WIDTH).astype(xs.dtype)
    return rmsnorm(y * jax.nn.silu(z), norm_g)

def conformer_conv(val, gate, dw_w, dw_b, ln_g, ln_b):
    u = val * jax.nn.sigmoid(gate)
    u = depthwise_conv(u, dw_w, dw_b)
    return jax.nn.silu(layernorm(u, ln_g, ln_b))

def neighbourhood_attention(q, k, v, rpb):
    b, L, h, d = q.shape
    S = L - N_META
    rows = S // GRID_W
    kh = min(NA_KH, rows)
    kw = NA_KW
    scale = d ** -0.5
    qm, km, vm = q[:, :N_META], k[:, :N_META], v[:, :N_META]
    qg = q[:, N_META:].reshape(b, rows, GRID_W, h, d)
    kg = k[:, N_META:].reshape(b, rows, GRID_W, h, d)
    vg = v[:, N_META:].reshape(b, rows, GRID_W, h, d)

    s_mm = jnp.einsum("bqhd,bkhd->bhqk", qm, km).astype(jnp.float32) * scale
    o_meta = jnp.einsum("bhqk,bkhd->bqhd", jax.nn.softmax(s_mm, axis=-1).astype(v.dtype), vm)

    col = np.arange(GRID_W)
    col_start = np.clip(col - kw // 2, 0, GRID_W - kw)
    col_mask = (col[None, :] >= col_start[:, None]) & (col[None, :] < col_start[:, None] + kw)
    col_idx = np.clip(col[None, :] - col[:, None] + NA_KW - 1, 0, 2 * NA_KW - 2)
    bias_cols = rpb[:, :, col_idx].astype(jnp.float32)

    def row_block(r):
        rs = jnp.clip(r - kh // 2, 0, rows - kh)
        k_rows = lax.dynamic_slice_in_dim(kg, rs, kh, axis=1)
        v_rows = lax.dynamic_slice_in_dim(vg, rs, kh, axis=1)
        q_row = lax.dynamic_index_in_dim(qg, r, axis=1, keepdims=False)
        s = jnp.einsum("bqhd,bjkhd->bhqjk", q_row, k_rows).astype(jnp.float32) * scale
        dr = rs + jnp.arange(kh) - r + NA_KH - 1
        bias = jnp.take(bias_cols, dr, axis=1)
        s = s + jnp.transpose(bias, (0, 2, 1, 3))[None]
        s = jnp.where(col_mask[None, None, :, None, :], s, -jnp.inf)
        s = s.reshape(b, h, GRID_W, kh * GRID_W)
        s_m = jnp.einsum("bqhd,bkhd->bhqk", q_row, km).astype(jnp.float32) * scale
        p = jax.nn.softmax(jnp.concatenate([s, s_m], axis=-1), axis=-1).astype(v.dtype)
        o = (jnp.einsum("bhqj,bjhd->bqhd", p[..., :kh * GRID_W], v_rows.reshape(b, kh * GRID_W, h, d))
             + jnp.einsum("bhqm,bmhd->bqhd", p[..., kh * GRID_W:], vm))
        return o

    o_grid = lax.map(row_block, jnp.arange(rows))
    o_grid = jnp.moveaxis(o_grid, 0, 1).reshape(b, S, h, d)
    return jnp.concatenate([o_meta, o_grid], axis=1)

def even_layer(h, norm_g, w_in, conv_w, conv_b, dt_bias, A_log, D_skip, ssd_norm_g,
               dw_w, dw_b, ln_g, ln_b, w_out):
    u = rmsnorm(h, norm_g)
    proj = jnp.einsum("bld,de->ble", u, w_in)
    z_a, xs, Bm, Cm, dt_f, dt_b, z_b, glu_v, glu_g = split_cols(proj, IN_E_SIZES)
    y_a = ssd_mixer(xs, Bm, Cm, dt_f, dt_b, z_a, conv_w, conv_b, dt_bias, A_log, D_skip, ssd_norm_g)
    y_b = conformer_conv(glu_v, glu_g, dw_w, dw_b, ln_g, ln_b) * jax.nn.silu(z_b)
    return h + jnp.einsum("ble,ed->bld", jnp.concatenate([y_a, y_b], axis=-1), w_out)

def odd_layer(h, norm_g, w_in, rpb, w_out):
    b, L, _ = h.shape
    u = rmsnorm(h, norm_g)
    proj = jnp.einsum("bld,de->ble", u, w_in)
    q, k, v, z = split_cols(proj, (NA_WIDTH,) * 4)
    shp = (b, L, NA_HEADS, NA_HEAD_DIM)
    o = neighbourhood_attention(q.reshape(shp), k.reshape(shp), v.reshape(shp), rpb)
    o = o.reshape(b, L, NA_WIDTH) * jax.nn.silu(z)
    return h + jnp.einsum("ble,ed->bld", o, w_out)

def second_inputs(seed: int = 0) -> dict:
    key = jax.random.key(seed)
    ks = jax.random.split(key, 24)
    f32 = jnp.float32
    ne, no = N_EVEN, N_ODD

    def nrm(k, shape, scale):
        return jax.random.normal(k, shape, f32) * scale

    dt0 = jnp.exp(jax.random.uniform(ks[6], (ne, 2, SSD_HEADS), f32, math.log(1e-3), math.log(1e-1)))
    return {
        "x": nrm(ks[0], (BATCH, SEQ, D_MODEL), 1.0),
        "meta_tokens": nrm(ks[1], (N_META, D_MODEL), 1.0),
        "e_norm_g": 1.0 + nrm(ks[2], (ne, D_MODEL), 0.02),
        "e_w_in": nrm(ks[3], (ne, D_MODEL, IN_E), D_MODEL ** -0.5),
        "e_conv_w": nrm(ks[4], (ne, SSD_CONV, SSD_CONV_CH), SSD_CONV ** -0.5),
        "e_conv_b": nrm(ks[5], (ne, SSD_CONV_CH), 0.02),
        "e_dt_bias": dt0 + jnp.log(-jnp.expm1(-dt0)),
        "e_A_log": jnp.log(jax.random.uniform(ks[7], (ne, 2, SSD_HEADS), f32, 1.0, 16.0)),
        "e_D": 1.0 + nrm(ks[8], (ne, SSD_HEADS), 0.1),
        "e_ssd_norm_g": 1.0 + nrm(ks[9], (ne, SSD_WIDTH), 0.02),
        "e_dw_w": nrm(ks[10], (ne, CONV_KERNEL, CONV_WIDTH), CONV_KERNEL ** -0.5),
        "e_dw_b": nrm(ks[11], (ne, CONV_WIDTH), 0.02),
        "e_ln_g": 1.0 + nrm(ks[12], (ne, CONV_WIDTH), 0.02),
        "e_ln_b": nrm(ks[13], (ne, CONV_WIDTH), 0.02),
        "e_w_out": nrm(ks[14], (ne, OUT_E, D_MODEL), OUT_E ** -0.5),
        "o_norm_g": 1.0 + nrm(ks[15], (no, D_MODEL), 0.02),
        "o_w_in": nrm(ks[16], (no, D_MODEL, IN_O), D_MODEL ** -0.5),
        "o_rpb": nrm(ks[17], (no, NA_HEADS, 2 * NA_KH - 1, 2 * NA_KW - 1), 0.1),
        "o_w_out": nrm(ks[18], (no, NA_WIDTH, D_MODEL), NA_WIDTH ** -0.5),
        "final_norm_g": 1.0 + nrm(ks[19], (D_MODEL,), 0.02),
    }

def second_block(x, meta_tokens, e_norm_g, e_w_in, e_conv_w, e_conv_b, e_dt_bias, e_A_log, e_D,
              e_ssd_norm_g, e_dw_w, e_dw_b, e_ln_g, e_ln_b, e_w_out,
              o_norm_g, o_w_in, o_rpb, o_w_out, final_norm_g):
    b = x.shape[0]
    meta = jnp.broadcast_to(meta_tokens.astype(x.dtype)[None], (b, N_META, x.shape[-1]))
    h = jnp.concatenate([meta, x], axis=1)
    for i in range(DEPTH_2):
        j = i // 2
        if i % 2 == 0:
            h = even_layer(h, e_norm_g[j], e_w_in[j], e_conv_w[j], e_conv_b[j], e_dt_bias[j],
                           e_A_log[j], e_D[j], e_ssd_norm_g[j], e_dw_w[j], e_dw_b[j],
                           e_ln_g[j], e_ln_b[j], e_w_out[j])
        else:
            h = odd_layer(h, o_norm_g[j], o_w_in[j], o_rpb[j], o_w_out[j])
    h = rmsnorm(h, final_norm_g)
    return h[:, N_META:]


def setup_inputs(seed=0):
    out = dict(first_inputs(seed))
    for name, value in second_inputs(seed + 1).items():
        if name != "x":
            out[name + "_2"] = value
    return out


def reference(
    x, p, norm_g, w_in, cmp_pe_k, cmp_w1_k, cmp_w2_k, cmp_pe_v, cmp_w1_v, cmp_w2_v, ln_v_g,
    ln_v_b, sgu_w, sgu_b, w_up_a, w_up_b, w_out, w_ple, w_ple_gate, final_g, meta_tokens_2,
    e_norm_g_2, e_w_in_2, e_conv_w_2, e_conv_b_2, e_dt_bias_2, e_A_log_2, e_D_2, e_ssd_norm_g_2,
    e_dw_w_2, e_dw_b_2, e_ln_g_2, e_ln_b_2, e_w_out_2, o_norm_g_2, o_w_in_2, o_rpb_2, o_w_out_2,
    final_norm_g_2,
):
    x = first_block(
        x, p, norm_g, w_in, cmp_pe_k, cmp_w1_k, cmp_w2_k, cmp_pe_v, cmp_w1_v, cmp_w2_v, ln_v_g,
        ln_v_b, sgu_w, sgu_b, w_up_a, w_up_b, w_out, w_ple, w_ple_gate, final_g,
    )
    return second_block(
        x, meta_tokens_2, e_norm_g_2, e_w_in_2, e_conv_w_2, e_conv_b_2, e_dt_bias_2, e_A_log_2,
        e_D_2, e_ssd_norm_g_2, e_dw_w_2, e_dw_b_2, e_ln_g_2, e_ln_b_2, e_w_out_2, o_norm_g_2,
        o_w_in_2, o_rpb_2, o_w_out_2, final_norm_g_2,
    )


_drawn_inputs = setup_inputs


def setup_inputs(seed=0):
    import zlib

    import numpy as np

    out = dict(_drawn_inputs(seed))
    spreads = {}
    factors = {'cmp_pe_k': 8.0,
     'cmp_w1_k': 3.673,
     'cmp_w2_k': 3.627,
     'cmp_pe_v': 5.703,
     'ln_v_g': 7.526,
     'ln_v_b': 8.0,
     'sgu_b': 4.974,
     'e_norm_g_2': 3.155,
     'e_conv_b_2': 3.18,
     'e_ssd_norm_g_2': 4.87,
     'e_dw_b_2': 7.323,
     'e_ln_g_2': 8.0,
     'e_ln_b_2': 8.0,
     'o_norm_g_2': 8.0,
     'o_rpb_2': 8.0,
     'final_norm_g_2': 22.166,
     'e_D_2': 37.911}
    for name, (base, spread) in spreads.items():
        noise = np.random.default_rng([zlib.crc32(name.encode()), seed]).standard_normal(out[name].shape)
        drawn = base * np.exp(spread * noise) if base else spread * noise
        out[name] = __import__('jax').numpy.asarray(drawn.astype(out[name].dtype))
    for name, factor in factors.items():
        out[name] = (out[name] * factor).astype(out[name].dtype)
    return out
```

```python
from contextlib import ExitStack, contextmanager

import concourse.bass as bass
from concourse import mybir

F = mybir.dt.float32
R = mybir.dt.float32r
ALU = mybir.AluOpType
ACT = mybir.ActivationFunctionType
AX = mybir.AxisListType
ds = bass.ds

P = 128
D = 2048
DT = D // P
S1 = 256
META = 16
T2 = S1 + META
HD = 64
NEG = -1e30

HEADS, GROUPS = 16, 4
CMP_LEN, CMP_STRIDE = 32, 16
NC = S1 // CMP_STRIDE - 1
AW = HEADS * HD
PLE = 256
BW = 1024
BG = 8
EPS1 = 1e-6
SH, SG, SN = 32, 8, 128
K5, K31 = 5, 31
EPS2 = 1e-5
GRID = 64
KH, KWIN = 4, 16

C_GATE = AW + 6 * GROUPS * HD
C_ZA = C_GATE + 3 * HEADS
C_UV = C_ZA + AW
C_ZB = C_UV + 2 * BW
C_MERGE = C_ZB + BW
E_Z, E_XS, E_BC, E_DT = 0, D, 2 * D, 3 * D
E_ZB = E_DT + 2 * SH
E_GV = E_ZB + D
E_GG = E_GV + D

(R_NORM, R_FINAL, R_ENORM, R_SSD, R_ONORM, R_FNORM, R_LNG, R_LNB, R_DWB, R_LNV) = range(10)
R_DW = 10
R_CW = R_DW + K31
R_CB = R_CW + 2 * K5
R_META = R_CB + 2
NROW = R_META + META

CH = 2048
RING = 4
SEED = 3

_STREAMS = [("qkv", 5, 20, 10), ("gate", 0, 1, 1), ("za", 2, 8, 4), ("uv", 4, 16, 8), ("zb", 2, 8, 4),
            ("merge", 8, 32, 16), ("upa", 2, 8, 8), ("upb", 2, 8, 8), ("ple", 0, 2, 8),
            ("out1", 4, 16, 8), ("pgate", 4, 16, 8),
            ("gv", 4, 16, 8), ("gg", 4, 16, 8), ("dt", 0, 1, 1), ("xs", 4, 16, 8), ("bc", 4, 16, 8),
            ("z2", 4, 16, 8), ("zb2", 4, 16, 8), ("oa", 4, 16, 8), ("ob", 4, 16, 8),
            ("v", 4, 16, 8), ("k", 4, 16, 8), ("q", 4, 16, 8), ("z3", 4, 16, 8), ("o3", 4, 16, 8)]


class Stream:
    def __init__(self, name, its, chunks, pairs, c0, p0):
        self.name, self.its, self.chunks, self.pairs, self.c0, self.p0 = name, its, chunks, pairs, c0, p0
        self.end = c0 + chunks
        self.ppi = pairs // its if its else pairs


ST = {}
_c = _p = 0
for _n, _i, _k, _q in _STREAMS:
    ST[_n] = Stream(_n, _i, _k, _q, _c, _p)
    _c += _k
    _p += _q
CHUNKS = _c

_SPLITS = [("h1", 4), ("oa1", 4), ("ob1", 4), ("p", 1), ("merged", 4), ("x1", 4), ("h2", 4), ("ya", 4),
           ("yb", 4), ("h3", 4), ("o3", 4)]
SPL = {}
_g = 0
for _n, _k in _SPLITS:
    SPL[_n] = (_g, _k)
    _g += _k


SSD_COLS = [(0, 0, 0, T2, 0), (0, 1, P, T2, 272), (1, 0, 0, P, 416), (1, 1, 0, 2 * P, 544),
            (0, 2, 2 * P, T2, 800), (1, 2, 0, T2, 816)]

TMPC = {"gg": 0, "z2": 8, "z3": 16}


class Steps:

    def __init__(self, eng, sem):
        self.eng, self.sem, self.n, self.it, self.per = eng, sem, 0, None, 0

    def do(self, ins):
        ins.then_inc(self.sem, 1)
        self.n += 1

    def sync(self):
        at = self.n
        if self.it is not None:
            at = self.it * self.per + (self.n - self.lo * self.per)
        self.eng.wait_ge(self.sem, at)

    @contextmanager
    def loop(self, lo, hi, per):
        start = self.n
        with self.eng.Fori(lo, hi) as it:
            self.it, self.per, self.lo = it, per, lo
            yield it
            assert self.n - start == per, f"{self.n - start} steps in an iteration"
        self.it = None
        self.n = start + per * (hi - lo)


def build(nc, A, out):
    with ExitStack() as ctx:
        def sb(name, shape, dt=F):
            return ctx.enter_context(nc.sbuf_tensor(name, shape, dt))

        sems = {}

        def S(name):
            if name not in sems:
                sems[name] = ctx.enter_context(nc.semaphore(name))
            return sems[name]

        raw = [sb(f"raw{i}", [P, CH]) for i in range(RING)]
        whi = [sb(f"whi{i}", [P, CH], R) for i in range(2)]
        wlo = [sb(f"wlo{i}", [P, CH], R) for i in range(2)]
        MH = sb("op_hi", [P, DT, T2], R)
        ML = sb("op_lo", [P, DT, T2], R)
        RES = sb("residual", [P, DT, T2])
        PC = sb("param_cols", [P, DT, NROW])
        ident = sb("ident", [P, P])
        ones = sb("ones", [P, P])
        triF = sb("tri_f", [P, P])
        triB = sb("tri_b", [P, P])
        rstd = sb("rstd", [P, T2])
        ms = sb("ms", [P, T2])
        slopes = sb("slopes", [P, HEADS])
        nslopes = sb("nslopes", [P, HEADS])
        gates = sb("gates", [P, 2, 3 * HEADS])
        small = sb("small", [P, 64])
        Dcol = sb("d_cols", [P, DT])
        AN = 20352
        arena = sb("arena", [P, AN])
        ps = ctx.enter_context(nc.psum_tensor("ps", [P, 8, 512], F))

        def ar(off, *dims):
            n = 1
            for d in dims:
                n *= d
            assert off + n <= AN, (off, dims)
            v = arena[:, off:off + n]
            if len(dims) == 1:
                return v
            names = "abcd"[:len(dims)]
            kw = {names[i]: dims[i] for i in range(len(dims))}
            return v.rearrange(f"p ({' '.join(names)}) -> p {' '.join(names)}", **kw)

        SQX = ar(16724, 2, 4, T2)
        xnat = ar(0, 2, D)
        PR = ar(11392, D)
        qkvT = ar(0, 20, S1)
        Vn = ar(5120, 2, 2, S1)
        KSg = ar(6144, 2, GROUPS, S1)
        QSg = ar(8192, 2, S1)
        SCb = ar(8704, 2, 384)
        Eb = ar(9472, 2, 384)
        PTb = ar(10240, 2, 384)
        DM = ar(11008, 384)
        ON = ar(11392, 2, AW)
        W1 = ar(6144, CMP_LEN, P)
        KB = ar(13440, 2, NC, CMP_LEN)
        KST = ar(13440, 2, S1)
        VCB = ar(14400, 2, 512)
        Pc = ar(15424, 2, HEADS, NC)
        PcT = ar(15904, 2, 2, P)
        BC = ar(16416, 2, HEADS, NC)
        MC = ar(16896, 2, HEADS, NC)
        KCD = ar(17376, GROUPS, NC)
        VCN = ar(17440, S1)
        hid = ar(17700, 2, NC)
        W2 = ar(17730, P)
        W2v = ar(17858, P)
        peT = ar(17990, 2, CMP_LEN)
        dcb = ar(18060, 2, NC)
        dc_i = ar(18100, 2 * NC)
        DMi = ar(18140, 384)
        cmx = ar(18540, 32)
        cz = ar(18580, 32)
        cco = ar(18620, 32)
        ZA = ar(0, 8, S1)
        UV = ar(2048, 16, S1)
        Vv = ar(4096, 8, S1)
        ZB = ar(6144, 8, S1)
        SQv = ar(8192, 8, S1)
        VN = ar(8192, 2, 8, P)
        SGB = ar(10240, 8, P)
        WS = ar(13440, 8, P)
        WST = ar(14464, 8, P)
        SGB2 = ar(15488, 2, S1)
        G = ar(8192, 32, S1)
        PLEb = ar(0, 16, S1)
        G2 = ar(4096, 16, S1)
        pnat = ar(16384, 2, PLE)
        pT = ar(16896, 2, S1)
        PH, PL = MH[:, 0:2, 0:S1], ML[:, 0:2, 0:S1]
        GU = ar(0, DT, T2)
        XBC = ar(4352, 32, T2)
        XS = ar(4352, DT, T2)
        ZB2 = ar(8704, DT, T2)
        q = 13056
        ROWS = ar(q, 2, 2, 2, T2)
        TRI = ar(q, 2, 3, T2)
        q += 2176
        SEG = ar(q, 2, 1088)
        q += 2176
        CBM = ar(q, 1088)
        q += 1088
        XST = ar(q, 2, T2)
        BS = ar(q + 2 * T2, T2)
        YN = ar(q, 3, S1)
        q += 3 * T2
        XNAT = ar(q, 3, S1)
        assert q + 768 <= AN
        dtN = sb("dt_nat", [P, 3, 2 * SH])
        cN = sb("cum_nat", [P, 3, 2 * SH])
        sp = [ar(15240 + 192 * i, 3, 2 * SH) for i in range(6)]
        aN = ar(15240 + 192 * 6, 3, 2 * SH)
        alog = ar(15240 + 192 * 7, 2 * SH)
        dtb = ar(15240 + 192 * 7 + 64, 2 * SH)
        CF = ar(13056 + 4352, 2, T2)
        TMP = ar(16724, 2, 2, T2)
        ACC = ar(20080, 1, T2)
        KT = ar(0, DT, T2)
        VO = ar(4352, 3, D)
        QO = ar(10496, DT, S1)
        q = 14592
        BIAS = ar(q, 2, 2, T2)
        SO = ar(q + 4 * T2, 2, 2, T2)
        q += 8 * T2
        PT1 = ar(q, 2, S1)
        PT2 = ar(q + 512, S1)
        QS = ar(q + 768, 2, S1)
        KS = ar(q + 1280, 2, T2)
        MW = ar(q + 1824, GRID)
        TAB = ar(14592, 7, P)
        onat = ar(0, 2, D)
        XF = ar(4352, DT, S1)

        tab_dram = nc.dram_tensor("rpb_table", [SH, 7, P], F, kind="Internal").ap()
        bias_dram = nc.dram_tensor("bias_by_column", [SH, GRID, 7, GRID], F, kind="Internal").ap()
        cum_dram = nc.dram_tensor("cum_rows", [2 * SH, T2], F, kind="Internal").ap()

        W_in = A["w_in"][0].rearrange("(t p) n -> p t n", p=P)
        W_ein = A["e_w_in_2"][0].rearrange("(t p) n -> p t n", p=P)
        W_eout = A["e_w_out_2"][0].rearrange("(t p) n -> p t n", p=P)
        W_oin = A["o_w_in_2"][0].rearrange("(t p) n -> p t n", p=P)
        W_oout = A["o_w_out_2"][0].rearrange("(t p) n -> p t n", p=P)
        W_up = {k: A[f"w_up_{k}"][0].rearrange("(t p) n -> p t n", p=P) for k in "ab"}
        W_out = A["w_out"][0].rearrange("(t p) n -> p t n", p=P)
        W_pg = A["w_ple_gate"][0].rearrange("(t p) n -> p t n", p=P)
        W_ple = A["w_ple"][0].rearrange("(t p) n -> p t n", p=P)
        SRC = {"qkv": (W_in, 0, 0), "za": (W_in, C_ZA, 0), "uv": (W_in, C_UV, 0), "zb": (W_in, C_ZB, 0),
               "merge": (W_in, C_MERGE, 0), "upa": (W_up["a"], 0, 0), "upb": (W_up["b"], 0, 0),
               "out1": (W_out, 0, 0), "pgate": (W_pg, 0, 0), "gv": (W_ein, E_GV, 0),
               "gg": (W_ein, E_GG, 0), "xs": (W_ein, E_XS, 0), "bc": (W_ein, E_BC, 0),
               "z2": (W_ein, E_Z, 0), "zb2": (W_ein, E_ZB, 0), "oa": (W_eout, 0, 0),
               "ob": (W_eout, 0, DT), "v": (W_oin, 2 * D, 0), "k": (W_oin, D, 0), "q": (W_oin, 0, 0),
               "z3": (W_oin, 3 * D, 0), "o3": (W_oout, 0, 0)}

        wide = [r[:, :].rearrange("p (t n) -> p t n", t=8) for r in raw]
        hi8 = [r[:, :].rearrange("p (t n) -> p t n", t=8) for r in whi]
        lo8 = [r[:, :].rearrange("p (t n) -> p t n", t=8) for r in wlo]
        landed = [S(f"chunk_landed_{i}") for i in range(RING)]
        hi_ready, lo_dve, lo_pool, chunk_done = S("hi_ready"), S("lo_dve"), S("lo_pool"), S("chunk_done")
        acc_free = S("acc_free")
        src_ready, mh_ready, ml_ready = S("src_ready"), S("mh_ready"), S("ml_ready")

        def lo_wait(eng, c0, it, upto):
            c = c0 + upto
            sem = lo_dve if c % 2 == 0 else lo_pool
            eng.wait_ge(sem, it * 2 + c // 2 + 1)

        def load_chunk(sp_eng, s, it, i, dst, src):
            c = s.c0 + i
            if not isinstance(it, int) or c + 4 * it >= RING:
                lo_wait(sp_eng, s.c0, it, i - RING)
            sp_eng.dma_start(dst, src).then_inc(landed[c % RING], 16)

        def load_stream(sp_eng, name, lo=0, hi=None):
            s = ST[name]
            w, col, row = SRC[name]
            per = s.chunks // s.pairs

            def body(it):
                for i in range(4):
                    r = row + 8 * (i % per)
                    at = it * (s.ppi * 256) + (col + 256 * (i // per))
                    cols = ds(at, 256) if not isinstance(at, int) else slice(at, at + 256)
                    load_chunk(sp_eng, s, it, i, wide[(s.c0 + i) % RING], w[:, r:r + 8, cols])

            if hi is None:
                hi = s.its
            if lo == 0 and s.c0 == 0:
                body(0)
                lo = 1
            if hi - lo == 1:
                body(lo)
            elif hi > lo:
                with sp_eng.Fori(lo, hi) as it:
                    body(it)

        def split_hi(act, s, it, i):
            c = s.c0 + i
            if isinstance(it, int) and c + 4 * it >= CHUNKS:
                return
            act.wait_ge(landed[c % RING], it * 16 + 16 * (c // RING + 1))
            if not isinstance(it, int) or c + 4 * it >= 2:
                act.wait_ge(chunk_done, it * 4 + c - 1)
            nc.scalar.activation(whi[c % 2][:, :], raw[c % RING][:, :], ACT.Copy).then_inc(hi_ready, 1)

        def split_lo(eng, s, it, i):
            c = s.c0 + i
            own = nc.vector if c % 2 == 0 else nc.gpsimd
            if isinstance(it, int) and c + 4 * it >= CHUNKS:
                return
            eng.wait_ge(hi_ready, it * 4 + c + 1)
            own.tensor_tensor(wlo[c % 2][:, :], raw[c % RING][:, :], whi[c % 2][:, :].bitcast(F),
                              ALU.subtract).then_inc(lo_dve if c % 2 == 0 else lo_pool, 1)

        def halves(eng, kind, s, it, i):
            if kind == "act":
                split_hi(eng, s, it, i)
            elif (kind == "dve") == ((s.c0 + i) % 2 == 0):
                split_lo(eng, s, it, i)

        def run_loop(eng, s, body, steps=None, per=0):
            hi = s.its - 1 if s.end == CHUNKS else s.its
            if steps is None:
                with eng.Fori(0, hi) as it:
                    body(it)
            else:
                with steps.loop(0, hi, per) as it:
                    body(it)
            if hi < s.its:
                body(hi)

        def stream_side(eng, kind, name, evac=None, steps=None, per=0, extra=None):
            s = ST[name]

            def body(it):
                n = s.ppi
                for i in range(4):
                    halves(eng, kind, s, it, i + 2)
                    if (i + 1) % (4 // n) == 0 and evac is not None:
                        j = (i + 1) // (4 // n) - 1
                        eng.wait_ge(chunk_done, it * 4 + s.c0 + i + 1)
                        evac(it, j, (s.p0 + j) % 2)
                if extra is not None:
                    extra(it)

            run_loop(eng, s, body, steps, per)

        def stream_pe(pe, name, NT=S1, off=0, tile0=0, need=None):
            s = ST[name]
            cpp = s.chunks // s.pairs
            if need is not None:
                pe.wait_ge(ml_ready, sum(SPL[need]))

            def body(it):
                for i in range(4):
                    c = s.c0 + i
                    j = i // cpp
                    b = 2 * ((s.p0 + j) % 2)
                    if i % cpp == 0:
                        pe.wait_ge(acc_free, it * s.ppi + s.p0 + j - 1 + SEED)
                    lo_wait(pe, s.c0, it, i)
                    for n in range(2):
                        for k in range(8):
                            t = tile0 + 8 * (i % cpp) + k
                            wh = hi8[c % 2][:, k, n * P:(n + 1) * P]
                            wl = lo8[c % 2][:, k, n * P:(n + 1) * P]
                            xh, xl = MH[:, t, off:off + NT], ML[:, t, off:off + NT]
                            o = ps[:, b + n, 0:NT]
                            first = i % cpp == 0 and k == 0
                            last = i % cpp == cpp - 1 and k == 7
                            nc.tensor.matmul(o, wh, xh, start=first, stop=False)
                            nc.tensor.matmul(o, wh, xl, start=False, stop=False)
                            mm = nc.tensor.matmul(o, wl, xh, start=False, stop=last)
                    mm.then_inc(chunk_done, 1)

            with pe.Fori(0, s.its) as it:
                body(it)

        def natural(pe, name, toks, n):
            s = ST[name]
            c = s.c0
            pe.wait_ge(acc_free, s.p0 - 1 + SEED)
            lo_wait(pe, c, 0, 0)
            wh = whi[c % 2][:, 0:DT * n].rearrange("p (t n) -> p t n", t=DT)
            wl = wlo[c % 2][:, 0:DT * n].rearrange("p (t n) -> p t n", t=DT)
            for i, (tok, m) in enumerate(toks):
                o = ps[0:m, 2 * (s.p0 % 2), n * i:n * i + n]
                for t in range(DT):
                    xh, xl = MH[:, t, tok:tok + m], ML[:, t, tok:tok + m]
                    nc.tensor.matmul(o, xh, wh[:, t, :], start=(t == 0), stop=False)
                    nc.tensor.matmul(o, xl, wh[:, t, :], start=False, stop=False)
                    mm = nc.tensor.matmul(o, xh, wl[:, t, :], start=False, stop=(t == DT - 1))
            mm.then_inc(chunk_done, 1)

        def pairof(par):
            return slice(2 * par, 2 * par + 2)

        def split_op_act(act, name, src, hi, per, free_at=0):
            g0, n = SPL[name]
            if free_at:
                act.wait_ge(chunk_done, free_at)
            for g in range(n):
                act.wait_ge(src_ready, g0 + g + 1)
                nc.scalar.activation(hi(g), src(g), ACT.Copy).then_inc(mh_ready, 1)

        def split_op_dve(dve, name, src, hi, lo, g):
            g0, n = SPL[name]
            dve.wait_ge(mh_ready, g0 + g + 1)
            nc.vector.tensor_tensor(lo(g), src(g), hi(g).bitcast(F), ALU.subtract).then_inc(ml_ready, 1)

        def op(t, NT, n=4, tile0=0, off=0):
            return lambda g: t[:, tile0 + n * g:tile0 + n * (g + 1), off:off + NT]

        norm_sq, norm_sqfree = S("norm_sq"), S("norm_sqfree")
        norm_sum, norm_ms, norm_rt = S("norm_sum"), S("norm_ms"), S("norm_rt")
        NORM = {n: i for i, n in enumerate(["h1", "fin1", "h2", "ya", "cf", "h3", "fin2"])}

        def norm_act(act, name, src, NT):
            e = NORM[name]
            for g in range(4):
                if e or g >= 2:
                    act.wait_ge(norm_sqfree, 4 * e + g - 1)
                nc.scalar.activation(SQX[:, g % 2, :, 0:NT], src(g), ACT.Square).then_inc(norm_sq, 1)
            act.wait_ge(norm_ms, e + 1)
            nc.scalar.activation(rstd[:, 0:NT], ms[:, 0:NT], ACT.Sqrt).then_inc(norm_rt, 1)

        def norm_pe(pe, name, NT, bank=4):
            e = NORM[name]
            for g in range(4):
                pe.wait_ge(norm_sq, 4 * e + g + 1)
                for t in range(4):
                    mm = nc.tensor.matmul(ps[:, bank, 0:NT], ones[:, :], SQX[:, g % 2, t, 0:NT],
                                          start=(g == 0 and t == 0), stop=(g == 3 and t == 3))
                mm.then_inc(norm_sqfree, 1)

        def norm_dve(dve, v, name, NT, eps, bank=4, width=D):
            e = NORM[name]
            dve.wait_ge(norm_sqfree, 4 * e + 4)
            nc.vector.tensor_scalar(ms[:, 0:NT], ps[:, bank, 0:NT], 1.0 / width, eps, ALU.mult,
                                    ALU.add).then_inc(norm_ms, 1)
            dve.wait_ge(norm_rt, e + 1)
            v.do(nc.vector.reciprocal(rstd[:, 0:NT], rstd[:, 0:NT]))
            v.sync()

        def apply_dve(dve, v, name, src, row, NT, off=0, dst=None):
            g0, _ = SPL[name]
            at = (lambda g: SQX[:, g % 2, :, 0:NT]) if dst is None else dst
            for g in range(5):
                if g < 4:
                    if g >= 2 and dst is None:
                        dve.wait_ge(ml_ready, g0 + g - 1)
                    for t in range(4):
                        ins = nc.vector.scalar_tensor_tensor(
                            out=at(g)[:, t, :], in0=src(g)[:, t, :], scalar=PC[:, 4 * g + t, row:row + 1],
                            in1=rstd[:, 0:NT], op0=ALU.mult, op1=ALU.mult)
                    ins.then_inc(src_ready, 1)
                if g >= 1:
                    split_op_dve(dve, name, at, op(MH, NT), op(ML, NT), g - 1)

        block = ctx.enter_context(nc.Block())

        @block.sync
        def _(sp_eng):
            nc.sync.dma_start(xnat, A["x"][0].rearrange("(t p) n -> p t n", p=P)).then_inc(S("x_landed"), 16)
            rows = [("norm_g", R_NORM), ("e_norm_g_2", R_ENORM), ("e_ssd_norm_g_2", R_SSD),
                    ("o_norm_g_2", R_ONORM), ("e_ln_g_2", R_LNG), ("e_ln_b_2", R_LNB), ("e_dw_b_2", R_DWB)]
            srcs = [(A[n], r, 1) for n, r in rows]
            srcs += [(A["final_g"].rearrange("(a n) -> a n", a=1), R_FINAL, 1),
                     (A["final_norm_g_2"].rearrange("(a n) -> a n", a=1), R_FNORM, 1),
                     (A["e_dw_w_2"][0], R_DW, K31),
                     (A["e_conv_w_2"][0].rearrange("k (h n) -> (k h) n", h=2), R_CW, 2 * K5),
                     (A["e_conv_b_2"].rearrange("a (h n) -> (a h) n", h=2), R_CB, 2),
                     (A["meta_tokens_2"], R_META, META)]
            for src, r, n in srcs:
                nc.sync.dma_start(PR[r:r + n, :], src).then_inc(S("params_landed"), 16)
            nc.sync.dma_start(PR[R_LNV:R_LNV + 1, 0:BW], A["ln_v_g"]).then_inc(S("params_landed"), 16)
            nc.sync.dma_start(PR[R_LNV:R_LNV + 1, BW:D], A["ln_v_b"]).then_inc(S("params_landed"), 16)
            load_stream(sp_eng, "qkv")
            s = ST["gate"]
            load_chunk(sp_eng, s, 0, 0, raw[s.c0 % RING][:, 0:DT * 48].rearrange("p (t n) -> p t n", t=DT),
                       W_in[:, :, C_GATE:C_ZA])
            for n in ("za", "uv", "zb", "merge", "upa", "upb"):
                load_stream(sp_eng, n)
            s = ST["ple"]
            for i in range(2):
                load_chunk(sp_eng, s, 0, i, raw[(s.c0 + i) % RING][:, :].rearrange("p (t n) -> p t n", t=2),
                           W_ple[:, :, 1024 * i:1024 * i + 1024])
            for n in ("out1", "pgate", "gv", "gg"):
                load_stream(sp_eng, n)
            s = ST["dt"]
            load_chunk(sp_eng, s, 0, 0, raw[s.c0 % RING][:, 0:DT * 64].rearrange("p (t n) -> p t n", t=DT),
                       W_ein[:, :, E_DT:E_ZB])
            for n in ("xs", "bc"):
                load_stream(sp_eng, n)
            load_stream(sp_eng, "z2", 0, 1)
            sp_eng.wait_ge(S("cum_rows_ready"), 2)
            for d in range(2):
                nc.sync.dma_start(cum_dram[d * SH:(d + 1) * SH, :], CF[0:SH, d, :]).then_inc(S("cum_stored"), 16)
            sp_eng.wait_ge(S("cum_stored"), 32)
            sp_eng.wait_ge(S("tri_free"), 1)
            with sp_eng.Fori(0, SG) as it:
                for hp in range(2):
                    sp_eng.wait_ge(S("rows_used"), it * 4 + 2 * hp - 2 + SEED)
                    src = bass.AP(cum_dram.tensor, it * (4 * T2) + hp * 2 * T2,
                                  [[0, P], [SH * T2, 2], [T2, 2], [1, T2]])
                    nc.sync.dma_start(ROWS[:, hp], src).then_inc(S(f"rows_landed_{hp}"), 16)
            load_stream(sp_eng, "z2", 1)
            for n in ("zb2", "oa", "ob", "v", "k", "q"):
                load_stream(sp_eng, n)
            load_stream(sp_eng, "z3", 0, 1)
            with sp_eng.Fori(0, SH // 2) as it:
                for e in range(2):
                    sp_eng.wait_ge(S("bias_used"), it * 2 + e - 1 + SEED)
                    for qt in range(2):
                        for r in range(2):
                            row = KH - 1 - 2 * qt - r
                            src = bias_dram[ds(it * 2 + e, 1), :, row:row + KH, :].rearrange("a q j c -> (a q) (j c)")
                            dst = BIAS[GRID * r:GRID * (r + 1), e, qt, META:T2]
                            nc.sync.dma_start(dst, src).then_inc(S(f"bias_landed_{e}"), 16)
            load_stream(sp_eng, "z3", 1)
            load_stream(sp_eng, "o3")
            sp_eng.wait_ge(S("out_ready"), 8)
            nc.sync.dma_start(out[0].rearrange("(t p) n -> p t n", p=P), onat).then_inc(S("out_stored"), 16)
            sp_eng.wait_ge(S("out_stored"), 16)

        @block.gpsimd
        def _(pool):
            g = Steps(pool, S("pool_step"))

            def side(name):
                stream_side(pool, "pool", name)

            def one(name, chunks=1):
                for i in range(chunks):
                    halves(pool, "pool", ST[name], 0, i + 2)

            def diag(t, cmp, step):
                nc.gpsimd.affine_select(out=t[:, :], in_=ones[:, :], compare_op=cmp, fill=0.0, base=0,
                                        pattern=[[step, P]], channel_multiplier=-step).then_inc(S("consts_ready"), 1)

            g.do(nc.gpsimd.memset(ones[:, :], 1.0))
            g.sync()
            diag(ident, ALU.is_equal, 1)
            diag(triF, ALU.is_ge, 1)
            diag(triB, ALU.is_ge, -1)
            for h in range(HEADS):
                sl = 2.0 ** (-8.0 * (h + 1) / HEADS)
                nc.gpsimd.memset(slopes[:, h:h + 1], sl)
                ins = nc.gpsimd.memset(nslopes[:, h:h + 1], -sl)
            ins.then_inc(S("slopes_ready"), 1)
            halves(pool, "pool", ST["qkv"], 0, 0)
            halves(pool, "pool", ST["qkv"], 0, 1)
            side("qkv")
            one("gate")
            pool.wait_ge(ml_ready, sum(SPL["h1"]))
            dci = dc_i.bitcast(mybir.dt.int32).rearrange("p (a n) -> p a n", a=2)
            g.do(nc.gpsimd.iota(dci, pattern=[[P, 2], [-CMP_STRIDE, NC]], base=-(CMP_LEN - 1), channel_multiplier=1))
            dmi = DMi.bitcast(mybir.dt.int32)
            g.do(nc.gpsimd.iota(dmi[:, 0:P], pattern=[[-1, P]], base=0, channel_multiplier=1))
            g.do(nc.gpsimd.iota(dmi[:, P:384], pattern=[[-1, S1]], base=P, channel_multiplier=1))
            g.do(nc.gpsimd.memset(MC, 1.0))
            g.do(nc.gpsimd.memset(VCB, 0.0))
            g.sync()
            g.do(nc.gpsimd.tensor_copy(dcb, dci))
            g.do(nc.gpsimd.affine_select(out=MC, in_=MC, compare_op=ALU.is_ge, fill=0.0, base=-(CMP_LEN - 1),
                                         pattern=[[P, 2], [0, HEADS], [-CMP_STRIDE, NC]], channel_multiplier=1))
            g.do(nc.gpsimd.tensor_copy(DM, dmi))
            g.sync()
            big = -NEG * 256.0
            g.do(nc.gpsimd.affine_select(out=DM[:, 0:P], in_=DM[:, 0:P], compare_op=ALU.is_ge, fill=big, base=0,
                                         pattern=[[-1, P]], channel_multiplier=1))
            g.do(nc.gpsimd.affine_select(out=DM[:, P:384], in_=DM[:, P:384], compare_op=ALU.is_ge, fill=big, base=P,
                                         pattern=[[-1, S1]], channel_multiplier=1))
            g.do(nc.gpsimd.tensor_tensor(
                BC, dcb.unsqueeze(2).to_broadcast([P, 2, HEADS, NC]),
                nslopes[:, :].unsqueeze(1).unsqueeze(3).to_broadcast([P, 2, HEADS, NC]), ALU.mult))
            g.sync()
            g.do(nc.gpsimd.affine_select(out=BC, in_=BC, compare_op=ALU.is_ge, fill=NEG, base=-(CMP_LEN - 1),
                                         pattern=[[P, 2], [0, HEADS], [-CMP_STRIDE, NC]], channel_multiplier=1))
            g.sync()
            pool.sem_inc(S("masks_ready"), 1)
            for j in range(2):
                if j:
                    pool.wait_ge(S("w1_used"), 1)
                else:
                    pool.wait_ge(ml_ready, sum(SPL["h1"]))
                g.do(nc.gpsimd.memset(W1, 0.0))
                g.do(nc.gpsimd.memset(W2v if j else W2, 0.0))
                g.sync()
                pool.sem_inc(S("w1_zeroed"), 1)
            for n in ("za", "uv", "zb", "merge", "upa", "upb"):
                side(n)
            one("ple", 2)
            for n in ("out1", "pgate", "gv", "gg"):
                side(n)
            one("dt")
            for n in ("xs", "bc", "z2", "zb2", "oa", "ob", "v", "k", "q"):
                side(n)
            pool.wait_ge(S("bias_stored"), 7 * 16)
            g.do(nc.gpsimd.memset(BIAS, 0.0))
            g.do(nc.gpsimd.memset(MW, 0.0))
            g.sync()
            for half in range(2):
                m = MW[GRID * half:GRID * (half + 1), :]
                g.do(nc.gpsimd.affine_select(out=m[:, 0:48], in_=m[:, 0:48], compare_op=ALU.is_ge, fill=NEG, base=8,
                                             pattern=[[1, 48]], channel_multiplier=-1))
                g.sync()
                g.do(nc.gpsimd.affine_select(out=m[:, 16:64], in_=m[:, 16:64], compare_op=ALU.is_ge, fill=NEG,
                                             base=7 - 16, pattern=[[-1, 48]], channel_multiplier=1))
            g.sync()
            pool.sem_inc(S("bias_used"), SEED)
            with g.loop(0, SH // 2, 0) as it:
                for e in range(2):
                    pool.wait_ge(S(f"bias_landed_{e}"), it * 64 + 64)
                    for qt in range(2):
                        b = BIAS[:, e, qt, META:T2].rearrange("p (j c) -> p j c", j=KH)
                        ins = nc.gpsimd.tensor_tensor(b, b, MW.unsqueeze(1).to_broadcast([P, KH, GRID]), ALU.add)
                    ins.then_inc(S("bias_ready"), 1)
            side("z3")
            side("o3")

        @block.scalar
        def _(act):
            a = Steps(act, S("act_step"))

            def side(name, evac=None, **kw):
                stream_side(act, "act", name, evac, **kw)

            def one(name, chunks=1):
                for i in range(chunks):
                    halves(act, "act", ST[name], 0, i + 2)

            def tiles(dst, it, j, ppi, n=2):
                return dst[:, ds(it * (2 * ppi) + 2 * j, n), :] if not isinstance(it, int) else \
                    dst[:, 2 * ppi * it + 2 * j:2 * ppi * it + 2 * j + n, :]

            def copy_to(dst, fn, name, NT, scale=1.0):
                ppi = ST[name].ppi

                def evac(it, j, par):
                    nc.scalar.activation(tiles(dst, it, j, ppi), ps[:, pairof(par), 0:NT], fn,
                                         scale=scale).then_inc(acc_free, 1)
                return evac

            def via_tmp(fn, name, NT):
                s = ST[name]

                def evac(it, j, par):
                    act.wait_ge(S("tmp_used"), it * s.ppi + TMPC[name] + j - 1 + SEED)
                    nc.scalar.activation(TMP[:, par, :, 0:NT], ps[:, pairof(par), 0:NT], fn).then_inc(acc_free, 1)
                return evac

            for half in range(2):
                src = bass.AP(A["e_D_2"].tensor, half, [[0, HD], [2, DT]])
                nc.scalar.dma_start(Dcol[HD * half:HD * (half + 1), :], src, allow_slow_non_contiguous=True).then_inc(S("d_landed"), 16)

            halves(act, "act", ST["qkv"], 0, 0)
            halves(act, "act", ST["qkv"], 0, 1)
            act.wait_ge(S("xT_copied"), 8)
            norm_act(act, "h1", op(RES, S1, off=META), S1)
            split_op_act(act, "h1", lambda gg: SQX[:, gg % 2, :, 0:S1], op(MH, S1), 4)
            side("qkv", copy_to(qkvT, ACT.Copy, "qkv", S1))
            one("gate")
            act.wait_ge(chunk_done, ST["gate"].end)
            nc.scalar.activation(gates[:, :, :], ps[:, 2 * (ST["gate"].p0 % 2), 0:96].rearrange("p (a n) -> p a n", a=2),
                                 ACT.Sigmoid).then_inc(acc_free, 1)
            for j, nm in enumerate("kv"):
                act.wait_ge(S("w1_zeroed"), j + 1)
                w2 = W2v if j else W2
                for half in range(2):
                    o = slice(HD * half, HD * (half + 1))
                    nc.scalar.dma_start(W1[o, :, HD * half:HD * (half + 1)],
                                        A[f"cmp_w1_{nm}"][0].rearrange("l d e -> d l e")).then_inc(S("w1_landed"), 16)
                    nc.scalar.dma_start(w2[o, HD * half:HD * (half + 1)], A[f"cmp_w2_{nm}"][0]).then_inc(S("w1_landed"), 16)
                    nc.scalar.dma_start(peT[o, j, :], A[f"cmp_pe_{nm}"][0].rearrange("l d -> d l"), allow_slow_non_contiguous=True).then_inc(S("w1_landed"), 16)
                act.wait_ge(S("hid_summed"), j + 1)
                if j:
                    act.wait_ge(S("kc_psum"), 1)
                nc.scalar.activation(hid, ps[:, 4, 0:2 * NC].rearrange("p (a n) -> p a n", a=2),
                                     ACT.Silu).then_inc(S("hid_ready"), 1)
            act.wait_ge(S("vcn_ready"), 1)
            for h in range(HEADS):
                r = NC * (h % 8)
                nc.scalar.dma_start(VCB[r:r + NC, h // 8, (h % 8) * HD:(h % 8 + 1) * HD],
                                    VCN[0:NC, (h // 4) * HD:(h // 4 + 1) * HD]).then_inc(S("vcb_landed"), 16)
            act.wait_ge(S("cmp_shifted"), 1)
            nc.scalar.activation(Pc, Pc, ACT.Exp).then_inc(S("cmp_exp"), 1)
            act.wait_ge(S("pct_psum"), 1)
            nc.scalar.activation(PcT[0:120], ps[0:120, 6, :].rearrange("p (a b n) -> p a b n", a=2, b=2),
                                 ACT.Copy).then_inc(S("pct_ready"), 1)
            for qb in range(2):
                for half in range(2):
                    act.wait_ge(S("oc_psum"), 2 * qb + half + 1)
                    nc.scalar.activation(ON[:, qb, 512 * half:512 * half + 512], ps[:, 4 + half, :],
                                         ACT.Copy).then_inc(S("oc_ready"), 1)
            with a.loop(0, GROUPS, 0) as it:
                for u in range(8):
                    act.wait_ge(S("a_negmax"), it * 8 + u + 1)
                    act.wait_ge(S("a_ptpsum"), it * 8 + u - 1 + SEED)
                    nc.scalar.activation(Eb[:, u % 2, 0:P], SCb[:, u % 2, 0:P], ACT.Exp, bias=small[:, 2 * (u % 2):2 * (u % 2) + 1],
                                         accum_out=small[:, 8 + 2 * (u % 2):9 + 2 * (u % 2)])
                    nc.scalar.activation(Eb[:, u % 2, P:384], SCb[:, u % 2, P:384], ACT.Exp,
                                         bias=small[:, 2 * (u % 2) + 1:2 * (u % 2) + 2],
                                         accum_out=small[:, 9 + 2 * (u % 2):10 + 2 * (u % 2)]).then_inc(S("a_exp"), 1)
                    act.wait_ge(S("a_ptpsum"), it * 8 + u + 1 + SEED)
                    act.wait_ge(S("a_pv"), it * 8 + u - 1 + SEED)
                    nc.scalar.activation(PTb[:, u % 2, :], ps[:, 6, 0:384], ACT.Copy).then_inc(S("a_pt"), 1)
            act.wait_ge(S("a_acc"), 2 * HEADS + SEED)
            side("za", copy_to(ZA, ACT.Silu, "za", S1))
            nc.scalar.dma_start(pnat, A["p"][0, 0].rearrange("(t p) n -> p t n", p=P)).then_inc(S("p_landed"), 16)
            side("uv", copy_to(UV, ACT.Gelu_apprx_tanh, "uv", S1))
            side("zb", copy_to(ZB, ACT.Silu, "zb", S1))
            nc.scalar.dma_start(WS, A["sgu_w"][0].rearrange("g t s -> t g s")).then_inc(S("ws_landed"), 16)
            nc.scalar.dma_start(SGB, bass.AP(A["sgu_b"].tensor, 0, [[0, P], [1, BG * P]]).rearrange("p (g t) -> p g t", g=BG)) \
                .then_inc(S("ws_landed"), 16)
            act.wait_ge(S("v_centred"), 1)
            nc.scalar.activation(SQv, Vv, ACT.Square).then_inc(S("v_sq"), 1)
            act.wait_ge(S("v_ms"), 1)
            nc.scalar.activation(rstd[:, 0:S1], ms[:, 0:S1], ACT.Sqrt).then_inc(S("v_rt"), 1)
            act.wait_ge(S("oT_used"), 4)
            for i in range(4):
                act.wait_ge(S("vn_psum"), i + 1)
                nc.scalar.activation(VN[:, i // 2, 4 * (i % 2):4 * (i % 2) + 4, :],
                                     ps[:, 4 + i % 4, :].rearrange("p (a n) -> p a n", a=4), ACT.Copy).then_inc(S("vn_ready"), 1)
            act.wait_ge(S("ob_ready"), 1)
            side("merge", copy_to(G, ACT.Sigmoid, "merge", S1))
            split_op_act(act, "oa1", op(ZA, S1, 2), op(MH, S1, 2), 4, ST["merge"].end)
            split_op_act(act, "ob1", op(ZB, S1, 2), op(MH, S1, 2, 8), 4)
            side("upa")
            side("upb")
            split_op_act(act, "p", lambda gg: pT, lambda gg: PH, 1, ST["upb"].end)
            s = ST["ple"]
            for i in range(2):
                for j in range(4 * i, 4 * i + 4):
                    act.wait_ge(S("ple_psum"), j + 1)
                    nc.scalar.activation(PLEb[:, 2 * j:2 * j + 2, :], ps[:, pairof((s.p0 + j) % 2), 0:S1], ACT.Copy).then_inc(acc_free, 1)
                halves(act, "act", s, 0, i + 2)
            split_op_act(act, "merged", op(G, S1), op(MH, S1), 4, ST["ple"].end)
            side("out1")
            split_op_act(act, "x1", op(RES, S1, off=META), op(MH, S1), 4, ST["out1"].end)

            def pgate(it, j, par):
                nc.scalar.activation(tiles(G2, it, j, 2), ps[:, pairof(par), 0:S1], ACT.Sigmoid).then_inc(acc_free, 1)
            side("pgate", pgate)
            act.wait_ge(S("x2_ready"), 1)
            norm_act(act, "fin1", op(RES, S1, off=META), S1)
            act.wait_ge(S("block2_in"), 1)
            nc.scalar.dma_start(dtb, bass.AP(A["e_dt_bias_2"].tensor, 0, [[0, P], [1, 2 * SH]])).then_inc(S("dt_params"), 16)
            nc.scalar.dma_start(alog, bass.AP(A["e_A_log_2"].tensor, 0, [[0, P], [1, 2 * SH]])).then_inc(S("dt_params"), 16)
            norm_act(act, "h2", op(RES, T2), T2)
            split_op_act(act, "h2", lambda gg: SQX[:, gg % 2], op(MH, T2), 4, ST["pgate"].end)
            act.sem_inc(S("tmp_used"), SEED)
            side("gv", copy_to(GU, ACT.Copy, "gv", T2))
            side("gg", via_tmp(ACT.Sigmoid, "gg", T2))
            one("dt")
            act.wait_ge(S("dtr_ready"), 1)
            act.wait_ge(S("dt_params"), 32)
            nc.scalar.activation(sp[1], sp[0], ACT.Abs).then_inc(S("sp_abs"), 1)
            act.wait_ge(S("sp_abs"), 1)
            nc.scalar.activation(sp[1], sp[1], ACT.Exp, scale=-1.0).then_inc(S("sp_exp"), 1)
            nc.scalar.activation(alog, alog, ACT.Exp).then_inc(S("sp_exp"), 1)

            def silu_in_place(name):
                s = ST[name]
                base = 16 if name == "bc" else 0

                def evac(it, j, par):
                    act.wait_ge(acc_free, it * 2 + s.p0 + j + 1 + SEED)
                    t = ds(it * 4 + (base + 2 * j), 2)
                    nc.scalar.activation(XBC[:, t, :], XBC[:, t, :], ACT.Silu).then_inc(S("xbc_ready"), 1)
                return evac
            side("xs", silu_in_place("xs"))
            side("bc", silu_in_place("bc"))
            with a.loop(0, SG, 2) as it:
                act.wait_ge(S("xbc_ready"), 16)
                act.wait_ge(S("y_used"), it * 2 + SEED)
                a.do(nc.scalar.activation(XST, XS[:, ds(it * 2, 2), :], ACT.Copy))
                nc.scalar.activation(BS, XBC[:, ds(it + 16, 1), :].rearrange("p a n -> p (a n)"), ACT.Copy).then_inc(S("staged"), 1)
                act.wait_ge(S("x_psum"), it + 1)
                nc.scalar.activation(XNAT[:, 0:2, :], ps[:, 4, :].rearrange("p (a n) -> p a n", a=2), ACT.Copy)
                a.do(nc.scalar.activation(XNAT[0:META, 2, :], ps[0:META, 5, 0:S1], ACT.Copy))
                a.sync()
                act.sem_inc(S("xnat_ready"), 1)
                for h in range(4):
                    act.wait_ge(S("seg_ready"), it * 4 + h + 1)
                    b = h % 2
                    nc.scalar.activation(SEG[:, b, 0:800], SEG[:, b, 0:800], ACT.Exp)
                    nc.scalar.activation(SEG[0:META, b, 800:1088], SEG[0:META, b, 800:1088], ACT.Exp).then_inc(S("seg_exp"), 1)
                    act.wait_ge(S("y_psum"), it * 4 + h + 1 + SEED)
                    if h == 0:
                        act.wait_ge(S("cb_psum"), it + 1)
                    nc.scalar.activation(YN[:, 0:2, HD * h:HD * h + HD], ps[:, 2 + b, 0:128].rearrange("p (a n) -> p a n", a=2), ACT.Copy)
                    nc.scalar.activation(YN[0:META, 2, HD * h:HD * h + HD], ps[0:META, 2 + b, 128:192], ACT.Copy).then_inc(S("yn_ready"), 1)
            act.wait_ge(S("y_used"), 2 * SG + SEED)
            side("z2", via_tmp(ACT.Silu, "z2", T2))
            side("zb2", copy_to(ZB2, ACT.Silu, "zb2", T2))
            act.wait_ge(S("tmp_used"), TMPC["z2"] + 8 + SEED)
            norm_act(act, "ya", op(XS, T2), T2)
            split_op_act(act, "ya", op(XS, T2), op(MH, T2), 4, ST["zb2"].end)
            side("oa")
            act.wait_ge(S("cf_centred"), 1)
            norm_act(act, "cf", op(GU, T2), T2)
            for gq in range(4):
                act.wait_ge(S("cf_scaled"), gq + 1)
                for t in range(4 * gq, 4 * gq + 4):
                    ins = nc.scalar.activation(GU[:, t, :], GU[:, t, :], ACT.Silu, bias=PC[:, t, R_LNB:R_LNB + 1])
                ins.then_inc(S("cf_silu"), 1)
            split_op_act(act, "yb", op(GU, T2), op(MH, T2), 4, ST["oa"].end)
            side("ob")
            act.wait_ge(S("even_done"), 8)
            norm_act(act, "h3", op(RES, T2), T2)
            split_op_act(act, "h3", lambda gg: SQX[:, gg % 2], op(MH, T2), 4, ST["ob"].end)
            side("v", copy_to(KT, ACT.Copy, "v", T2))
            for i in range(12):
                act.wait_ge(S("vo_psum"), i + 1)
                n = P if i % 3 < 2 else META
                nc.scalar.activation(VO[0:n, i % 3, 512 * (i // 3):512 * (i // 3) + 512], ps[0:n, 4 + i % 4, :],
                                     ACT.Copy).then_inc(S("vo_ready"), 1)
            side("k", copy_to(KT, ACT.Copy, "k", T2))
            act.wait_ge(S("tab_zeroed"), 1)
            nc.scalar.dma_start(TAB[0:SH, :, 48:48 + 31], A["o_rpb_2"][0][:, KH:KH + 7, :]).then_inc(S("tab_landed"), 16)
            act.wait_ge(S("tab_landed"), 16)
            nc.scalar.dma_start(tab_dram, TAB[0:SH]).then_inc(S("tab_stored"), 16)
            act.wait_ge(S("tab_stored"), 16)
            for row in range(7):
                nc.scalar.dma_start(bias_dram[:, :, row, :], bass.AP(tab_dram.tensor, row * P + GRID - 1,
                                                                     [[7 * P, SH], [-1, GRID], [1, GRID]])).then_inc(S("bias_stored"), 16)
            side("q", copy_to(QO, ACT.Copy, "q", S1, scale=HD ** -0.5))
            with a.loop(0, SH // 2, 0) as it:
                for e in range(2):
                    act.wait_ge(S("n_negmax"), it * 2 + e + 1)
                    for qt in range(2):
                        ins = nc.scalar.activation(SO[:, e, qt, :], SO[:, e, qt, :], ACT.Exp, bias=small[:, 16 + 2 * e + qt:17 + 2 * e + qt],
                                                   accum_out=small[:, 20 + 2 * e + qt:21 + 2 * e + qt])
                    ins.then_inc(S("n_exp"), 1)
                    act.wait_ge(S("n_ptpsum"), it * 2 + e + 1 + SEED)
                    act.wait_ge(S("n_pv"), it * 2 + e + SEED)
                    nc.scalar.activation(PT1, ps[:, 0, :].rearrange("p (a n) -> p a n", a=2), ACT.Copy)
                    nc.scalar.activation(PT2[0:META], ps[0:META, 1, 0:S1], ACT.Copy).then_inc(S("n_pt"), 1)
            side("z3", via_tmp(ACT.Silu, "z3", S1))
            split_op_act(act, "o3", op(QO, S1), op(MH, S1), 4, ST["z3"].end)
            side("o3")
            act.wait_ge(S("odd_done"), 8)
            norm_act(act, "fin2", op(RES, S1, off=META), S1)

        @block.vector
        def _(dve):
            v = Steps(dve, S("dve_step"))
            V = nc.vector

            def side(name, evac=None, **kw):
                stream_side(dve, "dve", name, evac, **kw)

            def one(name, chunks=1):
                for i in range(chunks):
                    halves(dve, "dve", ST[name], 0, i + 2)

            def tl(it, j, ppi=2, base=0):
                if isinstance(it, int):
                    return slice(2 * ppi * it + base + 2 * j, 2 * ppi * it + base + 2 * j + 2)
                return ds(it * (2 * ppi) + (base + 2 * j), 2)

            v.do(V.memset(small[:, :], 0.0))
            v.sync()
            for n in ("acc_free", "a_biased", "a_acc", "n_acc", "rows_used"):
                dve.sem_inc(S(n), SEED)
            halves(dve, "dve", ST["qkv"], 0, 0)
            halves(dve, "dve", ST["qkv"], 0, 1)
            for i in range(8):
                dve.wait_ge(S("xT_psum"), i + 1)
                V.tensor_copy(RES[:, 2 * i:2 * i + 2, META:T2],
                              ps[:, 4 + i % 4, :].rearrange("p (a n) -> p a n", a=2)).then_inc(S("xT_copied"), 1)
            for i in range(4):
                dve.wait_ge(S("pc_psum"), i + 1)
                V.tensor_copy(PC[:, 4 * i:4 * i + 4, :],
                              ps[:, 4 + i, 0:4 * NROW].rearrange("p (a n) -> p a n", a=4)).then_inc(S("pc_ready"), 1)
            dve.wait_ge(S("pc_ready"), 4)
            V.tensor_copy(RES[:, :, 0:META], PC[:, :, R_META:NROW]).then_inc(S("meta_ready"), 1)
            norm_dve(dve, v, "h1", S1, EPS1)
            apply_dve(dve, v, "h1", op(RES, S1, off=META), R_NORM, S1)
            side("qkv")
            one("gate")
            dve.wait_ge(acc_free, ST["gate"].p0 + 1 + SEED)
            for j in range(2):
                dve.wait_ge(S("w1_landed"), 96 * (j + 1))
                if j:
                    dve.wait_ge(S("hid_summed"), 1)
                for half in range(2):
                    src = qkvT[:, 8 + 2 * j + half, :]
                    win = bass.AP(src.tensor, src.offset, [src.ap[0], [CMP_STRIDE, NC], [1, CMP_LEN]])
                    ins = V.tensor_tensor(KB[:, half], win, peT[:, j:j + 1, :].to_broadcast([P, NC, CMP_LEN]), ALU.add)
                ins.then_inc(S("kb_ready"), 1)
                if j == 0:
                    dve.wait_ge(S("kc_psum"), 1)
                    for gg in range(GROUPS):
                        o = HD * (gg % 2)
                        for half in range(2):
                            ins = V.tensor_scalar(KCD[HD * half:HD * (half + 1), gg, :],
                                                  ps[o:o + HD, 5, NC * (gg // 2):NC * (gg // 2 + 1)], HD ** -0.5, None, ALU.mult)
                    ins.then_inc(S("kcd_ready"), 1)
                else:
                    dve.wait_ge(S("vc_psum"), 1)
                    V.tensor_copy(VCN[0:NC, :], ps[0:NC, 5, 256:512]).then_inc(S("vcn_ready"), 1)
            dve.wait_ge(S("sc_psum"), 2)
            dve.wait_ge(S("masks_ready"), 1)
            for e in range(2):
                def heads_of(t):
                    return t.rearrange("p a (h e) n -> p a h e n", e=2)[:, :, :, e, :]
                v.do(V.tensor_tensor(heads_of(Pc), ps[:, (7, 3)[e], 0:240].rearrange("p (a h n) -> p a h n", a=2, h=8),
                                     heads_of(BC), ALU.add))
            v.sync()
            v.do(V.tensor_reduce(cmx, Pc.rearrange("p a h n -> p (a h) n"), AX.X, ALU.max))
            v.sync()
            Pc3 = Pc.rearrange("p a h n -> p (a h) n")
            V.tensor_tensor(Pc3, Pc3, cmx.unsqueeze(2).to_broadcast([P, 32, NC]), ALU.subtract).then_inc(S("cmp_shifted"), 1)
            dve.wait_ge(S("cmp_exp"), 1)
            v.do(V.tensor_reduce(cz, Pc3, AX.X, ALU.add))
            v.sync()
            v.do(V.reciprocal(cz, cz))
            v.do(V.tensor_tensor(Pc3, Pc3, MC.rearrange("p a h n -> p (a h) n"), ALU.mult))
            v.sync()
            v.do(V.tensor_tensor(cco.rearrange("p (a h) -> p a h", a=2), cz.rearrange("p (a h) -> p a h", a=2),
                                 gates[:, :, 0:HEADS], ALU.mult))
            v.sync()
            V.tensor_tensor(Pc3, Pc3, cco.unsqueeze(2).to_broadcast([P, 32, NC]), ALU.mult).then_inc(S("pc_norm"), 1)
            dve.wait_ge(S("hid_summed"), 2)
            for br in range(2):
                for gg in range(GROUPS):
                    v.do(V.tensor_copy(KSg[0:HD, br, gg, :],
                                       qkvT[HD * (gg % 2):HD * (gg % 2) + HD, 12 + 4 * br + gg // 2, :]))
            for br in range(2):
                dve.wait_ge(S("vn1_psum"), br + 1)
                v.do(V.tensor_copy(Vn[:, br], ps[:, 4 + br, :].rearrange("p (a n) -> p a n", a=2)))
            v.sync()
            dve.wait_ge(S("oc_ready"), 4)
            dve.sem_inc(S("attn_in_ready"), 1)

            def attn_stage(it, r):
                dve.wait_ge(S("a_scores"), it * 8 + 2 * r - 2 + SEED)
                V.tensor_scalar(QSg[0:HD, r % 2, :],
                                qkvT[HD * (r % 2):HD * (r % 2) + HD, ds(it * 2 + r // 2, 1), :].rearrange("p a n -> p (a n)"),
                                HD ** -0.5, None, ALU.mult).then_inc(S("a_staged"), 1)

            def attn_soft(it, u):
                b = u % 2
                dve.wait_ge(S("a_scores"), it * 8 + u + 1 + SEED)
                dve.wait_ge(S("a_exp"), it * 8 + u - 1 + SEED)
                V.scalar_tensor_tensor(out=SCb[:, b, :], in0=DM, scalar=nslopes[:, ds(it * 4 + u // 2, 1)], in1=ps[:, 4 + b, 0:384],
                                       op0=ALU.mult, op1=ALU.add).then_inc(S("a_biased"), 1)
                dve.wait_ge(S("a_biased"), it * 8 + u + 1 + SEED)
                V.tensor_reduce(small[:, 2 * b:2 * b + 1], SCb[:, b, 0:P], AX.X, ALU.max, negate=True)
                V.tensor_reduce(small[:, 2 * b + 1:2 * b + 2], SCb[:, b, P:384], AX.X, ALU.max, negate=True).then_inc(S("a_negmax"), 1)

            def attn_acc(it, u):
                b, r = u % 2, u // 2
                dve.wait_ge(S("a_exp"), it * 8 + u + 1 + SEED)
                v.do(V.reciprocal(small[:, 12 + 2 * b:14 + 2 * b], small[:, 8 + 2 * b:10 + 2 * b]))
                v.sync()
                v.do(V.tensor_tensor(small[:, 12 + 2 * b:14 + 2 * b].unsqueeze(2), small[:, 12 + 2 * b:14 + 2 * b].unsqueeze(2),
                                     gates[:, :, ds(it * 4 + (HEADS * (1 + b) + r), 1)], ALU.mult))
                v.sync()
                dve.wait_ge(S("a_pv"), it * 8 + u + 1 + SEED)
                for qb in range(2):
                    o = ON[:, qb, ds(it * 256 + HD * r, HD)]
                    ins = V.scalar_tensor_tensor(out=o, in0=ps[:, 7, HD * qb:HD * qb + HD],
                                                 scalar=small[:, 12 + 2 * b + qb:13 + 2 * b + qb], in1=o, op0=ALU.mult, op1=ALU.add)
                ins.then_inc(S("a_acc"), 1)

            with v.loop(0, GROUPS, 16) as it:
                dve.wait_ge(S("a_scores"), it * 8 + SEED)
                V.tensor_scalar(KST[0:HD], KSg[0:HD, :, ds(it, 1), :].rearrange("p b a n -> p b (a n)"), 1.0, None, ALU.mult)
                attn_stage(it, 0)
                attn_stage(it, 1)
                attn_soft(it, 0)
                for u in range(8):
                    if u < 7:
                        attn_soft(it, u + 1)
                    if u % 2 == 0 and 1 <= u // 2 and u // 2 < 3:
                        attn_stage(it, u // 2 + 1)
                    attn_acc(it, u)
            dve.wait_ge(S("a_acc"), 2 * HEADS + SEED)
            side("za")
            side("uv")
            side("zb")
            dve.wait_ge(acc_free, ST["merge"].p0 + SEED)
            for i in range(4):
                dve.wait_ge(S("oT_psum"), i + 1)
                V.tensor_tensor(ZA[:, 2 * i:2 * i + 2, :], ZA[:, 2 * i:2 * i + 2, :],
                                ps[:, i, :].rearrange("p (a n) -> p a n", a=2), ALU.mult).then_inc(S("oT_used"), 1)
            dve.wait_ge(S("v_sum"), 1)
            v.do(V.tensor_scalar(ms[:, 0:S1], ps[:, 4, 0:S1], 1.0 / BW, None, ALU.mult))
            v.sync()
            V.tensor_tensor(Vv, Vv, ms[:, 0:S1].unsqueeze(1).to_broadcast([P, 8, S1]), ALU.subtract).then_inc(S("v_centred"), 1)
            dve.wait_ge(S("v_var"), 1)
            V.tensor_scalar(ms[:, 0:S1], ps[:, 5, 0:S1], 1.0 / BW, EPS1, ALU.mult, ALU.add).then_inc(S("v_ms"), 1)
            dve.wait_ge(S("v_rt"), 1)
            v.do(V.reciprocal(rstd[:, 0:S1], rstd[:, 0:S1]))
            v.sync()
            for t in range(8):
                v.do(V.scalar_tensor_tensor(out=Vv[:, t, :], in0=Vv[:, t, :], scalar=PC[:, t, R_LNV:R_LNV + 1], in1=rstd[:, 0:S1],
                                            op0=ALU.mult, op1=ALU.mult))
            v.sync()
            for t in range(8):
                V.tensor_scalar(Vv[:, t, :], Vv[:, t, :], PC[:, 8 + t, R_LNV:R_LNV + 1], None, ALU.add).then_inc(S("v_normed"), 1)
            for i in range(2):
                dve.wait_ge(S("wst_psum"), i + 1)
                V.tensor_tensor(WST[:, 4 * i:4 * i + 4, :], ps[:, 6 + i, :].rearrange("p (a n) -> p a n", a=4),
                                triF[:, :].unsqueeze(1).to_broadcast([P, 4, P]), ALU.mult).then_inc(S("wst_ready"), 1)
            dve.wait_ge(S("ws_landed"), 32)
            for i in range(4):
                dve.wait_ge(S("sv_psum"), i + 1)
                v.sync()
                m = ps[:, i, :].rearrange("p (a c n) -> p a c n", a=2, c=2)
                for k in range(2):
                    t = 2 * i + k
                    v.do(V.tensor_tensor(SGB2[:, k].rearrange("p (c n) -> p c n", c=2), m[:, k],
                                         SGB[:, t, :].unsqueeze(1).to_broadcast([P, 2, P]), ALU.add))
                v.do(V.tensor_tensor(UV[:, 2 * i:2 * i + 2, :], UV[:, 2 * i:2 * i + 2, :], ZB[:, 2 * i:2 * i + 2, :], ALU.mult))
                v.sync()
                v.do(V.tensor_tensor(ZB[:, 2 * i:2 * i + 2, :], UV[:, 2 * i:2 * i + 2, :], SGB2, ALU.mult))
            v.sync()
            dve.sem_inc(S("ob_ready"), 1)
            dve.sem_inc(src_ready, 8)
            side("merge")
            for gq in range(4):
                split_op_dve(dve, "oa1", op(ZA, S1, 2), op(MH, S1, 2), op(ML, S1, 2), gq)
            for gq in range(4):
                split_op_dve(dve, "ob1", op(ZB, S1, 2), op(MH, S1, 2, 8), op(ML, S1, 2, 8), gq)

            def up_a(it, j, par):
                g_ = G[:, tl(it, j, 4), :]
                V.tensor_tensor(g_, g_, ps[:, pairof(par), 0:S1], ALU.mult).then_inc(acc_free, 1)

            def up_b(it, j, par):
                gb = G[:, tl(it, j, 4, 16), :]
                ga = G[:, tl(it, j, 4), :]
                V.tensor_tensor(gb, gb, ps[:, pairof(par), 0:S1], ALU.mult).then_inc(acc_free, 1)
                dve.wait_ge(acc_free, (it * 4 if not isinstance(it, int) else 4 * it) + ST["upb"].p0 + j + 1 + SEED)
                v.do(V.tensor_tensor(ga, ga, gb, ALU.add))

            side("upa", up_a)
            side("upb", up_b, steps=v, per=4)
            dve.wait_ge(S("pT_psum"), 1)
            V.tensor_copy(pT, ps[:, 4, :].rearrange("p (a n) -> p a n", a=2)).then_inc(src_ready, 1)
            split_op_dve(dve, "p", lambda gg: pT, lambda gg: PH, lambda gg: PL, 0)
            v.sync()
            dve.sem_inc(src_ready, 4)
            one("ple", 2)
            for gq in range(4):
                split_op_dve(dve, "merged", op(G, S1), op(MH, S1), op(ML, S1), gq)

            def add_res(NT, off=0, name=None):
                def evac(it, j, par):
                    r = RES[:, tl(it, j), off:off + NT]
                    ins = V.tensor_tensor(r, r, ps[:, pairof(par), 0:NT], ALU.add).then_inc(acc_free, 1)
                return evac

            side("out1", add_res(S1, META))
            dve.wait_ge(acc_free, ST["pgate"].p0 + SEED)
            dve.sem_inc(src_ready, 4)
            for gq in range(4):
                split_op_dve(dve, "x1", op(RES, S1, off=META), op(MH, S1), op(ML, S1), gq)

            def ple_add(it, j, par):
                t = tl(it, j)
                dve.wait_ge(acc_free, it * 2 + ST["pgate"].p0 + j + 1 + SEED)
                v.do(V.tensor_tensor(PLEb[:, t, :], PLEb[:, t, :], G2[:, t, :], ALU.mult))
                v.sync()
                v.do(V.tensor_tensor(RES[:, t, META:T2], RES[:, t, META:T2], PLEb[:, t, :], ALU.add))

            side("pgate", ple_add, steps=v, per=4)
            v.sync()
            dve.sem_inc(S("x2_ready"), 1)
            norm_dve(dve, v, "fin1", S1, EPS1)
            for t in range(DT):
                v.do(V.scalar_tensor_tensor(out=RES[:, t, META:T2], in0=RES[:, t, META:T2], scalar=PC[:, t, R_FINAL:R_FINAL + 1],
                                            in1=rstd[:, 0:S1], op0=ALU.mult, op1=ALU.mult))
            v.sync()
            dve.sem_inc(S("block2_in"), 1)
            norm_dve(dve, v, "h2", T2, EPS2)
            apply_dve(dve, v, "h2", op(RES, T2), R_ENORM, T2)
            side("gv")

            def times(dst, name, NT, per=2, base=0):
                s = ST[name]

                def evac(it, j, par):
                    dve.wait_ge(acc_free, it * 2 + s.p0 + j + 1 + SEED)
                    d = dst[:, tl(it, j), 0:NT]
                    V.tensor_tensor(d, d, TMP[:, par, :, 0:NT], ALU.mult).then_inc(S("tmp_used"), 1)
                return evac

            side("gg", times(GU, "gg", T2))
            one("dt")
            v.do(V.memset(sp[0], 0.0))
            v.do(V.memset(TRI, 1.0))
            dve.wait_ge(S("dt_params"), 32)
            dve.wait_ge(chunk_done, ST["dt"].end)
            v.sync()
            b = 2 * (ST["dt"].p0 % 2)
            v.do(V.tensor_tensor(sp[0][:, 0:2, :], ps[:, b, 0:128].rearrange("p (a n) -> p a n", a=2),
                                 dtb.unsqueeze(1).to_broadcast([P, 2, 2 * SH]), ALU.add))
            v.do(V.tensor_tensor(sp[0][0:META, 2, :], ps[0:META, b, 128:192], dtb[0:META], ALU.add))
            v.sync()
            dve.sem_inc(acc_free, 1)
            dve.sem_inc(S("dtr_ready"), 1)
            for i in range(3):
                for d, tri in enumerate((triF, triB)):
                    n = P if i < 2 else META
                    if d == 0 and i:
                        V.memset(TRI[:, 0, i, 0:P * i], 0.0)
                    if d == 1 and i < 2:
                        V.memset(TRI[:, 1, i, P * i + P:T2], 0.0)
                    v.do(V.tensor_copy(TRI[:, d, i, P * i:P * i + n], tri[:, 0:n]))
            dve.wait_ge(S("sp_exp"), 2)
            v.do(V.tensor_scalar(sp[2], sp[1], 2.0, None, ALU.add))
            v.sync()
            v.do(V.reciprocal(sp[2], sp[2]))
            v.sync()
            v.do(V.tensor_tensor(sp[2], sp[1], sp[2], ALU.mult))
            v.sync()
            v.do(V.tensor_tensor(sp[3], sp[2], sp[2], ALU.mult))
            v.sync()
            v.do(V.tensor_scalar(sp[4], sp[3], 1.0 / 19, None, ALU.mult))
            for k in range(8, 0, -1):
                v.sync()
                v.do(V.scalar_tensor_tensor(out=sp[4], in0=sp[4], scalar=1.0 / (2 * k + 1), in1=sp[3], op0=ALU.add, op1=ALU.mult))
            v.sync()
            v.do(V.scalar_tensor_tensor(out=sp[4], in0=sp[4], scalar=1.0, in1=sp[2], op0=ALU.add, op1=ALU.mult))
            v.do(V.tensor_scalar(sp[5], sp[0], 0.0, None, ALU.max))
            v.sync()
            v.do(V.scalar_tensor_tensor(out=dtN[:, :, :], in0=sp[4], scalar=2.0, in1=sp[5], op0=ALU.mult, op1=ALU.add))
            v.sync()
            v.do(V.scalar_tensor_tensor(out=aN, in0=dtN[:, :, :], scalar=-1.0, in1=alog.unsqueeze(1).to_broadcast([P, 3, 2 * SH]),
                                        op0=ALU.mult, op1=ALU.mult))
            v.sync()
            dve.sem_inc(S("a_nat_ready"), 1)
            for d in range(2):
                dve.wait_ge(S("cum_psum"), d + 1)
                V.tensor_copy(CF[0:SH, d, :], ps[0:SH, 4 + d, 0:T2]).then_inc(S("cum_rows_ready"), 1)
            dve.wait_ge(S("cn_psum"), 1)
            v.do(V.tensor_copy(cN[:, 0:2, :], ps[:, 6, 0:128].rearrange("p (a n) -> p a n", a=2)))
            v.do(V.tensor_copy(cN[0:META, 2, :], ps[0:META, 6, 128:192]))
            v.sync()
            dve.sem_inc(S("tri_free"), 1)

            def conv5(name, half):
                def evac(it, j, par):
                    for k in range(2):
                        t = ds(it * 4 + (2 * j + k), 1)
                        x = ps[:, 2 * par + k, 0:T2]
                        o = XBC[:, ds(it * 4 + (16 * half + 2 * j + k), 1), :].rearrange("p a n -> p (a n)")

                        def w(tap):
                            c = R_CW + 2 * tap + half
                            return PC[:, t, c:c + 1].rearrange("p a n -> p (a n)")
                        cb = PC[:, t, R_CB + half:R_CB + half + 1].rearrange("p a n -> p (a n)")
                        v.do(V.tensor_scalar(o, x, w(2), cb, ALU.mult, ALU.add))
                        for tap in (0, 1, 3, 4):
                            d = tap - 2
                            lo, hi = max(0, -d), T2 - max(0, d)
                            v.sync()
                            ins = V.scalar_tensor_tensor(out=o[:, lo:hi], in0=x[:, lo + d:hi + d], scalar=w(tap), in1=o[:, lo:hi],
                                                         op0=ALU.mult, op1=ALU.add)
                            if tap < 4 or k == 0:
                                v.do(ins)
                            else:
                                ins.then_inc(acc_free, 1)
                return evac

            def conv31(tile, first=None):
                x = GU[:, tile, :].rearrange("p a n -> p (a n)")

                def w(tap):
                    return PC[:, tile, R_DW + tap:R_DW + tap + 1].rearrange("p a n -> p (a n)")
                acc = ACC[:, 0, :]
                mid = K31 // 2
                cb = PC[:, tile, R_DWB:R_DWB + 1].rearrange("p a n -> p (a n)")
                v.do(V.tensor_scalar(acc, x, w(mid), cb, ALU.mult, ALU.add))
                for tap in [k for k in range(K31) if k != mid]:
                    d = tap - mid
                    lo, hi = max(0, -d), T2 - max(0, d)
                    v.sync()
                    v.do(V.scalar_tensor_tensor(out=acc[:, lo:hi], in0=x[:, lo + d:hi + d], scalar=w(tap), in1=acc[:, lo:hi],
                                                op0=ALU.mult, op1=ALU.add))
                v.sync()
                v.do(V.tensor_scalar(x, acc, 1.0, None, ALU.mult))

            def conv_tile(base):
                return lambda it: conv31(ds(it + base, 1))

            side("xs", conv5("xs", 0), steps=v, per=18)
            side("bc", conv5("bc", 1), steps=v, per=18 + 32, extra=conv_tile(0))
            dve.wait_ge(S("xbc_ready"), 16)
            dve.sem_inc(S("ssd_go"), 1)
            dve.wait_ge(S("d_landed"), 32)
            with v.loop(0, SG, 6 + 4) as it:
                def seg(h):
                    b, hp = h % 2, h // 2
                    dve.wait_ge(S(f"rows_landed_{hp}"), it * 16 + 16)
                    dve.wait_ge(S("y_psum"), it * 4 + h - 1 + SEED)
                    for i, (d, st, lo, hi, at) in enumerate(SSD_COLS):
                        n = P if st < 2 else META
                        ins = V.tensor_scalar(SEG[0:n, b, at:at + hi - lo], ROWS[0:n, hp, d, h % 2, lo:hi],
                                              cN[0:n, st, ds(it * 4 + (SH * d + h), 1)], 0.0, ALU.subtract, ALU.min)
                    ins.then_inc(S("seg_ready"), 1)

                def weigh(h):
                    b = h % 2
                    dve.wait_ge(S("seg_exp"), it * 4 + h + 1)
                    dve.sem_inc(S("rows_used"), 1)
                    for i, (d, st, lo, hi, at) in enumerate(SSD_COLS):
                        n = P if st < 2 else META
                        sg = SEG[0:n, b, at:at + hi - lo]
                        ins = V.scalar_tensor_tensor(out=sg, in0=sg, scalar=dtN[0:n, st, ds(it * 4 + (SH * d + h), 1)],
                                                     in1=CBM[0:n, at:at + hi - lo], op0=ALU.mult, op1=ALU.mult)
                    ins.then_inc(S("w_ready"), 1)

                seg(0)
                dve.wait_ge(S("cb_psum"), it + 1)
                for d, st, lo, hi, at in SSD_COLS:
                    n = P if st < 2 else META
                    dlo, dn = P * st, n
                    src = ps[0:n, (6, 7, 1)[st], :]
                    m = (triF, triB)[d]
                    if hi - lo > dn:
                        rest = (lo + dn, hi) if d == 0 else (lo, dlo)
                        V.tensor_copy(CBM[0:n, at + rest[0] - lo:at + rest[1] - lo], src[:, rest[0]:rest[1]])
                    v.do(V.tensor_tensor(CBM[0:n, at + dlo - lo:at + dlo - lo + dn], src[:, dlo:dlo + dn], m[0:n, 0:dn], ALU.mult))
                v.sync()
                for h in range(4):
                    if h < 3:
                        seg(h + 1)
                    weigh(h)
                for k in range(2):
                    dve.wait_ge(S("yT_psum"), it * 2 + k + 1)
                    t = ds(it * 2 + k, 1)
                    xt = XS[:, t, :].rearrange("p a n -> p (a n)")
                    v.do(V.tensor_scalar(xt, xt, Dcol[:, t], None, ALU.mult))
                    v.sync()
                    v.do(V.tensor_tensor(xt, xt, ps[:, 4 + k, 0:T2], ALU.add))
                v.sync()
                dve.sem_inc(S("y_used"), 2)
            side("z2", times(XS, "z2", T2), steps=v, per=32, extra=conv_tile(4))
            side("zb2", steps=v, per=32, extra=conv_tile(8))
            norm_dve(dve, v, "ya", T2, EPS2)
            apply_dve(dve, v, "ya", op(XS, T2), R_SSD, T2, dst=op(XS, T2))
            side("oa", add_res(T2), steps=v, per=32, extra=conv_tile(12))
            v.sync()
            dve.sem_inc(S("conv31_done"), 1)
            dve.wait_ge(S("cf_sum"), 1)
            v.do(V.tensor_scalar(ms[:, :], ps[:, 5, 0:T2], 1.0 / D, None, ALU.mult))
            v.sync()
            V.tensor_tensor(GU, GU, ms[:, :].unsqueeze(1).to_broadcast([P, DT, T2]), ALU.subtract).then_inc(S("cf_centred"), 1)
            norm_dve(dve, v, "cf", T2, EPS2)
            for t in range(DT):
                ins = V.scalar_tensor_tensor(out=GU[:, t, :], in0=GU[:, t, :], scalar=PC[:, t, R_LNG:R_LNG + 1], in1=rstd[:, :],
                                             op0=ALU.mult, op1=ALU.mult)
                if t % 4 == 3:
                    ins.then_inc(S("cf_scaled"), 1)
            for gq in range(4):
                dve.wait_ge(S("cf_silu"), gq + 1)
                V.tensor_tensor(op(GU, T2)(gq), op(GU, T2)(gq), op(ZB2, T2)(gq), ALU.mult).then_inc(src_ready, 1)
            for gq in range(4):
                split_op_dve(dve, "yb", op(GU, T2), op(MH, T2), op(ML, T2), gq)
            side("ob", add_res(T2))
            dve.wait_ge(acc_free, ST["v"].p0 + SEED)
            dve.sem_inc(S("even_done"), 8)
            norm_dve(dve, v, "h3", T2, EPS2)
            apply_dve(dve, v, "h3", op(RES, T2), R_ONORM, T2)
            side("v")
            side("k")
            v.do(V.memset(TAB[0:SH], 0.0))
            v.sync()
            dve.sem_inc(S("tab_zeroed"), 1)
            side("q")
            with v.loop(0, SH // 2, 4) as it:
                def stage(e):
                    h = slice(HD * e, HD * e + HD)
                    dve.wait_ge(S("n_scores"), it * 2 + e - 1 + SEED)
                    V.tensor_scalar(QS[0:HD, e, :], QO[h, ds(it, 1), :].rearrange("p a n -> p (a n)"), 1.0, None, ALU.mult)
                    V.tensor_scalar(KS[0:HD, e, :], KT[h, ds(it, 1), :].rearrange("p a n -> p (a n)"), 1.0, None, ALU.mult).then_inc(S("n_staged"), 1)

                def soft(e):
                    dve.wait_ge(S("n_scores"), it * 2 + e + 1 + SEED)
                    dve.wait_ge(S("bias_ready"), it * 2 + e + 1)
                    dve.wait_ge(S("n_ptpsum"), it * 2 + e - 1 + SEED)
                    V.tensor_tensor(SO[:, e], BIAS[:, e], ps[:, 4 + 2 * e:6 + 2 * e, 0:T2], ALU.add).then_inc(S("bias_used"), 1)
                    dve.wait_ge(S("bias_used"), it * 2 + e + 1 + SEED)
                    V.tensor_reduce(small[:, 16 + 2 * e:18 + 2 * e], SO[:, e], AX.X, ALU.max, negate=True).then_inc(S("n_negmax"), 1)

                def acc(e):
                    dve.wait_ge(S("n_exp"), it * 2 + e + 1)
                    v.do(V.reciprocal(small[:, 24 + 2 * e:26 + 2 * e], small[:, 20 + 2 * e:22 + 2 * e]))
                    v.sync()
                    dve.wait_ge(S("n_pv"), it * 2 + e + 1 + SEED)
                    for qt in range(2):
                        o = QO[:, ds(it, 1), P * qt + HD * e:P * qt + HD * e + HD].rearrange("p a n -> p (a n)")
                        ins = V.tensor_scalar(o, ps[:, 2 + e, HD * qt:HD * qt + HD], small[:, 24 + 2 * e + qt:25 + 2 * e + qt], None, ALU.mult)
                        if qt == 0:
                            v.do(ins)
                    ins.then_inc(S("n_acc"), 1)
                stage(0)
                stage(1)
                soft(0)
                soft(1)
                acc(0)
                acc(1)
            for i in range(8):
                dve.wait_ge(S("oT3_psum"), i + 1)
                V.tensor_copy(QO[:, 2 * i:2 * i + 2, :], ps[:, 4 + i % 4, :].rearrange("p (a n) -> p a n", a=2)).then_inc(S("oT3_ready"), 1)
            dve.wait_ge(S("oT3_ready"), 8)
            side("z3", times(QO, "z3", S1))
            dve.wait_ge(S("tmp_used"), TMPC["z3"] + 8 + SEED)
            dve.sem_inc(src_ready, 4)
            for gq in range(4):
                split_op_dve(dve, "o3", op(QO, S1), op(MH, S1), op(ML, S1), gq)
            side("o3", add_res(S1, META))
            dve.wait_ge(acc_free, ST["o3"].p0 + 8 + SEED)
            dve.sem_inc(S("odd_done"), 8)
            norm_dve(dve, v, "fin2", S1, EPS2)
            for t in range(DT):
                V.scalar_tensor_tensor(out=XF[:, t, :], in0=RES[:, t, META:T2], scalar=PC[:, t, R_FNORM:R_FNORM + 1],
                                       in1=rstd[:, 0:S1], op0=ALU.mult, op1=ALU.mult).then_inc(S("xf_ready"), 1)
            for i in range(8):
                dve.wait_ge(S("out_psum"), i + 1)
                V.tensor_copy(onat[:, i % 2, 512 * (i // 2):512 * (i // 2) + 512], ps[:, 4 + i % 4, :]).then_inc(S("out_ready"), 1)

        @block.tensor
        def _(pe):
            T = nc.tensor
            pe.wait_ge(S("consts_ready"), 3)
            pe.wait_ge(S("x_landed"), 16)
            for i in range(8):
                if i >= 4:
                    pe.wait_ge(S("xT_copied"), i - 3)
                for k in range(2):
                    for tt in range(2):
                        mm = T.transpose(ps[:, 4 + i % 4, 256 * k + P * tt:256 * k + P * tt + P],
                                         xnat[:, tt, (2 * i + k) * P:(2 * i + k + 1) * P], ident[:, :])
                mm.then_inc(S("xT_psum"), 1)
            pe.wait_ge(S("params_landed"), 15 * 16)
            for i in range(4):
                pe.wait_ge(S("xT_copied"), 5 + i)
                for k in range(4):
                    mm = T.transpose(ps[:, 4 + i, NROW * k:NROW * (k + 1)], PR[0:NROW, (4 * i + k) * P:(4 * i + k + 1) * P],
                                     ident[0:NROW, 0:NROW])
                mm.then_inc(S("pc_psum"), 1)
            pe.wait_ge(S("pc_ready"), 4)
            norm_pe(pe, "h1", S1)
            stream_pe(pe, "qkv", need="h1")
            natural(pe, "gate", [(0, P), (P, P)], 3 * HEADS)
            for j in range(2):
                pe.wait_ge(S("kb_ready"), j + 1)
                if j:
                    pe.wait_ge(S("hid_ready"), 1)
                for l in range(CMP_LEN):
                    mm = T.matmul(ps[:, 4, 0:2 * NC].rearrange("p (a n) -> p a n", a=2), W1[:, l, :], KB[:, :, :, l],
                                  start=(l == 0), stop=(l == CMP_LEN - 1))
                mm.then_inc(S("hid_summed"), 1)
                pe.wait_ge(S("hid_ready"), j + 1)
                if j == 0:
                    pe.wait_ge(S("hid_summed"), 1)
                    T.matmul(ps[:, 5, 0:2 * NC], W2[:, :], hid.rearrange("p a n -> p (a n)"), start=True, stop=True).then_inc(S("kc_psum"), 1)
                    pe.sem_inc(S("w1_used"), 1)
                else:
                    pe.wait_ge(S("kcd_ready"), 1)
                    for a_ in range(2):
                        mm = T.matmul(ps[0:NC, 5, 256 + P * a_:256 + P * a_ + P], hid[:, a_, :], W2v[:, :], start=True, stop=True)
                    mm.then_inc(S("vc_psum"), 1)
            for qb in range(2):
                for h in range(HEADS):
                    o = HD * (h % 2)
                    at = (HEADS // 2 * qb + h // 2) * NC
                    mm = T.matmul(ps[:, 3 if h % 2 else 7, at:at + NC],
                                  qkvT[o:o + HD, h // 2, P * qb:P * qb + P], KCD[o:o + HD, h // 4, :], start=True, stop=True)
                    if qb == 1 and h >= HEADS - 2:
                        mm.then_inc(S("sc_psum"), 1)
            pe.wait_ge(S("pc_norm"), 1)
            for half in range(2):
                for qb in range(2):
                    mm = T.transpose(ps[0:120, 6, (2 * half + qb) * P:(2 * half + qb + 1) * P],
                                     Pc[:, qb, 8 * half:8 * half + 8, :].rearrange("p h n -> p (h n)"), ident[:, :])
            mm.then_inc(S("pct_psum"), 1)
            pe.wait_ge(S("pct_ready"), 1)
            pe.wait_ge(S("vcb_landed"), 16 * HEADS)
            pe.wait_ge(S("vcn_ready"), 1)
            for qb in range(2):
                for half in range(2):
                    if qb:
                        pe.wait_ge(S("oc_ready"), half + 1)
                    T.matmul(ps[:, 4 + half, :], PcT[0:120, half, qb, :], VCB[0:120, half, :], start=True,
                             stop=True).then_inc(S("oc_psum"), 1)
            pe.wait_ge(S("oc_ready"), 4)
            for br in range(2):
                for tt in range(2):
                    for j in range(2):
                        mm = T.transpose(ps[:, 4 + br, 256 * tt + P * j:256 * tt + P * j + P],
                                         qkvT[:, 14 + 4 * br + j, P * tt:P * tt + P], ident[:, :])
                mm.then_inc(S("vn1_psum"), 1)
            pe.wait_ge(S("attn_in_ready"), 1)
            for n in ("a_scores", "a_exp", "a_ptpsum", "a_pt", "a_pv", "y_psum", "n_scores", "n_pv", "n_ptpsum", "n_pt", "y_used"):
                pe.sem_inc(S(n), SEED)

            def a_scores(it, u):
                b, r = u % 2, u // 2
                pe.wait_ge(S("a_staged"), it * 4 + r + 1)
                pe.wait_ge(S("a_biased"), it * 8 + u - 1 + SEED)
                for qb in range(2):
                    n = P * (qb + 1)
                    mm = T.matmul(ps[:, 4 + b, P * qb:P * qb + n], QSg[0:HD, r % 2, P * qb:P * qb + P],
                                  KST[0:HD, b, 0:n], start=True, stop=True)
                mm.then_inc(S("a_scores"), 1)

            def a_rest(it, u):
                b = u % 2
                pe.wait_ge(S("a_exp"), it * 8 + u + 1 + SEED)
                pe.wait_ge(S("a_pt"), it * 8 + u + SEED)
                for k in range(3):
                    mm = T.transpose(ps[:, 6, P * k:P * k + P], Eb[:, b, P * k:P * k + P], ident[:, :])
                mm.then_inc(S("a_ptpsum"), 1)
                pe.wait_ge(S("a_pt"), it * 8 + u + 1 + SEED)
                pe.wait_ge(S("a_acc"), it * 8 + u + SEED)
                for o, blocks in ((0, [(0, 0)]), (HD, [(1, 0), (2, 1)])):
                    for k, (blk, tt) in enumerate(blocks):
                        mm = T.matmul(ps[:, 7, o:o + HD], PTb[:, b, P * blk:P * blk + P], Vn[:, b, tt, ds(it * HD, HD)],
                                      start=(k == 0), stop=(k == len(blocks) - 1))
                mm.then_inc(S("a_pv"), 1)

            with pe.Fori(0, GROUPS) as it:
                a_scores(it, 0)
                for u in range(8):
                    if u < 7:
                        a_scores(it, u + 1)
                    a_rest(it, u)
            pe.wait_ge(S("a_acc"), 2 * HEADS + SEED)
            for n in ("za", "uv", "zb"):
                stream_pe(pe, n)
            pe.wait_ge(acc_free, ST["merge"].p0 + SEED)
            for i in range(4):
                for k in range(2):
                    for qb in range(2):
                        mm = T.transpose(ps[:, i, 256 * k + P * qb:256 * k + P * qb + P],
                                         ON[:, qb, (2 * i + k) * P:(2 * i + k + 1) * P], ident[:, :])
                mm.then_inc(S("oT_psum"), 1)
            for t in range(8):
                mm = T.matmul(ps[:, 4, 0:S1], ones[:, :], Vv[:, t, :], start=(t == 0), stop=(t == 7))
            mm.then_inc(S("v_sum"), 1)
            pe.wait_ge(S("v_sq"), 1)
            for t in range(8):
                mm = T.matmul(ps[:, 5, 0:S1], ones[:, :], SQv[:, t, :], start=(t == 0), stop=(t == 7))
            mm.then_inc(S("v_var"), 1)
            pe.wait_ge(S("ws_landed"), 32)
            for i in range(2):
                for k in range(4):
                    mm = T.transpose(ps[:, 6 + i, P * k:P * k + P], WS[:, 4 * i + k, :], ident[:, :])
                mm.then_inc(S("wst_psum"), 1)
            pe.wait_ge(S("v_normed"), 8)
            pe.wait_ge(S("wst_ready"), 2)
            for i in range(4):
                for k in range(4):
                    mm = T.transpose(ps[:, 4 + i, P * k:P * k + P], Vv[:, 4 * (i % 2) + k, P * (i // 2):P * (i // 2) + P], ident[:, :])
                mm.then_inc(S("vn_psum"), 1)
            pe.wait_ge(S("vn_ready"), 4)
            pe.wait_ge(S("oT_used"), 4)
            for i in range(4):
                for k in range(2):
                    for c in range(2):
                        mm = T.matmul(ps[:, i, 256 * k + P * c:256 * k + P * c + P], VN[:, c, 2 * i + k, :], WST[:, 2 * i + k, :],
                                      start=True, stop=True)
                mm.then_inc(S("sv_psum"), 1)
            pe.wait_ge(S("ob_ready"), 1)
            stream_pe(pe, "merge")
            pe.wait_ge(S("p_landed"), 16)
            for k in range(2):
                for tt in range(2):
                    mm = T.transpose(ps[:, 4, 256 * k + P * tt:256 * k + P * tt + P], pnat[:, tt, P * k:P * k + P], ident[:, :])
            mm.then_inc(S("pT_psum"), 1)
            stream_pe(pe, "upa", need="oa1")
            stream_pe(pe, "upb", tile0=8, need="ob1")
            s = ST["ple"]
            pe.wait_ge(ml_ready, sum(SPL["p"]))
            for i in range(2):
                c = s.c0 + i
                lo_wait(pe, s.c0, 0, i)
                wh = whi[c % 2][:, :].rearrange("p (t n) -> p t n", t=2)
                wl = wlo[c % 2][:, :].rearrange("p (t n) -> p t n", t=2)
                for j in range(4):
                    pr = 4 * i + j
                    pe.wait_ge(acc_free, s.p0 + pr - 1 + SEED)
                    for n in range(2):
                        o = ps[:, 2 * ((s.p0 + pr) % 2) + n, 0:S1]
                        cc = slice((2 * j + n) * P, (2 * j + n + 1) * P)
                        for k in range(2):
                            T.matmul(o, wh[:, k, cc], PH[:, k, :], start=(k == 0), stop=False)
                            T.matmul(o, wh[:, k, cc], PL[:, k, :], start=False, stop=False)
                            mm = T.matmul(o, wl[:, k, cc], PH[:, k, :], start=False, stop=(k == 1))
                    mm.then_inc(S("ple_psum"), 1)
                pe.wait_ge(S("ple_psum"), 4 * i + 4)
                pe.sem_inc(chunk_done, 1)
            stream_pe(pe, "out1", need="merged")
            stream_pe(pe, "pgate", need="x1")
            norm_pe(pe, "fin1", S1)
            norm_pe(pe, "h2", T2)
            stream_pe(pe, "gv", NT=T2, need="h2")
            stream_pe(pe, "gg", NT=T2)
            natural(pe, "dt", [(0, P), (P, P), (2 * P, META)], 2 * SH)
            pe.wait_ge(S("a_nat_ready"), 1)
            for d in range(2):
                for i in range(3):
                    n = P if i < 2 else META
                    mm = T.matmul(ps[0:SH, 4 + d, 0:T2], aN[0:n, i, SH * d:SH * d + SH], TRI[0:n, d, i, :], start=(i == 0), stop=(i == 2))
                mm.then_inc(S("cum_psum"), 1)
            pe.wait_ge(S("cum_rows_ready"), 2)
            for d in range(2):
                for i in range(3):
                    n = P if i < 2 else META
                    mm = T.transpose(ps[0:n, 6, 64 * i + SH * d:64 * i + SH * d + SH], CF[0:SH, d, P * i:P * i + n], ident[0:SH, 0:SH])
            mm.then_inc(S("cn_psum"), 1)
            stream_pe(pe, "xs", NT=T2)
            stream_pe(pe, "bc", NT=T2)
            pe.wait_ge(S("ssd_go"), 1)
            with pe.Fori(0, SG) as it:
                pe.wait_ge(S("staged"), it + 1)
                for i in range(3):
                    n = P if i < 2 else META
                    for k in range(2):
                        o = ps[0:n, 4, 256 * i + P * k:256 * i + P * k + P] if i < 2 else ps[0:n, 5, P * k:P * k + P]
                        mm = T.transpose(o, XST[:, k, P * i:P * i + n], ident[:, :])
                mm.then_inc(S("x_psum"), 1)
                for i in range(3):
                    n = P if i < 2 else META
                    mm = T.matmul(ps[0:n, (6, 7, 1)[i], 0:T2], BS[:, P * i:P * i + n],
                                  XBC[:, ds(it + 24, 1), :].rearrange("p a n -> p (a n)"), start=True, stop=True)
                mm.then_inc(S("cb_psum"), 1)
                pe.wait_ge(S("xnat_ready"), it + 1)
                for h in range(4):
                    b = h % 2
                    pe.wait_ge(S("w_ready"), it * 4 + h + 1)
                    if h >= 2:
                        pe.wait_ge(S("yn_ready"), it * 4 + h - 1)
                    for tt in range(3):
                        m = P if tt < 2 else META
                        parts = []
                        for d, st, lo, hi, at in SSD_COLS:
                            if lo <= P * tt < hi:
                                parts.append((st, at + P * tt - lo))
                        for k, (st, at) in enumerate(parts):
                            n = P if st < 2 else META
                            mm = T.matmul(ps[0:m, 2 + b, HD * tt:HD * tt + HD], SEG[0:n, b, at:at + m], XNAT[0:n, st, HD * h:HD * h + HD],
                                          start=(k == 0), stop=(k == len(parts) - 1))
                    mm.then_inc(S("y_psum"), 1)
                pe.wait_ge(S("yn_ready"), it * 4 + 4)
                for k in range(2):
                    for i in range(3):
                        n = P if i < 2 else META
                        mm = T.transpose(ps[:, 4 + k, P * i:P * i + n], YN[0:n, i, P * k:P * k + P], ident[0:n, 0:n])
                    mm.then_inc(S("yT_psum"), 1)
                pe.wait_ge(S("y_used"), it * 2 + 2 + SEED)
            stream_pe(pe, "z2", NT=T2)
            stream_pe(pe, "zb2", NT=T2)
            norm_pe(pe, "ya", T2)
            stream_pe(pe, "oa", NT=T2, need="ya")
            pe.wait_ge(S("conv31_done"), 1)
            for t in range(DT):
                mm = T.matmul(ps[:, 5, 0:T2], ones[:, :], GU[:, t, :], start=(t == 0), stop=(t == DT - 1))
            mm.then_inc(S("cf_sum"), 1)
            norm_pe(pe, "cf", T2)
            stream_pe(pe, "ob", NT=T2, need="yb")
            norm_pe(pe, "h3", T2)
            stream_pe(pe, "v", NT=T2, need="h3")
            pe.wait_ge(acc_free, ST["k"].p0 + SEED)
            for i in range(12):
                tq, kt = i // 3, i % 3
                n = P if kt < 2 else META
                if i >= 4:
                    pe.wait_ge(S("vo_ready"), i - 3)
                for k in range(4):
                    mm = T.transpose(ps[0:n, 4 + i % 4, P * k:P * k + P], KT[:, 4 * tq + k, P * kt:P * kt + n], ident[:, :])
                mm.then_inc(S("vo_psum"), 1)
            pe.wait_ge(S("vo_ready"), 12)
            stream_pe(pe, "k", NT=T2)
            stream_pe(pe, "q", NT=S1, off=META)
            pe.wait_ge(acc_free, ST["z3"].p0 + SEED)
            with pe.Fori(0, SH // 2) as it:
                for e in range(2):
                    pe.wait_ge(S("n_staged"), it * 2 + e + 1)
                    pe.wait_ge(S("bias_used"), it * 2 + e - 1 + SEED)
                    for qt in range(2):
                        mm = T.matmul(ps[:, 4 + 2 * e + qt, 0:T2], QS[0:HD, e, P * qt:P * qt + P], KS[0:HD, e, :], start=True, stop=True)
                    mm.then_inc(S("n_scores"), 1)
                for e in range(2):
                    pe.wait_ge(S("n_exp"), it * 2 + e + 1)
                    pe.wait_ge(S("n_pt"), it * 2 + e + SEED)
                    for qt in range(2):
                        for kt in range(3):
                            n = P if kt < 2 else META
                            o = ps[0:n, 0, S1 * kt + P * qt:S1 * kt + P * qt + P] if kt < 2 else ps[0:n, 1, P * qt:P * qt + P]
                            mm = T.transpose(o, SO[:, e, qt, P * kt:P * kt + n], ident[:, :])
                    mm.then_inc(S("n_ptpsum"), 1)
                    pe.wait_ge(S("n_pt"), it * 2 + e + 1 + SEED)
                    pe.wait_ge(S("n_acc"), it * 2 + e - 1 + SEED)
                    for qt in range(2):
                        for kt in range(3):
                            n = P if kt < 2 else META
                            w = PT1[:, kt, P * qt:P * qt + P] if kt < 2 else PT2[0:META, P * qt:P * qt + P]
                            mm = T.matmul(ps[:, 2 + e, HD * qt:HD * qt + HD], w, VO[0:n, kt, ds(it * P + HD * e, HD)],
                                          start=(kt == 0), stop=(kt == 2))
                    mm.then_inc(S("n_pv"), 1)
            pe.wait_ge(S("n_acc"), SH + SEED)
            for i in range(8):
                if i >= 4:
                    pe.wait_ge(S("oT3_ready"), i - 3)
                for k in range(2):
                    for qt in range(2):
                        mm = T.transpose(ps[:, 4 + i % 4, 256 * k + P * qt:256 * k + P * qt + P], QO[:, 2 * i + k, P * qt:P * qt + P], ident[:, :])
                mm.then_inc(S("oT3_psum"), 1)
            stream_pe(pe, "z3", NT=S1, off=META)
            stream_pe(pe, "o3", NT=S1, need="o3")
            norm_pe(pe, "fin2", S1)
            pe.wait_ge(S("xf_ready"), DT)
            for i in range(8):
                if i >= 4:
                    pe.wait_ge(S("out_ready"), i - 3)
                for k in range(4):
                    mm = T.transpose(ps[:, 4 + i % 4, P * k:P * k + P], XF[:, 4 * (i // 2) + k, P * (i % 2):P * (i % 2) + P], ident[:, :])
                mm.then_inc(S("out_psum"), 1)


_INS = ["x", "p", "norm_g", "w_in", "cmp_pe_k", "cmp_w1_k", "cmp_w2_k", "cmp_pe_v", "cmp_w1_v", "cmp_w2_v", "ln_v_g",
        "ln_v_b", "sgu_w", "sgu_b", "w_up_a", "w_up_b", "w_out", "w_ple", "w_ple_gate", "final_g", "meta_tokens_2",
        "e_norm_g_2", "e_w_in_2", "e_conv_w_2", "e_conv_b_2", "e_dt_bias_2", "e_A_log_2", "e_D_2", "e_ssd_norm_g_2",
        "e_dw_w_2", "e_dw_b_2", "e_ln_g_2", "e_ln_b_2", "e_w_out_2", "o_norm_g_2", "o_w_in_2", "o_rpb_2", "o_w_out_2",
        "final_norm_g_2"]


def kernel(**inputs):
    import numpy as np
    import concourse.bacc as bacc
    from concourse.bass_utils import run_bass_kernel_spmd

    nc = bacc.Bacc("TRN2", target_bir_lowering=False, num_devices=1)
    arrays, aps = {}, {}
    for name in _INS:
        a = np.ascontiguousarray(inputs[name])
        arrays[f"in_{name}_dram"] = a
        aps[name] = nc.dram_tensor(f"in_{name}_dram", a.shape, mybir.dt.from_np(a.dtype), kind="ExternalInput").ap()
    out = nc.dram_tensor("out_0_dram", (1, S1, D), F, kind="ExternalOutput").ap()
    build(nc, aps, out)
    r = run_bass_kernel_spmd(nc, [arrays], core_ids=[0])
    return r.results[0]["out_0_dram"]
```

```python
from contextlib import ExitStack, contextmanager

import concourse.bass as bass
from concourse import mybir

F = mybir.dt.float32
R = mybir.dt.float32r
ALU = mybir.AluOpType
ACT = mybir.ActivationFunctionType
AX = mybir.AxisListType
ds = bass.ds

P = 128
D = 2048
DT = D // P
S1 = 256
META = 16
T2 = S1 + META
HD = 64
NEG = -1e30

HEADS, GROUPS = 16, 4
CMP_LEN, CMP_STRIDE = 32, 16
NC = S1 // CMP_STRIDE - 1
AW = HEADS * HD
PLE = 256
BW = 1024
BG = 8
EPS1 = 1e-6
SH, SG, SN = 32, 8, 128
K5, K31 = 5, 31
EPS2 = 1e-5
GRID = 64
KH, KWIN = 4, 16

C_GATE = AW + 6 * GROUPS * HD
C_ZA = C_GATE + 3 * HEADS
C_UV = C_ZA + AW
C_ZB = C_UV + 2 * BW
C_MERGE = C_ZB + BW
E_Z, E_XS, E_BC, E_DT = 0, D, 2 * D, 3 * D
E_ZB = E_DT + 2 * SH
E_GV = E_ZB + D
E_GG = E_GV + D

(R_NORM, R_FINAL, R_ENORM, R_SSD, R_ONORM, R_FNORM, R_LNG, R_LNB, R_DWB, R_LNV) = range(10)
R_DW = 10
R_CW = R_DW + K31
R_CB = R_CW + 2 * K5
R_META = R_CB + 2
NROW = R_META + META

CH = 2048
CUT = 1024
RING = 4
SEED = 3

_STREAMS = [("kvc", 1, 4, 2), ("qa", 1, 4, 2), ("qb", 1, 4, 2), ("kvs", 1, 4, 2), ("gate", 0, 1, 1), ("kvw", 1, 4, 2), ("za", 2, 8, 4), ("uv", 4, 16, 8), ("zb", 2, 8, 4),
            ("merge", 8, 32, 16), ("upa", 2, 8, 8), ("upb", 2, 8, 8), ("ple", 0, 2, 8),
            ("out1", 4, 16, 8), ("pgate", 4, 16, 8),
            ("gv", 4, 16, 8), ("dt", 0, 1, 1), ("gg", 4, 16, 8), ("xs", 4, 16, 8), ("bc", 4, 16, 8),
            ("zb2", 4, 16, 8), ("z2", 4, 16, 8), ("oa", 4, 16, 8), ("ob", 4, 16, 8),
            ("v", 4, 16, 8), ("k", 4, 16, 8), ("q", 4, 16, 8), ("z3", 4, 16, 8), ("o3", 4, 16, 8)]


class Stream:
    def __init__(self, name, its, chunks, pairs, c0, p0):
        self.name, self.its, self.chunks, self.pairs, self.c0, self.p0 = name, its, chunks, pairs, c0, p0
        self.end = c0 + chunks
        self.ppi = pairs // its if its else pairs


ST = {}
_c = _p = 0
for _n, _i, _k, _q in _STREAMS:
    ST[_n] = Stream(_n, _i, _k, _q, _c, _p)
    _c += _k
    _p += _q
CHUNKS = _c

_SPLITS = [("h1", 4), ("oa1", 4), ("ob1", 4), ("p", 1), ("merged", 4), ("x1", 4), ("h2", 4), ("ya", 4),
           ("yb", 4), ("h3", 4), ("o3", 4)]
SPL = {}
_g = 0
for _n, _k in _SPLITS:
    SPL[_n] = (_g, _k)
    _g += _k


SSD_COLS = [(0, 0, 0, T2, 0), (0, 1, P, T2, 272), (1, 0, 0, P, 416), (1, 1, 0, 2 * P, 544),
            (0, 2, 2 * P, T2, 800), (1, 2, 0, T2, 816)]

TMPC = {"gg": 0, "z2": 8}


class Lin:

    def __init__(self, it, m, a):
        self.it, self.m, self.a = it, m, a

    def __mul__(self, k):
        return Lin(self.it, self.m * k, self.a * k)

    def __add__(self, c):
        return self.it * self.m + (self.a + c)


class Steps:

    def __init__(self, eng, sem):
        self.eng, self.sem, self.n, self.it, self.per = eng, sem, 0, None, 0

    def do(self, ins):
        ins.then_inc(self.sem, 1)
        self.n += 1

    def sync(self, back=0):
        at = self.n - back
        if self.it is not None:
            at = self.it * self.per + (self.n - back - self.lo * self.per)
        self.eng.wait_ge(self.sem, at)

    @contextmanager
    def loop(self, lo, hi, per):
        start = self.n
        with self.eng.Fori(lo, hi) as it:
            self.it, self.per, self.lo = it, per, lo
            yield it
            assert self.n - start == per, f"{self.n - start} steps in an iteration"
        self.it = None
        self.n = start + per * (hi - lo)


def build(nc, A, out):
    with ExitStack() as ctx:
        def sb(name, shape, dt=F):
            return ctx.enter_context(nc.sbuf_tensor(name, shape, dt))

        sems = {}

        def S(name):
            if name not in sems:
                sems[name] = ctx.enter_context(nc.semaphore(name))
            return sems[name]

        raw = [sb(f"raw{i}", [P, CH]) for i in range(RING)]
        whi = [sb(f"whi{i}", [P, CH], R) for i in range(2)]
        wlo = [sb(f"wlo{i}", [P, CH], R) for i in range(2)]
        MH = sb("op_hi", [P, DT, T2], R)
        ML = sb("op_lo", [P, DT, T2], R)
        RES = sb("residual", [P, DT, T2])
        PC = sb("param_cols", [P, DT, NROW])
        ident = sb("ident", [P, P])
        ones = sb("ones", [P, P])
        triF = sb("tri_f", [P, P])
        triB = sb("tri_b", [P, P])
        rstd = sb("rstd", [P, T2])
        ms = sb("ms", [P, T2])
        slopes = sb("slopes", [P, HEADS])
        nslopes = sb("nslopes", [P, HEADS])
        gates = sb("gates", [P, 2, 3 * HEADS])
        small = sb("small", [P, 64])
        Dcol = sb("d_cols", [P, DT])
        AN = 20352
        arena = sb("arena", [P, AN])
        ps = ctx.enter_context(nc.psum_tensor("ps", [P, 8, 512], F))

        def ar(off, *dims):
            n = 1
            for d in dims:
                n *= d
            assert off + n <= AN, (off, dims)
            v = arena[:, off:off + n]
            if len(dims) == 1:
                return v
            names = "abcd"[:len(dims)]
            kw = {names[i]: dims[i] for i in range(len(dims))}
            return v.rearrange(f"p ({' '.join(names)}) -> p {' '.join(names)}", **kw)

        SQX = ar(16724, 2, 4, T2)
        xnat = ar(0, 2, D)
        PR = ar(11392, D)
        qkvT = ar(0, 20, S1)
        Vn = ar(5120, 2, 2, S1)
        KSg = ar(6144, 2, GROUPS, S1)
        QSg = ar(8192, 2, S1)
        SCb = ar(8704, 2, 384)
        Eb = ar(9472, 2, 384)
        PTb = ar(10240, 2, 384)
        DM = ar(19860, 384)
        ON = ar(11392, 2, AW)
        W1 = [ar(6144, CMP_LEN, P), ar(10240, CMP_LEN, P)]
        W2 = [ar(5120, P), ar(5248, P)]
        peT = ar(5376, 2, CMP_LEN)
        KB = ar(18900, 2, NC, CMP_LEN)
        KST = ar(13440, 2, S1)
        VCB = ar(14400, 2, 512)
        Pc = ar(15424, 2, HEADS, NC)
        PcT = ar(15904, 2, 2, P)
        BC = ar(16416, 2, HEADS, NC)
        MC = ar(16896, 2, HEADS, NC)
        KCD = ar(17376, GROUPS, NC)
        VCN = ar(17440, S1)
        hid = ar(17700, 2, NC)
        dcb = ar(18060, 2, NC)
        dc_i = ar(18100, 2 * NC)
        DMi = ar(18140, 384)
        cmx = ar(18540, 32)
        cz = ar(18580, 32)
        cco = ar(18620, 32)
        ZA = ar(0, 8, S1)
        UV = ar(2048, 16, S1)
        Vv = ar(4096, 8, S1)
        ZB = ar(6144, 8, S1)
        SQv = ar(8192, 8, S1)
        VN = ar(8192, 2, 8, P)
        SGB = ar(10240, 8, P)
        WS = ar(13440, 8, P)
        WST = ar(14464, 8, P)
        SGB2 = ar(15488, 2, S1)
        GM = ar(8192, 32, S1)
        PLEb = ar(0, 16, S1)
        G2 = ar(4096, 16, S1)
        pnat = ar(16384, 2, PLE)
        pT = ar(16896, 2, S1)
        PH, PL = MH[:, 0:2, 0:S1], ML[:, 0:2, 0:S1]
        GU = ar(0, DT, T2)
        XBC = ar(4352, 32, T2)
        XS = ar(4352, DT, T2)
        ZB2 = ar(8704, DT, T2)
        q = 13056
        ROWS = ar(q, 2, 2, 2, T2)
        TRI = ar(q, 2, 3, T2)
        q += 2176
        SEG = ar(q, 2, 1088)
        q += 2176
        CBM = ar(q, 1088)
        q += 1088
        XST = ar(q, 2, T2)
        BS = ar(q + 2 * T2, T2)
        q += 3 * T2
        XNAT = ar(q, 3, S1)
        assert q + 768 <= AN
        CSUM = sb("conv_sum", [P, T2])
        dtN = sb("dt_nat", [P, 3, 2 * SH])
        cN = sb("cum_nat", [P, 3, 2 * SH])
        sp = [ar(15240 + 192 * i, 3, 2 * SH) for i in range(6)]
        aN = ar(15240 + 192 * 6, 3, 2 * SH)
        alog = ar(15240 + 192 * 7, 2 * SH)
        dtb = ar(15240 + 192 * 7 + 64, 2 * SH)
        CF = ar(13056 + 4352, 2, T2)
        TMP = ar(16724, 2, 2, T2)
        CS = ar(20080, T2)
        ACC = ar(16180, 2, T2)
        KT = ar(0, DT, T2)
        VO = ar(4352, 3, D)
        QO = ar(10496, DT, S1)
        q = 14592
        BIAS = ar(q, 2, 2, T2)
        SO = ar(q + 4 * T2, 2, 2, T2)
        q += 8 * T2
        PT1 = ar(q, 2, S1)
        PT2 = ar(q + 512, S1)
        QS = ar(q + 768, 2, S1)
        KS = ar(q + 1280, 2, T2)
        MW = ar(q + 1824, GRID)
        TAB = ar(14592, 7, P)
        onat = ar(0, 2, D)
        XF = ar(4352, DT, S1)

        tab_dram = nc.dram_tensor("rpb_table", [SH, 7, P], F, kind="Internal").ap()
        bias_dram = nc.dram_tensor("bias_by_column", [SH, GRID, 7, GRID], F, kind="Internal").ap()
        cum_dram = nc.dram_tensor("cum_rows", [2 * SH, T2], F, kind="Internal").ap()

        W_in = A["w_in"][0].rearrange("(t p) n -> p t n", p=P)
        W_ein = A["e_w_in_2"][0].rearrange("(t p) n -> p t n", p=P)
        W_eout = A["e_w_out_2"][0].rearrange("(t p) n -> p t n", p=P)
        W_oin = A["o_w_in_2"][0].rearrange("(t p) n -> p t n", p=P)
        W_oout = A["o_w_out_2"][0].rearrange("(t p) n -> p t n", p=P)
        W_up = {k: A[f"w_up_{k}"][0].rearrange("(t p) n -> p t n", p=P) for k in "ab"}
        W_out = A["w_out"][0].rearrange("(t p) n -> p t n", p=P)
        W_pg = A["w_ple_gate"][0].rearrange("(t p) n -> p t n", p=P)
        W_ple = A["w_ple"][0].rearrange("(t p) n -> p t n", p=P)
        SRC = {"kvc": (W_in, AW, 0), "qa": (W_in, 0, 0), "qb": (W_in, AW // 2, 0),
               "kvs": (W_in, AW + 512, 0), "kvw": (W_in, AW + 1024, 0), "za": (W_in, C_ZA, 0), "uv": (W_in, C_UV, 0), "zb": (W_in, C_ZB, 0),
               "merge": (W_in, C_MERGE, 0), "upa": (W_up["a"], 0, 0), "upb": (W_up["b"], 0, 0),
               "out1": (W_out, 0, 0), "pgate": (W_pg, 0, 0), "gv": (W_ein, E_GV, 0),
               "gg": (W_ein, E_GG, 0), "xs": (W_ein, E_XS, 0), "bc": (W_ein, E_BC, 0),
               "z2": (W_ein, E_Z, 0), "zb2": (W_ein, E_ZB, 0), "oa": (W_eout, 0, 0),
               "ob": (W_eout, 0, DT), "v": (W_oin, 2 * D, 0), "k": (W_oin, D, 0), "q": (W_oin, 0, 0),
               "z3": (W_oin, 3 * D, 0), "o3": (W_oout, 0, 0)}

        wide = [r[:, :].rearrange("p (t n) -> p t n", t=8) for r in raw]
        hi8 = [r[:, :].rearrange("p (t n) -> p t n", t=8) for r in whi]
        lo8 = [r[:, :].rearrange("p (t n) -> p t n", t=8) for r in wlo]
        landed = [S(f"chunk_landed_{i}") for i in range(RING)]
        hi_ready, lo_dve, lo_pool, chunk_done = S("hi_ready"), S("lo_dve"), S("lo_pool"), S("chunk_done")
        acc_free = S("acc_free")
        src_ready, mh_ready, ml_ready = S("src_ready"), S("mh_ready"), S("ml_ready")

        def lo_wait(eng, c0, it, upto):
            eng.wait_ge(lo_dve, it * 4 + (c0 + upto + 1))
            eng.wait_ge(lo_pool, it * 4 + (c0 + upto + 1))

        def load_chunk(sp_eng, s, it, i, dst, src):
            c = s.c0 + i
            if not isinstance(it, int) or c + 4 * it >= RING:
                lo_wait(sp_eng, s.c0, it, i - RING)
            sp_eng.dma_start(dst, src).then_inc(landed[c % RING], 16)

        def load_stream(sp_eng, name, between=None):
            s = ST[name]
            w, col, row = SRC[name]
            per = s.chunks // s.pairs

            def body(it):
                for i in range(4):
                    r = row + 8 * (i % per)
                    at = it * (s.ppi * 256) + (col + 256 * (i // per))
                    cols = ds(at, 256) if not isinstance(at, int) else slice(at, at + 256)
                    load_chunk(sp_eng, s, it, i, wide[(s.c0 + i) % RING], w[:, r:r + 8, cols])
                    if between is not None:
                        between(it, i)

            if s.its == 1:
                body(0)
            else:
                with sp_eng.Fori(0, s.its) as it:
                    body(it)

        def split_hi(act, s, it, i):
            c = s.c0 + i
            if isinstance(it, int) and c + 4 * it >= CHUNKS:
                return
            act.wait_ge(landed[c % RING], it * 16 + 16 * (c // RING + 1))
            if not isinstance(it, int) or c + 4 * it >= 2:
                act.wait_ge(chunk_done, it * 4 + c - 1)
            nc.scalar.activation(whi[c % 2][:, :], raw[c % RING][:, :], ACT.Copy).then_inc(hi_ready, 1)

        def split_lo(eng, s, it, i, eng_is_dve):
            c = s.c0 + i
            cut = CUT // 2 if s.name in ("xs", "bc") else CUT
            own, sem, part = (nc.vector, lo_dve, slice(0, cut)) if eng_is_dve else (nc.gpsimd, lo_pool, slice(cut, CH))
            if isinstance(it, int) and c + 4 * it >= CHUNKS:
                return
            eng.wait_ge(hi_ready, it * 4 + c + 1)
            own.tensor_tensor(wlo[c % 2][:, part], raw[c % RING][:, part], whi[c % 2][:, part].bitcast(F),
                              ALU.subtract).then_inc(sem, 1)

        def halves(eng, kind, s, it, i):
            if kind == "act":
                split_hi(eng, s, it, i)
            else:
                split_lo(eng, s, it, i, kind == "dve")

        def run_loop(eng, s, body, steps=None, per=0):
            if s.its == 1:
                body(0)
                return
            hi = s.its - 1 if s.end == CHUNKS else s.its
            if steps is None:
                with eng.Fori(0, hi) as it:
                    body(it)
            else:
                with steps.loop(0, hi, per) as it:
                    body(it)
            if hi < s.its:
                body(hi)

        def evacuate(eng, s, it, i, evac):
            j = (i + 1) // (4 // s.ppi) - 1
            eng.wait_ge(chunk_done, it * 4 + s.c0 + i + 1)
            evac(it, j, (s.p0 + j) % 2)

        def stream_side(eng, kind, name, evac=None, steps=None, per=0, extra=None):
            s = ST[name]

            def body(it):
                n = s.ppi
                for i in range(4):
                    halves(eng, kind, s, it, i + 2)
                    if (i + 1) % (4 // n) == 0 and evac is not None:
                        evacuate(eng, s, it, i, evac)
                    if extra is not None:
                        extra(it, i)

            run_loop(eng, s, body, steps, per)

        def multiply(pe, s, it, i, n, NT, off=0, tile0=0, need=None):
            cpp = s.chunks // s.pairs
            c = s.c0 + i
            j = i // cpp
            b = 2 * ((s.p0 + j) % 2)
            if n == 0:
                if i % cpp == 0:
                    pe.wait_ge(acc_free, it * s.ppi + s.p0 + j - 1 + SEED)
                lo_wait(pe, s.c0, it, i)
            for k in range(8):
                t = tile0 + 8 * (i % cpp) + k
                if need is not None and n == 0 and j == 0:
                    g0, groups = SPL[need]
                    per = 8 * cpp // groups
                    if (t - tile0) % per == 0:
                        pe.wait_ge(ml_ready, g0 + (t - tile0) // per + 1)
                wh = hi8[c % 2][:, k, n * P:(n + 1) * P]
                wl = lo8[c % 2][:, k, n * P:(n + 1) * P]
                xh, xl = MH[:, t, off:off + NT], ML[:, t, off:off + NT]
                o = ps[:, b + n, 0:NT]
                nc.tensor.matmul(o, wh, xh, start=(i % cpp == 0 and k == 0), stop=False)
                nc.tensor.matmul(o, wh, xl, start=False, stop=False)
                mm = nc.tensor.matmul(o, wl, xh, start=False, stop=(i % cpp == cpp - 1 and k == 7))
            if n == 1:
                mm.then_inc(chunk_done, 1)

        def stream_pe(pe, name, NT=S1, off=0, tile0=0, need=None):
            s = ST[name]

            def body(it):
                for i in range(4):
                    for n in range(2):
                        multiply(pe, s, it, i, n, NT, off, tile0, need)

            if s.its == 1:
                body(0)
            else:
                with pe.Fori(0, s.its) as it:
                    body(it)

        def natural(pe, name, toks, n):
            s = ST[name]
            c = s.c0
            pe.wait_ge(acc_free, s.p0 - 1 + SEED)
            lo_wait(pe, c, 0, 0)
            wh = whi[c % 2][:, 0:DT * n].rearrange("p (t n) -> p t n", t=DT)
            wl = wlo[c % 2][:, 0:DT * n].rearrange("p (t n) -> p t n", t=DT)
            for i, (tok, m) in enumerate(toks):
                o = ps[0:m, 2 * (s.p0 % 2), n * i:n * i + n]
                for t in range(DT):
                    xh, xl = MH[:, t, tok:tok + m], ML[:, t, tok:tok + m]
                    nc.tensor.matmul(o, xh, wh[:, t, :], start=(t == 0), stop=False)
                    nc.tensor.matmul(o, xl, wh[:, t, :], start=False, stop=False)
                    mm = nc.tensor.matmul(o, xh, wl[:, t, :], start=False, stop=(t == DT - 1))
            mm.then_inc(chunk_done, 1)

        def pairof(par):
            return slice(2 * par, 2 * par + 2)

        def split_op_act(act, name, src, hi, per, free_at=0, only=None):
            g0, n = SPL[name]
            if free_at:
                act.wait_ge(chunk_done, free_at)
            for g in range(n) if only is None else [only]:
                act.wait_ge(src_ready, g0 + g + 1)
                nc.scalar.activation(hi(g), src(g), ACT.Copy).then_inc(mh_ready, 1)

        def split_op_dve(dve, name, src, hi, lo, g):
            g0, n = SPL[name]
            dve.wait_ge(mh_ready, g0 + g + 1)
            nc.vector.tensor_tensor(lo(g), src(g), hi(g).bitcast(F), ALU.subtract).then_inc(ml_ready, 1)

        def op(t, NT, n=4, tile0=0, off=0):
            return lambda g: t[:, tile0 + n * g:tile0 + n * (g + 1), off:off + NT]

        norm_sq, norm_sqfree = S("norm_sq"), S("norm_sqfree")
        norm_half, norm_ms, norm_rt = S("norm_half"), S("norm_ms"), S("norm_rt")
        NORM = {n: i for i, n in enumerate(["h1", "fin1", "h2", "ya", "cf", "h3", "fin2"])}

        def norm_act(act, name, src, NT, by_group=None):
            e = NORM[name]
            for g in range(4):
                if by_group is not None:
                    act.wait_ge(by_group, g + 1)
                if e or g >= 2:
                    act.wait_ge(norm_sqfree, 4 * e + g - 1)
                nc.scalar.activation(SQX[:, g % 2, :, 0:NT], src(g), ACT.Square).then_inc(norm_sq, 1)
            act.wait_ge(norm_ms, e + 1)
            nc.scalar.activation(rstd[:, 0:NT], ms[:, 0:NT], ACT.Sqrt).then_inc(norm_rt, 1)

        def norm_pe(pe, name, NT, bank=4):
            e = NORM[name]
            for g in range(4):
                pe.wait_ge(norm_half, 4 * e + g + 1)
                for t in range(2):
                    mm = nc.tensor.matmul(ps[:, bank, 0:NT], ones[:, :], SQX[:, g % 2, t, 0:NT],
                                          start=(g == 0 and t == 0), stop=(g == 3 and t == 1))
                mm.then_inc(norm_sqfree, 1)

        def norm_dve(dve, v, name, NT, eps, bank=4, width=D):
            e = NORM[name]
            for g in range(4):
                dve.wait_ge(norm_sq, 4 * e + g + 1)
                nc.vector.tensor_tensor(SQX[:, g % 2, 0:2, 0:NT], SQX[:, g % 2, 0:2, 0:NT], SQX[:, g % 2, 2:4, 0:NT],
                                        ALU.add).then_inc(norm_half, 1)
            dve.wait_ge(norm_sqfree, 4 * e + 4)
            nc.vector.tensor_scalar(ms[:, 0:NT], ps[:, bank, 0:NT], 1.0 / width, eps, ALU.mult,
                                    ALU.add).then_inc(norm_ms, 1)
            dve.wait_ge(norm_rt, e + 1)
            v.do(nc.vector.reciprocal(rstd[:, 0:NT], rstd[:, 0:NT]))
            v.sync()

        def apply_dve(dve, v, name, src, row, NT, off=0, dst=None):
            g0, _ = SPL[name]
            at = (lambda g: SQX[:, g % 2, :, 0:NT]) if dst is None else dst
            for g in range(5):
                if g < 4:
                    if g >= 2 and dst is None:
                        dve.wait_ge(ml_ready, g0 + g - 1)
                    for t in range(4):
                        ins = nc.vector.scalar_tensor_tensor(
                            out=at(g)[:, t, :], in0=src(g)[:, t, :], scalar=PC[:, 4 * g + t, row:row + 1],
                            in1=rstd[:, 0:NT], op0=ALU.mult, op1=ALU.mult)
                    ins.then_inc(src_ready, 1)
                if g >= 1:
                    split_op_dve(dve, name, at, op(MH, NT), op(ML, NT), g - 1)

        block = ctx.enter_context(nc.Block())

        @block.sync
        def _(sp_eng):
            nc.sync.dma_start(xnat, A["x"][0].rearrange("(t p) n -> p t n", p=P)).then_inc(S("x_landed"), 16)
            rows = [("norm_g", R_NORM), ("e_norm_g_2", R_ENORM), ("e_ssd_norm_g_2", R_SSD),
                    ("o_norm_g_2", R_ONORM), ("e_ln_g_2", R_LNG), ("e_ln_b_2", R_LNB), ("e_dw_b_2", R_DWB)]
            srcs = [(A[n], r, 1) for n, r in rows]
            srcs += [(A["final_g"].rearrange("(a n) -> a n", a=1), R_FINAL, 1),
                     (A["final_norm_g_2"].rearrange("(a n) -> a n", a=1), R_FNORM, 1),
                     (A["e_dw_w_2"][0], R_DW, K31),
                     (A["e_conv_w_2"][0].rearrange("k (h n) -> (k h) n", h=2), R_CW, 2 * K5),
                     (A["e_conv_b_2"].rearrange("a (h n) -> (a h) n", h=2), R_CB, 2),
                     (A["meta_tokens_2"], R_META, META)]
            for src, r, n in srcs:
                nc.sync.dma_start(PR[r:r + n, :], src).then_inc(S("params_landed"), 16)
            nc.sync.dma_start(PR[R_LNV:R_LNV + 1, 0:BW], A["ln_v_g"]).then_inc(S("params_landed"), 16)
            nc.sync.dma_start(PR[R_LNV:R_LNV + 1, BW:D], A["ln_v_b"]).then_inc(S("params_landed"), 16)
            for n in ("kvc", "qa", "qb", "kvs"):
                load_stream(sp_eng, n)
            s = ST["gate"]
            load_chunk(sp_eng, s, 0, 0, raw[s.c0 % RING][:, 0:DT * 48].rearrange("p (t n) -> p t n", t=DT),
                       W_in[:, :, C_GATE:C_ZA])
            for n in ("kvw", "za", "uv", "zb", "merge", "upa", "upb"):
                load_stream(sp_eng, n)
            s = ST["ple"]
            for i in range(2):
                load_chunk(sp_eng, s, 0, i, raw[(s.c0 + i) % RING][:, :].rearrange("p (t n) -> p t n", t=2),
                           W_ple[:, :, 1024 * i:1024 * i + 1024])
            for n in ("out1", "pgate", "gv"):
                load_stream(sp_eng, n)
            s = ST["dt"]
            load_chunk(sp_eng, s, 0, 0, raw[s.c0 % RING][:, 0:DT * 64].rearrange("p (t n) -> p t n", t=DT),
                       W_ein[:, :, E_DT:E_ZB])
            for n in ("gg", "xs", "bc"):
                load_stream(sp_eng, n)
            sp_eng.wait_ge(S("cum_rows_ready"), 2)
            for d in range(2):
                nc.sync.dma_start(cum_dram[d * SH:(d + 1) * SH, :], CF[0:SH, d, :]).then_inc(S("cum_stored"), 16)
            sp_eng.wait_ge(S("cum_stored"), 32)
            sp_eng.wait_ge(S("tri_free"), 1)

            def load_rows(it, gg):
                G = Lin(it, 2, gg)
                for hp in range(2):
                    sp_eng.wait_ge(S("rows_used"), G * 4 + (2 * hp - 2 + SEED))
                    src = bass.AP(cum_dram.tensor, G * (4 * T2) + hp * 2 * T2,
                                  [[0, P], [SH * T2, 2], [T2, 2], [1, T2]])
                    nc.sync.dma_start(ROWS[:, hp], src).then_inc(S(f"rows_landed_{hp}"), 16)

            load_stream(sp_eng, "zb2", between=lambda it, i: load_rows(it, i // 2) if i % 2 else None)
            for n in ("z2", "oa", "ob", "v", "k", "q"):
                load_stream(sp_eng, n)

            def load_bias(it, i):
                G = Lin(it, 4, i)
                for e in range(2):
                    sp_eng.wait_ge(S("bias_used"), G * 2 + (e - 1 + SEED))
                    for qt in range(2):
                        for r in range(2):
                            row = KH - 1 - 2 * qt - r
                            src = bias_dram[ds(G * 2 + e, 1), :, row:row + KH, :].rearrange("a q j c -> (a q) (j c)")
                            dst = BIAS[GRID * r:GRID * (r + 1), e, qt, META:T2]
                            nc.sync.dma_start(dst, src).then_inc(S(f"bias_landed_{e}"), 16)

            load_stream(sp_eng, "z3", between=load_bias)
            load_stream(sp_eng, "o3")
            for part in range(4):
                cols = slice(512 * part, 512 * part + 512)
                sp_eng.wait_ge(S("out_ready"), 2 * part + 2)
                nc.sync.dma_start(out[0].rearrange("(t p) n -> p t n", p=P)[:, :, cols], onat[:, :, cols]) \
                    .then_inc(S("out_stored"), 16)
            sp_eng.wait_ge(S("out_stored"), 4 * 16)

        @block.gpsimd
        def _(pool):
            g = Steps(pool, S("pool_step"))

            def side(name):
                stream_side(pool, "pool", name)

            def one(name, chunks=1):
                for i in range(chunks):
                    halves(pool, "pool", ST[name], 0, i + 2)

            def diag(t, cmp, step):
                nc.gpsimd.affine_select(out=t[:, :], in_=ones[:, :], compare_op=cmp, fill=0.0, base=0,
                                        pattern=[[step, P]], channel_multiplier=-step).then_inc(S("consts_ready"), 1)

            g.do(nc.gpsimd.memset(ones[:, :], 1.0))
            g.sync()
            diag(ident, ALU.is_equal, 1)
            diag(triF, ALU.is_ge, 1)
            diag(triB, ALU.is_ge, -1)
            for h in range(HEADS):
                sl = 2.0 ** (-8.0 * (h + 1) / HEADS)
                nc.gpsimd.memset(slopes[:, h:h + 1], sl)
                ins = nc.gpsimd.memset(nslopes[:, h:h + 1], -sl)
            ins.then_inc(S("slopes_ready"), 1)

            def zero_w1(j):
                g.do(nc.gpsimd.memset(W1[j], 0.0))
                g.do(nc.gpsimd.memset(W2[j], 0.0))
                g.sync()
                pool.sem_inc(S("w1_zeroed"), 1)

            zero_w1(0)
            halves(pool, "pool", ST["kvc"], 0, 0)
            halves(pool, "pool", ST["kvc"], 0, 1)
            pool.wait_ge(S("pc_ready"), 4)
            zero_w1(1)
            side("kvc")
            side("qa")
            pool.wait_ge(ml_ready, sum(SPL["h1"]))
            dci = dc_i.bitcast(mybir.dt.int32).rearrange("p (a n) -> p a n", a=2)
            g.do(nc.gpsimd.iota(dci, pattern=[[P, 2], [-CMP_STRIDE, NC]], base=-(CMP_LEN - 1), channel_multiplier=1))
            dmi = DMi.bitcast(mybir.dt.int32)
            g.do(nc.gpsimd.iota(dmi[:, 0:P], pattern=[[-1, P]], base=0, channel_multiplier=1))
            g.do(nc.gpsimd.iota(dmi[:, P:384], pattern=[[-1, S1]], base=P, channel_multiplier=1))
            g.do(nc.gpsimd.memset(MC, 1.0))
            g.do(nc.gpsimd.memset(VCB, 0.0))
            g.sync()
            g.do(nc.gpsimd.tensor_copy(dcb, dci))
            g.do(nc.gpsimd.affine_select(out=MC, in_=MC, compare_op=ALU.is_ge, fill=0.0, base=-(CMP_LEN - 1),
                                         pattern=[[P, 2], [0, HEADS], [-CMP_STRIDE, NC]], channel_multiplier=1))
            g.do(nc.gpsimd.tensor_copy(DM, dmi))
            g.sync()
            big = -NEG * 256.0
            g.do(nc.gpsimd.affine_select(out=DM[:, 0:P], in_=DM[:, 0:P], compare_op=ALU.is_ge, fill=big, base=0,
                                         pattern=[[-1, P]], channel_multiplier=1))
            g.do(nc.gpsimd.affine_select(out=DM[:, P:384], in_=DM[:, P:384], compare_op=ALU.is_ge, fill=big, base=P,
                                         pattern=[[-1, S1]], channel_multiplier=1))
            g.do(nc.gpsimd.tensor_tensor(
                BC, dcb.unsqueeze(2).to_broadcast([P, 2, HEADS, NC]),
                nslopes[:, :].unsqueeze(1).unsqueeze(3).to_broadcast([P, 2, HEADS, NC]), ALU.mult))
            g.sync()
            g.do(nc.gpsimd.affine_select(out=BC, in_=BC, compare_op=ALU.is_ge, fill=NEG, base=-(CMP_LEN - 1),
                                         pattern=[[P, 2], [0, HEADS], [-CMP_STRIDE, NC]], channel_multiplier=1))
            g.sync()
            pool.sem_inc(S("masks_ready"), 1)
            side("qb")
            side("kvs")
            one("gate")
            side("kvw")
            for n in ("za", "uv", "zb", "merge", "upa", "upb"):
                side(n)
            one("ple", 2)
            for n in ("out1", "pgate", "gv"):
                side(n)
            one("dt")
            for n in ("gg", "xs", "bc", "zb2", "z2", "oa", "ob", "v"):
                side(n)
            pool.wait_ge(S("bias_stored"), 7 * 16)
            pool.wait_ge(ml_ready, sum(SPL["h3"]))
            g.do(nc.gpsimd.memset(BIAS, 0.0))
            g.do(nc.gpsimd.memset(MW, 0.0))
            g.sync()
            for half in range(2):
                m = MW[GRID * half:GRID * (half + 1), :]
                g.do(nc.gpsimd.affine_select(out=m[:, 0:48], in_=m[:, 0:48], compare_op=ALU.is_ge, fill=NEG, base=8,
                                             pattern=[[1, 48]], channel_multiplier=-1))
                g.sync()
                g.do(nc.gpsimd.affine_select(out=m[:, 16:64], in_=m[:, 16:64], compare_op=ALU.is_ge, fill=NEG,
                                             base=7 - 16, pattern=[[-1, 48]], channel_multiplier=1))
            g.sync()
            pool.sem_inc(S("bias_used"), SEED)
            side("k")
            side("q")

            def add_mask(it, i):
                G = Lin(it, 4, i)
                for e in range(2):
                    pool.wait_ge(S(f"bias_landed_{e}"), G * 64 + 64)
                    for qt in range(2):
                        b = BIAS[:, e, qt, META:T2].rearrange("p (j c) -> p j c", j=KH)
                        ins = nc.gpsimd.tensor_tensor(b, b, MW.unsqueeze(1).to_broadcast([P, KH, GRID]), ALU.add)
                    ins.then_inc(S("bias_ready"), 1)

            s = ST["z3"]
            add_mask(0, 0)

            def body(it):
                for i in range(4):
                    if not (isinstance(it, int) and i == 3):
                        add_mask(it, i + 1)
                    halves(pool, "pool", s, it, i + 2)

            with pool.Fori(0, s.its - 1) as it:
                body(it)
            body(s.its - 1)
            side("o3")

        @block.scalar
        def _(act):
            a = Steps(act, S("act_step"))

            def side(name, evac=None, **kw):
                stream_side(act, "act", name, evac, **kw)

            def one(name, chunks=1):
                for i in range(chunks):
                    halves(act, "act", ST[name], 0, i + 2)

            def tiles(dst, it, j, ppi, n=2):
                return dst[:, ds(it * (2 * ppi) + 2 * j, n), :] if not isinstance(it, int) else \
                    dst[:, 2 * ppi * it + 2 * j:2 * ppi * it + 2 * j + n, :]

            def copy_to(dst, fn, name, NT, scale=1.0):
                ppi = ST[name].ppi

                def evac(it, j, par):
                    nc.scalar.activation(tiles(dst, it, j, ppi), ps[:, pairof(par), 0:NT], fn,
                                         scale=scale).then_inc(acc_free, 1)
                return evac

            def via_tmp(fn, name, NT):
                s = ST[name]

                def evac(it, j, par):
                    act.wait_ge(S("tmp_used"), it * s.ppi + TMPC[name] + j - 1 + SEED)
                    nc.scalar.activation(TMP[:, par, :, 0:NT], ps[:, pairof(par), 0:NT], fn).then_inc(acc_free, 1)
                return evac

            for half in range(2):
                src = bass.AP(A["e_D_2"].tensor, half, [[0, HD], [2, DT]])
                nc.scalar.dma_start(Dcol[HD * half:HD * (half + 1), :], src, allow_slow_non_contiguous=True).then_inc(S("d_landed"), 16)

            halves(act, "act", ST["kvc"], 0, 0)
            halves(act, "act", ST["kvc"], 0, 1)

            def load_w1(j):
                act.wait_ge(S("w1_zeroed"), j + 1)
                nm = "kv"[j]
                for half in range(2):
                    o = slice(HD * half, HD * (half + 1))
                    nc.scalar.dma_start(W1[j][o, :, HD * half:HD * (half + 1)],
                                        A[f"cmp_w1_{nm}"][0].rearrange("l d e -> d l e")).then_inc(S(f"w1_landed_{nm}"), 16)
                    nc.scalar.dma_start(W2[j][o, HD * half:HD * (half + 1)], A[f"cmp_w2_{nm}"][0]).then_inc(S(f"w1_landed_{nm}"), 16)
                    nc.scalar.dma_start(peT[o, j, :], A[f"cmp_pe_{nm}"][0].rearrange("l d -> d l"),
                                        allow_slow_non_contiguous=True).then_inc(S(f"w1_landed_{nm}"), 16)

            def silu_hidden(j):
                act.wait_ge(S("hid_summed"), j + 1)
                if j:
                    act.wait_ge(S("kc_psum"), 1)
                nc.scalar.activation(hid, ps[:, 4, 0:2 * NC].rearrange("p (a n) -> p a n", a=2),
                                     ACT.Silu).then_inc(S("hid_ready"), 1)

            act.wait_ge(S("xT_copied"), 8)
            norm_act(act, "h1", op(RES, S1, off=META), S1)
            split_op_act(act, "h1", lambda gg: SQX[:, gg % 2, :, 0:S1], op(MH, S1), 4)
            load_w1(0)
            load_w1(1)
            side("kvc", copy_to(qkvT[:, 8:12], ACT.Copy, "kvc", S1))
            side("qa", copy_to(qkvT[:, 0:4], ACT.Copy, "qa", S1))
            silu_hidden(0)
            side("qb", copy_to(qkvT[:, 4:8], ACT.Copy, "qb", S1))
            silu_hidden(1)
            side("kvs", copy_to(qkvT[:, 12:16], ACT.Copy, "kvs", S1))
            one("gate")
            act.wait_ge(chunk_done, ST["gate"].end)
            nc.scalar.activation(gates[:, :, :], ps[:, 2 * (ST["gate"].p0 % 2), 0:96].rearrange("p (a n) -> p a n", a=2),
                                 ACT.Sigmoid).then_inc(acc_free, 1)
            act.wait_ge(S("vcn_ready"), 1)
            for h in range(HEADS):
                r = NC * (h % 8)
                nc.scalar.dma_start(VCB[r:r + NC, h // 8, (h % 8) * HD:(h % 8 + 1) * HD],
                                    VCN[0:NC, (h // 4) * HD:(h // 4 + 1) * HD]).then_inc(S("vcb_landed"), 16)
            act.wait_ge(S("cmp_shifted"), 1)
            nc.scalar.activation(Pc, Pc, ACT.Exp).then_inc(S("cmp_exp"), 1)
            side("kvw", copy_to(qkvT[:, 16:20], ACT.Copy, "kvw", S1))
            act.wait_ge(S("pct_psum"), 1)
            nc.scalar.activation(PcT[0:120], ps[0:120, 6, :].rearrange("p (a b n) -> p a b n", a=2, b=2),
                                 ACT.Copy).then_inc(S("pct_ready"), 1)
            for qb in range(2):
                for half in range(2):
                    act.wait_ge(S("oc_psum"), 2 * qb + half + 1)
                    nc.scalar.activation(ON[:, qb, 512 * half:512 * half + 512], ps[:, 4 + half, :],
                                         ACT.Copy).then_inc(S("oc_ready"), 1)
            za, za_to = ST["za"], copy_to(ZA, ACT.Copy, "za", S1)
            with act.Fori(0, GROUPS // 2) as it:
                for gg in range(2):
                    G = Lin(it, 2, gg)
                    for u in range(8):
                        b = u % 2
                        act.wait_ge(S("a_negmax"), G * 8 + (u + 1))
                        act.wait_ge(S("a_ptpsum"), G * 8 + (u - 1 + SEED))
                        nc.scalar.activation(Eb[:, b, 0:P], SCb[:, b, 0:P], ACT.Exp, bias=small[:, 2 * b:2 * b + 1],
                                             accum_out=small[:, 8 + 2 * b:9 + 2 * b])
                        nc.scalar.activation(Eb[:, b, P:384], SCb[:, b, P:384], ACT.Exp, bias=small[:, 2 * b + 1:2 * b + 2],
                                             accum_out=small[:, 9 + 2 * b:10 + 2 * b]).then_inc(S("a_exp"), 1)
                        act.wait_ge(S("a_ptpsum"), G * 8 + (u + 1 + SEED))
                        act.wait_ge(S("a_pv"), G * 8 + (u - 1 + SEED))
                        nc.scalar.activation(PTb[:, b, :], ps[:, 6, 0:384], ACT.Copy).then_inc(S("a_pt"), 1)
                        if u == 3:
                            halves(act, "act", za, it, 2 * gg + 2)
                    evacuate(act, za, it, 2 * gg + 1, za_to)
                    halves(act, "act", za, it, 2 * gg + 3)
            act.wait_ge(acc_free, ST["uv"].p0 + SEED)
            nc.scalar.activation(ZA, ZA, ACT.Silu).then_inc(S("za_silu"), 1)
            nc.scalar.dma_start(pnat, A["p"][0, 0].rearrange("(t p) n -> p t n", p=P)).then_inc(S("p_landed"), 16)
            nc.scalar.dma_start(WS, A["sgu_w"][0].rearrange("g t s -> t g s")).then_inc(S("ws_landed"), 16)
            side("uv", copy_to(UV, ACT.Gelu_apprx_tanh, "uv", S1))
            nc.scalar.dma_start(SGB, bass.AP(A["sgu_b"].tensor, 0, [[0, P], [1, BG * P]]).rearrange("p (g t) -> p g t", g=BG)) \
                .then_inc(S("sgb_landed"), 16)
            act.wait_ge(S("v_centred"), 1)
            nc.scalar.activation(SQv, Vv, ACT.Square).then_inc(S("v_sq"), 1)
            side("zb", copy_to(ZB, ACT.Silu, "zb", S1))
            act.wait_ge(S("v_ms"), 1)
            nc.scalar.activation(rstd[:, 0:S1], ms[:, 0:S1], ACT.Sqrt).then_inc(S("v_rt"), 1)
            act.wait_ge(S("oT_used"), 4)
            for i in range(4):
                act.wait_ge(S("vn_psum"), i + 1)
                nc.scalar.activation(VN[:, i // 2, 4 * (i % 2):4 * (i % 2) + 4, :],
                                     ps[:, 4 + i % 4, :].rearrange("p (a n) -> p a n", a=4), ACT.Copy).then_inc(S("vn_ready"), 1)
            act.wait_ge(S("ob_ready"), 1)
            side("merge", copy_to(GM, ACT.Sigmoid, "merge", S1))
            split_op_act(act, "oa1", op(ZA, S1, 2), op(MH, S1, 2), 4, ST["merge"].end)
            split_op_act(act, "ob1", op(ZB, S1, 2), op(MH, S1, 2, 8), 4)
            side("upa")
            side("upb")
            split_op_act(act, "p", lambda gg: pT, lambda gg: PH, 1, ST["upb"].end)
            s = ST["ple"]
            for i in range(2):
                for j in range(4 * i, 4 * i + 4):
                    act.wait_ge(S("ple_psum"), j + 1)
                    nc.scalar.activation(PLEb[:, 2 * j:2 * j + 2, :], ps[:, pairof((s.p0 + j) % 2), 0:S1], ACT.Copy).then_inc(acc_free, 1)
                halves(act, "act", s, 0, i + 2)
            split_op_act(act, "merged", op(GM, S1), op(MH, S1), 4, ST["ple"].end)
            side("out1")
            split_op_act(act, "x1", op(RES, S1, off=META), op(MH, S1), 4, ST["out1"].end)

            def pgate(it, j, par):
                nc.scalar.activation(tiles(G2, it, j, 2), ps[:, pairof(par), 0:S1], ACT.Sigmoid).then_inc(acc_free, 1)
            side("pgate", pgate)
            act.wait_ge(S("x2_ready"), 1)
            norm_act(act, "fin1", op(RES, S1, off=META), S1)
            act.wait_ge(S("block2_in"), 1)
            nc.scalar.dma_start(dtb, bass.AP(A["e_dt_bias_2"].tensor, 0, [[0, P], [1, 2 * SH]])).then_inc(S("dt_params"), 16)
            nc.scalar.dma_start(alog, bass.AP(A["e_A_log_2"].tensor, 0, [[0, P], [1, 2 * SH]])).then_inc(S("dt_params"), 16)
            norm_act(act, "h2", op(RES, T2), T2, S("block2_in"))
            split_op_act(act, "h2", lambda gg: SQX[:, gg % 2], op(MH, T2), 4, ST["pgate"].end)
            act.sem_inc(S("tmp_used"), SEED)
            side("gv", copy_to(GU, ACT.Copy, "gv", T2))
            one("dt")
            act.wait_ge(S("dtr_ready"), 1)
            act.wait_ge(S("dt_params"), 32)
            nc.scalar.activation(sp[1], sp[0], ACT.Abs).then_inc(S("sp_abs"), 1)
            act.wait_ge(S("sp_abs"), 1)
            nc.scalar.activation(sp[1], sp[1], ACT.Exp, scale=-1.0).then_inc(S("sp_exp"), 1)
            nc.scalar.activation(alog, alog, ACT.Exp).then_inc(S("sp_exp"), 1)

            side("gg", via_tmp(ACT.Sigmoid, "gg", T2))
            side("xs")
            act.wait_ge(acc_free, ST["bc"].p0 + SEED)

            def silu_xs(it, j, par):
                x = XS[:, ds(it * 4 + 2 * j, 2), :]
                nc.scalar.activation(x, x, ACT.Silu).then_inc(S("xbc_ready"), 1)
            side("bc", silu_xs)
            act.wait_ge(acc_free, ST["zb2"].p0 + SEED)
            for half in range(2):
                bc = XBC[:, 16 + 8 * half:24 + 8 * half, :]
                nc.scalar.activation(bc, bc, ACT.Silu).then_inc(S("xbc_ready"), 1)
            act.wait_ge(S("xbc_ready"), 10)
            s = ST["zb2"]

            def zb2_to(G):
                def evac(it, j, par):
                    dst = ZB2.rearrange("p (h i) n -> p i h n", h=2)[:, ds(G + 0, 1)].rearrange("p a h n -> p (a h) n")
                    nc.scalar.activation(dst, ps[:, pairof(par), 0:T2], ACT.Copy).then_inc(acc_free, 1)
                return evac

            with a.loop(0, SG // 2, 2 * 2) as it:
                for gg in range(2):
                    G = Lin(it, 2, gg)
                    nc.scalar.activation(BS, XBC[:, ds(G + 16, 1), :].rearrange("p a n -> p (a n)"), ACT.Copy)
                    nc.scalar.activation(CS, XBC[:, ds(G + 24, 1), :].rearrange("p a n -> p (a n)"), ACT.Copy)
                    nc.scalar.activation(XST, XS[:, ds(G * 2 + 0, 2), :], ACT.Copy).then_inc(S("staged"), 1)
                    act.wait_ge(S("x_psum"), G + 1)
                    a.do(nc.scalar.activation(XNAT[:, 0:2, :], ps[:, 4, :].rearrange("p (a n) -> p a n", a=2), ACT.Copy))
                    a.do(nc.scalar.activation(XNAT[0:META, 2, :], ps[0:META, 5, 0:S1], ACT.Copy))
                    a.sync()
                    act.sem_inc(S("xnat_ready"), 1)
                    for h in range(4):
                        act.wait_ge(S("seg_ready"), G * 4 + (h + 1))
                        nc.scalar.activation(SEG[:, h % 2, 0:800], SEG[:, h % 2, 0:800], ACT.Exp)
                        nc.scalar.activation(SEG[0:META, h % 2, 800:1088], SEG[0:META, h % 2, 800:1088], ACT.Exp).then_inc(S("seg_exp"), 1)
                        if h == 2:
                            halves(act, "act", s, it, 2 * gg + 2)
                    evacuate(act, s, it, 2 * gg + 1, zb2_to(G))
                    halves(act, "act", s, it, 2 * gg + 3)
            act.wait_ge(acc_free, ST["z2"].p0 + SEED)
            nc.scalar.activation(ZB2, ZB2, ACT.Silu).then_inc(S("zb2_silu"), 1)
            act.wait_ge(S("y_used"), 2 * SG + SEED)
            act.wait_ge(S("tab_zeroed"), 1)
            nc.scalar.dma_start(TAB[0:SH, :, 48:48 + 31], A["o_rpb_2"][0][:, KH:KH + 7, :]).then_inc(S("tab_landed"), 16)
            side("z2", via_tmp(ACT.Silu, "z2", T2))
            act.wait_ge(S("tmp_used"), TMPC["z2"] + 8 + SEED)
            act.wait_ge(S("tab_landed"), 16)
            nc.scalar.dma_start(tab_dram, TAB[0:SH]).then_inc(S("tab_stored"), 16)
            norm_act(act, "ya", op(XS, T2), T2)
            split_op_act(act, "ya", op(XS, T2), op(MH, T2), 4, ST["z2"].end)
            act.wait_ge(S("tab_stored"), 16)
            for row in range(7):
                nc.scalar.dma_start(bias_dram[:, :, row, :], bass.AP(tab_dram.tensor, row * P + GRID - 1,
                                                                     [[7 * P, SH], [-1, GRID], [1, GRID]])).then_inc(S("bias_stored"), 16)
            side("oa")
            norm_act(act, "cf", op(GU, T2), T2, S("cf_centred"))
            act.wait_ge(chunk_done, ST["oa"].end)
            for gq in range(5):
                if gq < 4:
                    act.wait_ge(S("cf_scaled"), gq + 1)
                    for t in range(4 * gq, 4 * gq + 4):
                        ins = nc.scalar.activation(GU[:, t, :], GU[:, t, :], ACT.Silu, bias=PC[:, t, R_LNB:R_LNB + 1])
                    ins.then_inc(S("cf_silu"), 1)
                if gq >= 1:
                    split_op_act(act, "yb", op(GU, T2), op(MH, T2), 4, only=gq - 1)
            side("ob")
            act.wait_ge(S("even_done"), 8)
            norm_act(act, "h3", op(RES, T2), T2)
            split_op_act(act, "h3", lambda gg: SQX[:, gg % 2], op(MH, T2), 4, ST["ob"].end)
            side("v", copy_to(KT, ACT.Copy, "v", T2))
            for i in range(12):
                act.wait_ge(S("vo_psum"), i + 1)
                n = P if i % 3 < 2 else META
                nc.scalar.activation(VO[0:n, i % 3, 512 * (i // 3):512 * (i // 3) + 512], ps[0:n, 4 + i % 4, :],
                                     ACT.Copy).then_inc(S("vo_ready"), 1)
            side("k", copy_to(KT, ACT.Copy, "k", T2))
            side("q", copy_to(QO, ACT.Copy, "q", S1, scale=HD ** -0.5))
            s, z3_to = ST["z3"], copy_to(KT[:, :, 0:S1], ACT.Copy, "z3", S1)
            with act.Fori(0, s.its) as it:
                for h in range(8):
                    H, e = Lin(it, 8, h), h % 2

                    def soft_exp(e, n):
                        act.wait_ge(S("n_negmax"), n)
                        for qt in range(2):
                            ins = nc.scalar.activation(SO[:, e, qt, :], SO[:, e, qt, :], ACT.Exp, bias=small[:, 16 + 2 * e + qt:17 + 2 * e + qt],
                                                       accum_out=small[:, 20 + 2 * e + qt:21 + 2 * e + qt])
                        ins.then_inc(S("n_exp"), 1)
                    def pair_done(h):
                        if h % 4 == 3:
                            evacuate(act, s, it, h // 2, z3_to)
                        halves(act, "act", s, it, h // 2 + 2)

                    soft_exp(e, H + 1)
                    if e == 0 and h > 0:
                        pair_done(h - 1)
                    act.wait_ge(S("n_ptpsum"), H + (1 + SEED))
                    act.wait_ge(S("n_pv"), H + SEED)
                    nc.scalar.activation(PT1, ps[:, 6, :].rearrange("p (a n) -> p a n", a=2), ACT.Copy)
                    nc.scalar.activation(PT2[0:META], ps[0:META, 7, 0:S1], ACT.Copy).then_inc(S("n_pt"), 1)
                    if h == 7:
                        pair_done(h)
            act.wait_ge(acc_free, ST["o3"].p0 + SEED)
            for i in range(4):
                nc.scalar.activation(op(KT, S1)(i), op(KT, S1)(i), ACT.Silu).then_inc(S("z3_silu"), 1)
            split_op_act(act, "o3", op(QO, S1), op(MH, S1), 4, ST["z3"].end)
            side("o3")
            act.wait_ge(S("odd_done"), 8)
            norm_act(act, "fin2", op(RES, S1, off=META), S1)

        @block.vector
        def _(dve):
            v = Steps(dve, S("dve_step"))
            V = nc.vector

            def side(name, evac=None, **kw):
                stream_side(dve, "dve", name, evac, **kw)

            def one(name, chunks=1):
                for i in range(chunks):
                    halves(dve, "dve", ST[name], 0, i + 2)

            def tl(it, j, ppi=2, base=0):
                if isinstance(it, int):
                    return slice(2 * ppi * it + base + 2 * j, 2 * ppi * it + base + 2 * j + 2)
                return ds(it * (2 * ppi) + (base + 2 * j), 2)

            v.do(V.memset(small[:, :], 0.0))
            v.sync()
            for n in ("acc_free", "a_biased", "a_acc", "n_acc", "rows_used"):
                dve.sem_inc(S(n), SEED)
            halves(dve, "dve", ST["kvc"], 0, 0)
            halves(dve, "dve", ST["kvc"], 0, 1)
            for i in range(8):
                dve.wait_ge(S("xT_psum"), i + 1)
                V.tensor_copy(RES[:, 2 * i:2 * i + 2, META:T2],
                              ps[:, 4 + i % 4, :].rearrange("p (a n) -> p a n", a=2)).then_inc(S("xT_copied"), 1)
            for i in range(4):
                dve.wait_ge(S("pc_psum"), i + 1)
                V.tensor_copy(PC[:, 4 * i:4 * i + 4, :],
                              ps[:, 4 + i, 0:4 * NROW].rearrange("p (a n) -> p a n", a=4)).then_inc(S("pc_ready"), 1)
            dve.wait_ge(S("pc_ready"), 4)
            V.tensor_copy(RES[:, :, 0:META], PC[:, :, R_META:NROW]).then_inc(S("meta_ready"), 1)
            norm_dve(dve, v, "h1", S1, EPS1)
            apply_dve(dve, v, "h1", op(RES, S1, off=META), R_NORM, S1)

            def blocks(j):
                dve.wait_ge(S(f"w1_landed_{'kv'[j]}"), 96)
                if j:
                    dve.wait_ge(S("hid_summed"), 1)
                for half in range(2):
                    src = qkvT[:, 8 + 2 * j + half, :]
                    win = bass.AP(src.tensor, src.offset, [src.ap[0], [CMP_STRIDE, NC], [1, CMP_LEN]])
                    ins = V.tensor_tensor(KB[:, half], win, peT[:, j:j + 1, :].to_broadcast([P, NC, CMP_LEN]), ALU.add)
                ins.then_inc(S("kb_ready"), 1)

            side("kvc")
            dve.wait_ge(acc_free, ST["qa"].p0 + SEED)
            blocks(0)
            side("qa")
            blocks(1)
            side("qb")
            dve.wait_ge(S("kc_psum"), 1)
            for gg in range(GROUPS):
                o = HD * (gg % 2)
                for half in range(2):
                    ins = V.tensor_scalar(KCD[HD * half:HD * (half + 1), gg, :],
                                          ps[o:o + HD, 5, NC * (gg // 2):NC * (gg // 2 + 1)], HD ** -0.5, None, ALU.mult)
            ins.then_inc(S("kcd_ready"), 1)
            side("kvs")
            one("gate")
            dve.wait_ge(S("vc_psum"), 1)
            V.tensor_copy(VCN[0:NC, :], ps[0:NC, 5, 256:512]).then_inc(S("vcn_ready"), 1)
            dve.wait_ge(S("sc_psum"), 2)
            dve.wait_ge(S("masks_ready"), 1)
            for e in range(2):
                def heads_of(t):
                    return t.rearrange("p a (h e) n -> p a h e n", e=2)[:, :, :, e, :]
                v.do(V.tensor_tensor(heads_of(Pc), ps[:, (7, 6)[e], 0:240].rearrange("p (a h n) -> p a h n", a=2, h=8),
                                     heads_of(BC), ALU.add))
            v.sync()
            v.do(V.tensor_reduce(cmx, Pc.rearrange("p a h n -> p (a h) n"), AX.X, ALU.max))
            v.sync()
            Pc3 = Pc.rearrange("p a h n -> p (a h) n")
            V.tensor_tensor(Pc3, Pc3, cmx.unsqueeze(2).to_broadcast([P, 32, NC]), ALU.subtract).then_inc(S("cmp_shifted"), 1)
            dve.wait_ge(S("cmp_exp"), 1)
            v.do(V.tensor_reduce(cz, Pc3, AX.X, ALU.add))
            v.sync()
            v.do(V.reciprocal(cz, cz))
            v.do(V.tensor_tensor(Pc3, Pc3, MC.rearrange("p a h n -> p (a h) n"), ALU.mult))
            v.sync()
            dve.wait_ge(acc_free, ST["kvw"].p0 + SEED)
            v.do(V.tensor_tensor(cco.rearrange("p (a h) -> p a h", a=2), cz.rearrange("p (a h) -> p a h", a=2),
                                 gates[:, :, 0:HEADS], ALU.mult))
            v.sync()
            V.tensor_tensor(Pc3, Pc3, cco.unsqueeze(2).to_broadcast([P, 32, NC]), ALU.mult).then_inc(S("pc_norm"), 1)
            side("kvw")
            dve.wait_ge(acc_free, ST["za"].p0 + SEED)
            for br in range(2):
                for gg in range(GROUPS):
                    v.do(V.tensor_copy(KSg[0:HD, br, gg, :],
                                       qkvT[HD * (gg % 2):HD * (gg % 2) + HD, 12 + 4 * br + gg // 2, :]))
            for br in range(2):
                dve.wait_ge(S("vn1_psum"), br + 1)
                v.do(V.tensor_copy(Vn[:, br], ps[:, 4 + br, :].rearrange("p (a n) -> p a n", a=2)))
            v.sync()
            dve.wait_ge(S("oc_ready"), 4)
            dve.sem_inc(S("attn_in_ready"), 1)

            def attn_stage(G, r):
                dve.wait_ge(S("a_scores"), G * 8 + (2 * r - 2 + SEED))
                V.tensor_scalar(QSg[0:HD, r % 2, :],
                                qkvT[HD * (r % 2):HD * (r % 2) + HD, ds(G * 2 + r // 2, 1), :].rearrange("p a n -> p (a n)"),
                                HD ** -0.5, None, ALU.mult).then_inc(S("a_staged"), 1)

            def attn_soft(G, u):
                b = u % 2
                dve.wait_ge(S("a_scores"), G * 8 + (u + 1 + SEED))
                dve.wait_ge(S("a_exp"), G * 8 + (u - 1 + SEED))
                V.scalar_tensor_tensor(out=SCb[:, b, :], in0=DM, scalar=nslopes[:, ds(G * 4 + u // 2, 1)], in1=ps[:, 4 + b, 0:384],
                                       op0=ALU.mult, op1=ALU.add).then_inc(S("a_biased"), 1)
                dve.wait_ge(S("a_biased"), G * 8 + (u + 1 + SEED))
                V.tensor_reduce(small[:, 2 * b:2 * b + 1], SCb[:, b, 0:P], AX.X, ALU.max, negate=True)
                V.tensor_reduce(small[:, 2 * b + 1:2 * b + 2], SCb[:, b, P:384], AX.X, ALU.max, negate=True).then_inc(S("a_negmax"), 1)

            def attn_acc(G, u):
                b, r = u % 2, u // 2
                dve.wait_ge(S("a_exp"), G * 8 + (u + 1 + SEED))
                v.do(V.reciprocal(small[:, 12 + 2 * b:14 + 2 * b], small[:, 8 + 2 * b:10 + 2 * b]))
                v.sync()
                v.do(V.tensor_tensor(small[:, 12 + 2 * b:14 + 2 * b].unsqueeze(2), small[:, 12 + 2 * b:14 + 2 * b].unsqueeze(2),
                                     gates[:, :, ds(G * 4 + (HEADS * (1 + b) + r), 1)], ALU.mult))
                v.sync()
                dve.wait_ge(S("a_pv"), G * 8 + (u + 1 + SEED))
                for qb in range(2):
                    o = ON[:, qb, ds(G * 256 + HD * r, HD)]
                    ins = V.scalar_tensor_tensor(out=o, in0=ps[:, 7, HD * qb:HD * qb + HD],
                                                 scalar=small[:, 12 + 2 * b + qb:13 + 2 * b + qb], in1=o, op0=ALU.mult, op1=ALU.add)
                ins.then_inc(S("a_acc"), 1)

            with v.loop(0, GROUPS // 2, 32) as it:
                for gg in range(2):
                    G = Lin(it, 2, gg)
                    dve.wait_ge(S("a_scores"), G * 8 + SEED)
                    V.tensor_scalar(KST[0:HD], KSg[0:HD, :, ds(G + 0, 1), :].rearrange("p b a n -> p b (a n)"), 1.0, None, ALU.mult)
                    attn_stage(G, 0)
                    attn_stage(G, 1)
                    attn_soft(G, 0)
                    for u in range(8):
                        if u < 7:
                            attn_soft(G, u + 1)
                        if u % 2 == 0 and 1 <= u // 2 and u // 2 < 3:
                            attn_stage(G, u // 2 + 1)
                        attn_acc(G, u)
                        if u in (3, 7):
                            halves(dve, "dve", ST["za"], it, 2 * gg + 2 + u // 4)
            side("uv")
            dve.wait_ge(S("v_sum"), 1)
            v.do(V.tensor_scalar(ms[:, 0:S1], ps[:, 4, 0:S1], 1.0 / BW, None, ALU.mult))
            v.sync()
            V.tensor_tensor(Vv, Vv, ms[:, 0:S1].unsqueeze(1).to_broadcast([P, 8, S1]), ALU.subtract).then_inc(S("v_centred"), 1)
            for i in range(2):
                dve.wait_ge(S("wst_psum"), i + 1)
                V.tensor_tensor(WST[:, 4 * i:4 * i + 4, :], ps[:, 6 + i, :].rearrange("p (a n) -> p a n", a=4),
                                triF[:, :].unsqueeze(1).to_broadcast([P, 4, P]), ALU.mult).then_inc(S("wst_ready"), 1)
            side("zb")
            dve.wait_ge(acc_free, ST["merge"].p0 + SEED)
            dve.wait_ge(S("za_silu"), 1)
            for i in range(4):
                dve.wait_ge(S("oT_psum"), i + 1)
                V.tensor_tensor(ZA[:, 2 * i:2 * i + 2, :], ZA[:, 2 * i:2 * i + 2, :],
                                ps[:, i, :].rearrange("p (a n) -> p a n", a=2), ALU.mult).then_inc(S("oT_used"), 1)
            dve.wait_ge(S("v_var"), 1)
            V.tensor_scalar(ms[:, 0:S1], ps[:, 5, 0:S1], 1.0 / BW, EPS1, ALU.mult, ALU.add).then_inc(S("v_ms"), 1)
            dve.wait_ge(S("v_rt"), 1)
            v.do(V.reciprocal(rstd[:, 0:S1], rstd[:, 0:S1]))
            v.sync()
            for t in range(8):
                v.do(V.scalar_tensor_tensor(out=Vv[:, t, :], in0=Vv[:, t, :], scalar=PC[:, t, R_LNV:R_LNV + 1], in1=rstd[:, 0:S1],
                                            op0=ALU.mult, op1=ALU.mult))
            v.sync()
            for t in range(8):
                V.tensor_scalar(Vv[:, t, :], Vv[:, t, :], PC[:, 8 + t, R_LNV:R_LNV + 1], None, ALU.add).then_inc(S("v_normed"), 1)
            dve.wait_ge(S("sgb_landed"), 16)
            for i in range(4):
                dve.wait_ge(S("sv_psum"), i + 1)
                v.sync()
                m = ps[:, i, :].rearrange("p (a c n) -> p a c n", a=2, c=2)
                for k in range(2):
                    t = 2 * i + k
                    v.do(V.tensor_tensor(SGB2[:, k].rearrange("p (c n) -> p c n", c=2), m[:, k],
                                         SGB[:, t, :].unsqueeze(1).to_broadcast([P, 2, P]), ALU.add))
                v.do(V.tensor_tensor(UV[:, 2 * i:2 * i + 2, :], UV[:, 2 * i:2 * i + 2, :], ZB[:, 2 * i:2 * i + 2, :], ALU.mult))
                v.sync()
                v.do(V.tensor_tensor(ZB[:, 2 * i:2 * i + 2, :], UV[:, 2 * i:2 * i + 2, :], SGB2, ALU.mult))
            v.sync()
            dve.sem_inc(S("ob_ready"), 1)
            dve.sem_inc(src_ready, 8)
            side("merge")
            for gq in range(4):
                split_op_dve(dve, "oa1", op(ZA, S1, 2), op(MH, S1, 2), op(ML, S1, 2), gq)
            for gq in range(4):
                split_op_dve(dve, "ob1", op(ZB, S1, 2), op(MH, S1, 2, 8), op(ML, S1, 2, 8), gq)

            def up_a(it, j, par):
                g_ = GM[:, tl(it, j, 4), :]
                V.tensor_tensor(g_, g_, ps[:, pairof(par), 0:S1], ALU.mult).then_inc(acc_free, 1)

            def up_b(it, j, par):
                gb = GM[:, tl(it, j, 4, 16), :]
                ga = GM[:, tl(it, j, 4), :]
                V.tensor_tensor(gb, gb, ps[:, pairof(par), 0:S1], ALU.mult).then_inc(acc_free, 1)
                dve.wait_ge(acc_free, (it * 4 if not isinstance(it, int) else 4 * it) + ST["upb"].p0 + j + 1 + SEED)
                v.do(V.tensor_tensor(ga, ga, gb, ALU.add))

            side("upa", up_a)
            side("upb", up_b, steps=v, per=4)
            dve.wait_ge(S("pT_psum"), 1)
            V.tensor_copy(pT, ps[:, 4, :].rearrange("p (a n) -> p a n", a=2)).then_inc(src_ready, 1)
            split_op_dve(dve, "p", lambda gg: pT, lambda gg: PH, lambda gg: PL, 0)
            v.sync()
            dve.sem_inc(src_ready, 4)
            one("ple", 2)
            for gq in range(4):
                split_op_dve(dve, "merged", op(GM, S1), op(MH, S1), op(ML, S1), gq)

            def add_res(NT, off=0, name=None):
                def evac(it, j, par):
                    r = RES[:, tl(it, j), off:off + NT]
                    ins = V.tensor_tensor(r, r, ps[:, pairof(par), 0:NT], ALU.add).then_inc(acc_free, 1)
                return evac

            side("out1", add_res(S1, META))
            dve.wait_ge(acc_free, ST["pgate"].p0 + SEED)
            dve.sem_inc(src_ready, 4)
            for gq in range(4):
                split_op_dve(dve, "x1", op(RES, S1, off=META), op(MH, S1), op(ML, S1), gq)

            def ple_add(it, j, par):
                t = tl(it, j)
                dve.wait_ge(acc_free, it * 2 + ST["pgate"].p0 + j + 1 + SEED)
                v.do(V.tensor_tensor(PLEb[:, t, :], PLEb[:, t, :], G2[:, t, :], ALU.mult))
                v.sync()
                v.do(V.tensor_tensor(RES[:, t, META:T2], RES[:, t, META:T2], PLEb[:, t, :], ALU.add))

            side("pgate", ple_add, steps=v, per=4)
            v.sync()
            dve.sem_inc(S("x2_ready"), 1)
            norm_dve(dve, v, "fin1", S1, EPS1)
            for t in range(DT):
                ins = V.scalar_tensor_tensor(out=RES[:, t, META:T2], in0=RES[:, t, META:T2], scalar=PC[:, t, R_FINAL:R_FINAL + 1],
                                             in1=rstd[:, 0:S1], op0=ALU.mult, op1=ALU.mult)
                if t % 4 == 3:
                    ins.then_inc(S("block2_in"), 1)
            dve.wait_ge(S("block2_in"), 4)
            norm_dve(dve, v, "h2", T2, EPS2)
            apply_dve(dve, v, "h2", op(RES, T2), R_ENORM, T2)
            side("gv")

            def times(dst, name, NT, per=2, base=0):
                s = ST[name]

                def evac(it, j, par):
                    dve.wait_ge(acc_free, it * 2 + s.p0 + j + 1 + SEED)
                    d = dst[:, tl(it, j), 0:NT]
                    V.tensor_tensor(d, d, TMP[:, par, :, 0:NT], ALU.mult).then_inc(S("tmp_used"), 1)
                return evac

            one("dt")
            v.do(V.memset(sp[0], 0.0))
            v.do(V.memset(TRI, 1.0))
            dve.wait_ge(S("dt_params"), 32)
            dve.wait_ge(chunk_done, ST["dt"].end)
            v.sync()
            b = 2 * (ST["dt"].p0 % 2)
            v.do(V.tensor_tensor(sp[0][:, 0:2, :], ps[:, b, 0:128].rearrange("p (a n) -> p a n", a=2),
                                 dtb.unsqueeze(1).to_broadcast([P, 2, 2 * SH]), ALU.add))
            v.do(V.tensor_tensor(sp[0][0:META, 2, :], ps[0:META, b, 128:192], dtb[0:META], ALU.add))
            v.sync()
            dve.sem_inc(acc_free, 1)
            dve.sem_inc(S("dtr_ready"), 1)
            for i in range(3):
                for d, tri in enumerate((triF, triB)):
                    n = P if i < 2 else META
                    if d == 0 and i:
                        V.memset(TRI[:, 0, i, 0:P * i], 0.0)
                    if d == 1 and i < 2:
                        V.memset(TRI[:, 1, i, P * i + P:T2], 0.0)
                    v.do(V.tensor_copy(TRI[:, d, i, P * i:P * i + n], tri[:, 0:n]))
            dve.wait_ge(S("sp_exp"), 2)
            v.do(V.tensor_scalar(sp[2], sp[1], 2.0, None, ALU.add))
            v.sync()
            v.do(V.reciprocal(sp[2], sp[2]))
            v.sync()
            v.do(V.tensor_tensor(sp[2], sp[1], sp[2], ALU.mult))
            v.sync()
            v.do(V.tensor_tensor(sp[3], sp[2], sp[2], ALU.mult))
            v.sync()
            v.do(V.tensor_scalar(sp[4], sp[3], 1.0 / 19, None, ALU.mult))
            for k in range(8, 0, -1):
                v.sync()
                v.do(V.scalar_tensor_tensor(out=sp[4], in0=sp[4], scalar=1.0 / (2 * k + 1), in1=sp[3], op0=ALU.add, op1=ALU.mult))
            v.sync()
            v.do(V.scalar_tensor_tensor(out=sp[4], in0=sp[4], scalar=1.0, in1=sp[2], op0=ALU.add, op1=ALU.mult))
            v.do(V.tensor_scalar(sp[5], sp[0], 0.0, None, ALU.max))
            v.sync()
            v.do(V.scalar_tensor_tensor(out=dtN[:, :, :], in0=sp[4], scalar=2.0, in1=sp[5], op0=ALU.mult, op1=ALU.add))
            v.sync()
            v.do(V.scalar_tensor_tensor(out=aN, in0=dtN[:, :, :], scalar=-1.0, in1=alog.unsqueeze(1).to_broadcast([P, 3, 2 * SH]),
                                        op0=ALU.mult, op1=ALU.mult))
            v.sync()
            dve.sem_inc(S("a_nat_ready"), 1)
            side("gg", times(GU, "gg", T2))
            dve.wait_ge(S("tmp_used"), TMPC["gg"] + 8 + SEED)
            for d in range(2):
                dve.wait_ge(S("cum_psum"), d + 1)
                V.tensor_copy(CF[0:SH, d, :], ps[0:SH, 4 + d, 0:T2]).then_inc(S("cum_rows_ready"), 1)

            def conv5(name, half):
                def evac(it, j, par):
                    def col(k, c):
                        return PC[:, ds(it * 4 + (2 * j + k), 1), c:c + 1].rearrange("p a n -> p (a n)")

                    x = [ps[:, 2 * par + k, 0:T2] for k in range(2)]
                    o = [XBC[:, ds(it * 4 + (16 * half + 2 * j + k), 1), :].rearrange("p a n -> p (a n)") for k in range(2)]
                    for k in range(2):
                        v.do(V.tensor_scalar(o[k], x[k], col(k, R_CW + 4 + half), col(k, R_CB + half), ALU.mult, ALU.add))
                    for tap in (0, 1, 3, 4):
                        d = tap - 2
                        lo, hi = max(0, -d), T2 - max(0, d)
                        for k in range(2):
                            last = tap == 4 and k == 1
                            v.sync(0 if last else 1)
                            ins = V.scalar_tensor_tensor(out=o[k][:, lo:hi], in0=x[k][:, lo + d:hi + d], scalar=col(k, R_CW + 2 * tap + half),
                                                         in1=o[k][:, lo:hi], op0=ALU.mult, op1=ALU.add)
                            if last:
                                ins.then_inc(acc_free, 1)
                            else:
                                v.do(ins)
                return evac

            def conv31(tile, part):
                x = GU[:, tile, :].rearrange("p a n -> p (a n)")
                mid = K31 // 2

                def w(tap):
                    return PC[:, tile, R_DW + tap:R_DW + tap + 1].rearrange("p a n -> p (a n)")
                if part == 0:
                    v.sync()
                    v.do(V.memset(ACC[:, 1, T2 - 1:T2], 0.0))
                    v.do(V.tensor_scalar(ACC[:, 0, :], x, w(mid), PC[:, tile, R_DWB:R_DWB + 1].rearrange("p a n -> p (a n)"),
                                         ALU.mult, ALU.add))
                    v.do(V.tensor_scalar(ACC[:, 1, 0:T2 - 1], x[:, 1:T2], w(mid + 1), None, ALU.mult))
                taps = [k for k in range(K31) if k not in (mid, mid + 1)]
                cuts = (0, 6, 14, 22, 29)
                for n in range(cuts[part], cuts[part + 1]):
                    d = taps[n] - mid
                    lo, hi = max(0, -d), T2 - max(0, d)
                    v.sync(1)
                    v.do(V.scalar_tensor_tensor(out=ACC[:, n % 2, lo:hi], in0=x[:, lo + d:hi + d], scalar=w(taps[n]), in1=ACC[:, n % 2, lo:hi],
                                                op0=ALU.mult, op1=ALU.add))
                if part == 3:
                    v.sync()
                    v.do(V.tensor_tensor(x, ACC[:, 0, :], ACC[:, 1, :], ALU.add))
                    v.sync()
                    v.do(V.tensor_tensor(CSUM[:, :], CSUM[:, :], x, ALU.add))

            def conv_tile(base):
                return lambda it, i: conv31(ds(it + base, 1), i)

            v.do(V.memset(CSUM[:, :], 0.0))
            side("xs", conv5("xs", 0), steps=v, per=18 + 34, extra=conv_tile(0))
            dve.wait_ge(S("cn_psum"), 1)
            v.do(V.tensor_copy(cN[:, 0:2, :], ps[:, 6, 0:128].rearrange("p (a n) -> p a n", a=2)))
            v.do(V.tensor_copy(cN[0:META, 2, :], ps[0:META, 6, 128:192]))
            v.sync()
            dve.sem_inc(S("tri_free"), 1)

            side("bc", conv5("bc", 1), steps=v, per=18 + 34, extra=conv_tile(4))
            dve.wait_ge(acc_free, ST["zb2"].p0 + SEED)
            v.sync()
            dve.wait_ge(S("d_landed"), 32)

            def seg(G, h):
                b, hp = h % 2, h // 2
                dve.wait_ge(S(f"rows_landed_{hp}"), G * 16 + 16)
                dve.wait_ge(S("y_psum"), G * 4 + (h - 1 + SEED))
                for i, (d, st, lo, hi, at) in enumerate(SSD_COLS):
                    n = P if st < 2 else META
                    ins = V.tensor_scalar(SEG[0:n, b, at:at + hi - lo], ROWS[0:n, hp, d, h % 2, lo:hi],
                                          cN[0:n, st, ds(G * 4 + (SH * d + h), 1)], 0.0, ALU.subtract, ALU.min)
                ins.then_inc(S("seg_ready"), 1)

            def weigh(G, h, cols=SSD_COLS):
                b = h % 2
                if cols[0] == SSD_COLS[0]:
                    dve.wait_ge(S("seg_exp"), G * 4 + (h + 1))
                    dve.sem_inc(S("rows_used"), 1)
                for i, (d, st, lo, hi, at) in enumerate(cols):
                    n = P if st < 2 else META
                    sg = SEG[0:n, b, at:at + hi - lo]
                    ins = V.scalar_tensor_tensor(out=sg, in0=sg, scalar=dtN[0:n, st, ds(G * 4 + (SH * d + h), 1)],
                                                 in1=CBM[0:n, at:at + hi - lo], op0=ALU.mult, op1=ALU.mult)
                if cols[-1] == SSD_COLS[-1]:
                    ins.then_inc(S("w_ready"), 1)

            def y_tile(G, k):
                dve.wait_ge(S("y_psum"), G * 4 + (2 * k + 2 + SEED))
                t = ds(G * 2 + k, 1)
                xt = XS[:, t, :].rearrange("p a n -> p (a n)")
                V.scalar_tensor_tensor(out=xt, in0=xt, scalar=Dcol[:, t], in1=ps[:, 4 + k, 0:T2],
                                       op0=ALU.mult, op1=ALU.add).then_inc(S("y_used"), 1)

            dve.wait_ge(S("xbc_ready"), 10)
            with v.loop(0, SG // 2, 2 * 6) as it:
                for gg in range(2):
                    G = Lin(it, 2, gg)
                    seg(G, 0)
                    seg(G, 1)

                    def masked_cb(cols):
                        for d, st, lo, hi, at in cols:
                            n = P if st < 2 else META
                            dlo, dn = P * st, n
                            src = ps[0:n, (6, 7, 5)[st], :]
                            m = (triF, triB)[d]
                            if hi - lo > dn:
                                rest = (lo + dn, hi) if d == 0 else (lo, dlo)
                                V.tensor_copy(CBM[0:n, at + rest[0] - lo:at + rest[1] - lo], src[:, rest[0]:rest[1]])
                            v.do(V.tensor_tensor(CBM[0:n, at + dlo - lo:at + dlo - lo + dn], src[:, dlo:dlo + dn], m[0:n, 0:dn], ALU.mult))
                        v.sync()

                    dve.wait_ge(S("cb_psum"), G * 2 + 1)
                    masked_cb(SSD_COLS[0:4])
                    weigh(G, 0, SSD_COLS[0:4])
                    dve.wait_ge(S("cb_psum"), G * 2 + 2)
                    masked_cb(SSD_COLS[4:6])
                    weigh(G, 0, SSD_COLS[4:6])
                    weigh(G, 1)
                    seg(G, 2)
                    seg(G, 3)
                    halves(dve, "dve", ST["zb2"], it, 2 * gg + 2)
                    weigh(G, 2)
                    weigh(G, 3)
                    y_tile(G, 0)
                    y_tile(G, 1)
                    halves(dve, "dve", ST["zb2"], it, 2 * gg + 3)
            dve.wait_ge(S("y_used"), 2 * SG + SEED)
            V.memset(TAB[0:SH], 0.0).then_inc(S("tab_zeroed"), 1)
            side("z2", times(XS, "z2", T2), steps=v, per=34, extra=conv_tile(8))
            norm_dve(dve, v, "ya", T2, EPS2)
            apply_dve(dve, v, "ya", op(XS, T2), R_SSD, T2, dst=op(XS, T2))
            side("oa", add_res(T2), steps=v, per=34, extra=conv_tile(12))
            dve.wait_ge(S("zb2_silu"), 1)
            v.sync()
            dve.sem_inc(S("conv31_done"), 1)
            dve.wait_ge(S("cf_sum"), 1)
            v.do(V.tensor_scalar(ms[:, :], ps[:, 5, 0:T2], 1.0 / D, None, ALU.mult))
            v.sync()
            for gq in range(4):
                gu = op(GU, T2)(gq)
                V.tensor_tensor(gu, gu, ms[:, :].unsqueeze(1).to_broadcast([P, 4, T2]), ALU.subtract).then_inc(S("cf_centred"), 1)
            norm_dve(dve, v, "cf", T2, EPS2)
            for gq in range(6):
                if gq < 4:
                    for t in range(4 * gq, 4 * gq + 4):
                        ins = V.scalar_tensor_tensor(out=GU[:, t, :], in0=GU[:, t, :], scalar=PC[:, t, R_LNG:R_LNG + 1], in1=rstd[:, :],
                                                     op0=ALU.mult, op1=ALU.mult)
                    ins.then_inc(S("cf_scaled"), 1)
                if 1 <= gq < 5:
                    dve.wait_ge(S("cf_silu"), gq)
                    gu = op(GU, T2)(gq - 1).rearrange("p (i h) n -> p i h n", h=2)
                    V.tensor_tensor(gu, gu, ZB2.rearrange("p (h i) n -> p i h n", h=2)[:, 2 * gq - 2:2 * gq], ALU.mult).then_inc(src_ready, 1)
                if gq >= 2:
                    split_op_dve(dve, "yb", op(GU, T2), op(MH, T2), op(ML, T2), gq - 2)
            side("ob", add_res(T2))
            dve.wait_ge(acc_free, ST["v"].p0 + SEED)
            dve.sem_inc(S("even_done"), 8)
            norm_dve(dve, v, "h3", T2, EPS2)
            apply_dve(dve, v, "h3", op(RES, T2), R_ONORM, T2)
            side("v")
            side("k")
            side("q")
            def stage(it, h):
                half, e, G, H = slice(HD * (h % 2), HD * (h % 2) + HD), h % 2, Lin(it, 4, h // 2), Lin(it, 8, h)
                dve.wait_ge(S("n_scores"), H + (SEED - 1))
                V.tensor_scalar(QS[0:HD, e, :], QO[half, ds(G + 0, 1), :].rearrange("p a n -> p (a n)"), 1.0, None, ALU.mult)
                V.tensor_scalar(KS[0:HD, e, :], KT[half, ds(G + 0, 1), :].rearrange("p a n -> p (a n)"), 1.0, None, ALU.mult) \
                    .then_inc(S("n_staged"), 1)

            def soft(it, h):
                e, H = h % 2, Lin(it, 8, h)
                dve.wait_ge(S("n_scores"), H + (1 + SEED))
                dve.wait_ge(S("bias_ready"), H + 1)
                dve.wait_ge(S("n_ptpsum"), H + (SEED - 1))
                V.tensor_tensor(SO[:, e], BIAS[:, e], ps[:, 4:6, 0:T2], ALU.add).then_inc(S("bias_used"), 1)
                dve.wait_ge(S("bias_used"), H + (1 + SEED))
                V.tensor_reduce(small[:, 16 + 2 * e:18 + 2 * e], SO[:, e], AX.X, ALU.max, negate=True).then_inc(S("n_negmax"), 1)

            def acc(it, h):
                e, H, G = h % 2, Lin(it, 8, h), Lin(it, 4, h // 2)
                dve.wait_ge(S("n_exp"), H + 1)
                v.do(V.reciprocal(small[:, 24 + 2 * e:26 + 2 * e], small[:, 20 + 2 * e:22 + 2 * e]))
                v.sync()
                dve.wait_ge(S("n_pv"), H + (1 + SEED))
                for qt in range(2):
                    o = QO[:, ds(G + 0, 1), P * qt + HD * e:P * qt + HD * e + HD].rearrange("p a n -> p (a n)")
                    ins = V.tensor_scalar(o, ps[:, 7, S1 + 128 * e + HD * qt:S1 + 128 * e + HD * qt + HD], small[:, 24 + 2 * e + qt:25 + 2 * e + qt],
                                          None, ALU.mult)
                    if qt == 0:
                        v.do(ins)
                ins.then_inc(S("n_acc"), 1)

            with v.loop(0, ST["z3"].its, 16) as it:
                stage(it, 0)
                stage(it, 1)
                soft(it, 0)
                for h in range(8):
                    if h < 7:
                        soft(it, h + 1)
                    if h < 6:
                        stage(it, h + 2)
                    acc(it, h)
                    if h % 2 == 1:
                        halves(dve, "dve", ST["z3"], it, h // 2 + 2)
            for i in range(8):
                dve.wait_ge(S("oT3_psum"), i + 1)
                dve.wait_ge(S("z3_silu"), i // 2 + 1)
                V.tensor_tensor(QO[:, 2 * i:2 * i + 2, :], KT[:, 2 * i:2 * i + 2, 0:S1], ps[:, 4 + i % 4, :].rearrange("p (a n) -> p a n", a=2),
                                ALU.mult).then_inc(S("oT3_ready"), 1)
            dve.wait_ge(S("oT3_ready"), 8)
            dve.sem_inc(src_ready, 4)
            for gq in range(4):
                split_op_dve(dve, "o3", op(QO, S1), op(MH, S1), op(ML, S1), gq)
            side("o3", add_res(S1, META))
            dve.wait_ge(acc_free, ST["o3"].p0 + 8 + SEED)
            dve.sem_inc(S("odd_done"), 8)
            norm_dve(dve, v, "fin2", S1, EPS2)
            for t in range(DT):
                V.scalar_tensor_tensor(out=XF[:, t, :], in0=RES[:, t, META:T2], scalar=PC[:, t, R_FNORM:R_FNORM + 1],
                                       in1=rstd[:, 0:S1], op0=ALU.mult, op1=ALU.mult).then_inc(S("xf_ready"), 1)
            for i in range(8):
                dve.wait_ge(S("out_psum"), i + 1)
                V.tensor_copy(onat[:, i % 2, 512 * (i // 2):512 * (i // 2) + 512], ps[:, 4 + i % 4, :]).then_inc(S("out_ready"), 1)

        @block.tensor
        def _(pe):
            T = nc.tensor
            pe.wait_ge(S("consts_ready"), 3)
            pe.wait_ge(S("x_landed"), 16)
            for i in range(8):
                if i >= 4:
                    pe.wait_ge(S("xT_copied"), i - 3)
                for k in range(2):
                    for tt in range(2):
                        mm = T.transpose(ps[:, 4 + i % 4, 256 * k + P * tt:256 * k + P * tt + P],
                                         xnat[:, tt, (2 * i + k) * P:(2 * i + k + 1) * P], ident[:, :])
                mm.then_inc(S("xT_psum"), 1)
            pe.wait_ge(S("params_landed"), 15 * 16)
            for i in range(4):
                pe.wait_ge(S("xT_copied"), 5 + i)
                for k in range(4):
                    mm = T.transpose(ps[:, 4 + i, NROW * k:NROW * (k + 1)], PR[0:NROW, (4 * i + k) * P:(4 * i + k + 1) * P],
                                     ident[0:NROW, 0:NROW])
                mm.then_inc(S("pc_psum"), 1)
            pe.wait_ge(S("pc_ready"), 4)
            norm_pe(pe, "h1", S1)
            def hidden(j):
                pe.wait_ge(S("kb_ready"), j + 1)
                for l in range(CMP_LEN):
                    mm = T.matmul(ps[:, 4, 0:2 * NC].rearrange("p (a n) -> p a n", a=2), W1[j][:, l, :], KB[:, :, :, l],
                                  start=(l == 0), stop=(l == CMP_LEN - 1))
                mm.then_inc(S("hid_summed"), 1)

            stream_pe(pe, "kvc", need="h1")
            stream_pe(pe, "qa")
            hidden(0)
            stream_pe(pe, "qb")
            pe.wait_ge(S("hid_ready"), 1)
            T.matmul(ps[:, 5, 0:2 * NC], W2[0], hid.rearrange("p a n -> p (a n)"), start=True, stop=True).then_inc(S("kc_psum"), 1)
            hidden(1)
            stream_pe(pe, "kvs")
            pe.wait_ge(S("hid_ready"), 2)
            pe.wait_ge(S("kcd_ready"), 1)
            for a_ in range(2):
                mm = T.matmul(ps[0:NC, 5, 256 + P * a_:256 + P * a_ + P], hid[:, a_, :], W2[1], start=True, stop=True)
            mm.then_inc(S("vc_psum"), 1)
            for qb in range(2):
                for h in range(HEADS):
                    o = HD * (h % 2)
                    at = (HEADS // 2 * qb + h // 2) * NC
                    mm = T.matmul(ps[:, 6 if h % 2 else 7, at:at + NC],
                                  qkvT[o:o + HD, h // 2, P * qb:P * qb + P], KCD[o:o + HD, h // 4, :], start=True, stop=True)
                    if qb == 1 and h >= HEADS - 2:
                        mm.then_inc(S("sc_psum"), 1)
            natural(pe, "gate", [(0, P), (P, P)], 3 * HEADS)
            stream_pe(pe, "kvw")
            pe.wait_ge(S("pc_norm"), 1)
            for half in range(2):
                for qb in range(2):
                    mm = T.transpose(ps[0:120, 6, (2 * half + qb) * P:(2 * half + qb + 1) * P],
                                     Pc[:, qb, 8 * half:8 * half + 8, :].rearrange("p h n -> p (h n)"), ident[:, :])
            mm.then_inc(S("pct_psum"), 1)
            pe.wait_ge(S("pct_ready"), 1)
            pe.wait_ge(S("vcb_landed"), 16 * HEADS)
            pe.wait_ge(S("vcn_ready"), 1)
            for qb in range(2):
                for half in range(2):
                    if qb:
                        pe.wait_ge(S("oc_ready"), half + 1)
                    T.matmul(ps[:, 4 + half, :], PcT[0:120, half, qb, :], VCB[0:120, half, :], start=True,
                             stop=True).then_inc(S("oc_psum"), 1)
            pe.wait_ge(S("oc_ready"), 4)
            pe.wait_ge(acc_free, ST["za"].p0 + SEED)
            for br in range(2):
                for tt in range(2):
                    for j in range(2):
                        mm = T.transpose(ps[:, 4 + br, 256 * tt + P * j:256 * tt + P * j + P],
                                         qkvT[:, 14 + 4 * br + j, P * tt:P * tt + P], ident[:, :])
                mm.then_inc(S("vn1_psum"), 1)
            pe.wait_ge(S("attn_in_ready"), 1)
            for n in ("a_scores", "a_exp", "a_ptpsum", "a_pt", "a_pv", "y_psum", "n_scores", "n_pv", "n_ptpsum", "n_pt", "y_used"):
                pe.sem_inc(S(n), SEED)

            def a_scores(G, u):
                b, r = u % 2, u // 2
                pe.wait_ge(S("a_staged"), G * 4 + (r + 1))
                pe.wait_ge(S("a_biased"), G * 8 + (u - 1 + SEED))
                for qb in range(2):
                    n = P * (qb + 1)
                    mm = T.matmul(ps[:, 4 + b, P * qb:P * qb + n], QSg[0:HD, r % 2, P * qb:P * qb + P],
                                  KST[0:HD, b, 0:n], start=True, stop=True)
                mm.then_inc(S("a_scores"), 1)

            def a_rest(G, u):
                b = u % 2
                pe.wait_ge(S("a_exp"), G * 8 + (u + 1 + SEED))
                pe.wait_ge(S("a_pt"), G * 8 + (u + SEED))
                for k in range(3):
                    mm = T.transpose(ps[:, 6, P * k:P * k + P], Eb[:, b, P * k:P * k + P], ident[:, :])
                mm.then_inc(S("a_ptpsum"), 1)
                pe.wait_ge(S("a_pt"), G * 8 + (u + 1 + SEED))
                pe.wait_ge(S("a_acc"), G * 8 + (u + SEED))
                for o, blocks in ((0, [(0, 0)]), (HD, [(1, 0), (2, 1)])):
                    for k, (blk, tt) in enumerate(blocks):
                        mm = T.matmul(ps[:, 7, o:o + HD], PTb[:, b, P * blk:P * blk + P], Vn[:, b, tt, ds(G * HD + 0, HD)],
                                      start=(k == 0), stop=(k == len(blocks) - 1))
                mm.then_inc(S("a_pv"), 1)

            with pe.Fori(0, GROUPS // 2) as it:
                for gg in range(2):
                    G = Lin(it, 2, gg)
                    a_scores(G, 0)
                    for u in range(8):
                        if u < 7:
                            a_scores(G, u + 1)
                        if u % 2 == 0:
                            multiply(pe, ST["za"], it, 2 * gg + u // 4, u // 2 % 2, S1)
                        a_rest(G, u)
            pe.wait_ge(S("a_acc"), 2 * HEADS + SEED)
            stream_pe(pe, "uv")
            pe.wait_ge(acc_free, ST["zb"].p0 + SEED)
            for t in range(8):
                mm = T.matmul(ps[:, 4, 0:S1], ones[:, :], Vv[:, t, :], start=(t == 0), stop=(t == 7))
            mm.then_inc(S("v_sum"), 1)
            pe.wait_ge(S("ws_landed"), 16)
            for i in range(2):
                for k in range(4):
                    mm = T.transpose(ps[:, 6 + i, P * k:P * k + P], WS[:, 4 * i + k, :], ident[:, :])
                mm.then_inc(S("wst_psum"), 1)
            stream_pe(pe, "zb")
            pe.wait_ge(S("v_sq"), 1)
            for t in range(8):
                mm = T.matmul(ps[:, 5, 0:S1], ones[:, :], SQv[:, t, :], start=(t == 0), stop=(t == 7))
            mm.then_inc(S("v_var"), 1)
            pe.wait_ge(acc_free, ST["merge"].p0 + SEED)
            for i in range(4):
                for k in range(2):
                    for qb in range(2):
                        mm = T.transpose(ps[:, i, 256 * k + P * qb:256 * k + P * qb + P],
                                         ON[:, qb, (2 * i + k) * P:(2 * i + k + 1) * P], ident[:, :])
                mm.then_inc(S("oT_psum"), 1)
            pe.wait_ge(S("v_normed"), 8)
            pe.wait_ge(S("wst_ready"), 2)
            for i in range(4):
                for k in range(4):
                    mm = T.transpose(ps[:, 4 + i, P * k:P * k + P], Vv[:, 4 * (i % 2) + k, P * (i // 2):P * (i // 2) + P], ident[:, :])
                mm.then_inc(S("vn_psum"), 1)
            pe.wait_ge(S("vn_ready"), 4)
            pe.wait_ge(S("oT_used"), 4)
            for i in range(4):
                for k in range(2):
                    for c in range(2):
                        mm = T.matmul(ps[:, i, 256 * k + P * c:256 * k + P * c + P], VN[:, c, 2 * i + k, :], WST[:, 2 * i + k, :],
                                      start=True, stop=True)
                mm.then_inc(S("sv_psum"), 1)
            pe.wait_ge(S("ob_ready"), 1)
            stream_pe(pe, "merge")
            pe.wait_ge(S("p_landed"), 16)
            for k in range(2):
                for tt in range(2):
                    mm = T.transpose(ps[:, 4, 256 * k + P * tt:256 * k + P * tt + P], pnat[:, tt, P * k:P * k + P], ident[:, :])
            mm.then_inc(S("pT_psum"), 1)
            stream_pe(pe, "upa", need="oa1")
            stream_pe(pe, "upb", tile0=8, need="ob1")
            s = ST["ple"]
            pe.wait_ge(ml_ready, sum(SPL["p"]))
            for i in range(2):
                c = s.c0 + i
                lo_wait(pe, s.c0, 0, i)
                wh = whi[c % 2][:, :].rearrange("p (t n) -> p t n", t=2)
                wl = wlo[c % 2][:, :].rearrange("p (t n) -> p t n", t=2)
                for j in range(4):
                    pr = 4 * i + j
                    pe.wait_ge(acc_free, s.p0 + pr - 1 + SEED)
                    for n in range(2):
                        o = ps[:, 2 * ((s.p0 + pr) % 2) + n, 0:S1]
                        cc = slice((2 * j + n) * P, (2 * j + n + 1) * P)
                        for k in range(2):
                            T.matmul(o, wh[:, k, cc], PH[:, k, :], start=(k == 0), stop=False)
                            T.matmul(o, wh[:, k, cc], PL[:, k, :], start=False, stop=False)
                            mm = T.matmul(o, wl[:, k, cc], PH[:, k, :], start=False, stop=(k == 1))
                    mm.then_inc(S("ple_psum"), 1)
                pe.wait_ge(S("ple_psum"), 4 * i + 4)
                pe.sem_inc(chunk_done, 1)
            stream_pe(pe, "out1", need="merged")
            stream_pe(pe, "pgate", need="x1")
            norm_pe(pe, "fin1", S1)
            norm_pe(pe, "h2", T2)
            stream_pe(pe, "gv", NT=T2, need="h2")
            natural(pe, "dt", [(0, P), (P, P), (2 * P, META)], 2 * SH)
            stream_pe(pe, "gg", NT=T2)
            pe.wait_ge(S("a_nat_ready"), 1)
            for d in range(2):
                for i in range(3):
                    n = P if i < 2 else META
                    mm = T.matmul(ps[0:SH, 4 + d, 0:T2], aN[0:n, i, SH * d:SH * d + SH], TRI[0:n, d, i, :], start=(i == 0), stop=(i == 2))
                mm.then_inc(S("cum_psum"), 1)
            stream_pe(pe, "xs", NT=T2)
            pe.wait_ge(S("cum_rows_ready"), 2)
            for d in range(2):
                for i in range(3):
                    n = P if i < 2 else META
                    mm = T.transpose(ps[0:n, 6, 64 * i + SH * d:64 * i + SH * d + SH], CF[0:SH, d, P * i:P * i + n], ident[0:SH, 0:SH])
            mm.then_inc(S("cn_psum"), 1)
            stream_pe(pe, "bc", NT=T2)
            s = ST["zb2"]
            with pe.Fori(0, SG // 2) as it:
                for gg in range(2):
                    G = Lin(it, 2, gg)
                    multiply(pe, s, it, 2 * gg, 0, T2)
                    pe.wait_ge(S("staged"), G + 1)

                    def cb(i):
                        n = P if i < 2 else META
                        return T.matmul(ps[0:n, (6, 7, 5)[i], 0:T2], BS[:, P * i:P * i + n], CS, start=True, stop=True)

                    cb(0)
                    cb(1).then_inc(S("cb_psum"), 1)
                    pe.wait_ge(S("y_used"), G * 2 + SEED)
                    for i in range(3):
                        n = P if i < 2 else META
                        for k in range(2):
                            o = ps[0:n, 4, 256 * i + P * k:256 * i + P * k + P] if i < 2 else ps[0:n, 5, P * k:P * k + P]
                            mm = T.transpose(o, XST[:, k, P * i:P * i + n], ident[:, :])
                    mm.then_inc(S("x_psum"), 1)
                    pe.wait_ge(S("xnat_ready"), G + 1)
                    cb(2).then_inc(S("cb_psum"), 1)
                    for h in range(4):
                        for i in {0: (1,), 2: (2, 3)}.get(h, ()):
                            multiply(pe, s, it, 2 * gg + i // 2, i % 2, T2)
                        pe.wait_ge(S("w_ready"), G * 4 + (h + 1))
                        o = HD * (h % 2)
                        for i, (d, st, lo, hi, at) in enumerate(SSD_COLS):
                            n = P if st < 2 else META
                            mm = T.matmul(ps[o:o + HD, 4 + h // 2, lo:hi], XNAT[0:n, st, HD * h:HD * h + HD], SEG[0:n, h % 2, at:at + hi - lo],
                                          start=(i == 0), stop=(i == len(SSD_COLS) - 1))
                        mm.then_inc(S("y_psum"), 1)
            stream_pe(pe, "z2", NT=T2)
            norm_pe(pe, "ya", T2)
            stream_pe(pe, "oa", NT=T2, need="ya")
            pe.wait_ge(S("conv31_done"), 1)
            mm = T.matmul(ps[:, 5, 0:T2], ones[:, :], CSUM[:, :], start=True, stop=True)
            mm.then_inc(S("cf_sum"), 1)
            norm_pe(pe, "cf", T2)
            stream_pe(pe, "ob", NT=T2, need="yb")
            norm_pe(pe, "h3", T2)
            stream_pe(pe, "v", NT=T2, need="h3")
            pe.wait_ge(acc_free, ST["k"].p0 + SEED)
            for i in range(12):
                tq, kt = i // 3, i % 3
                n = P if kt < 2 else META
                if i >= 4:
                    pe.wait_ge(S("vo_ready"), i - 3)
                for k in range(4):
                    mm = T.transpose(ps[0:n, 4 + i % 4, P * k:P * k + P], KT[:, 4 * tq + k, P * kt:P * kt + n], ident[:, :])
                mm.then_inc(S("vo_psum"), 1)
            pe.wait_ge(S("vo_ready"), 12)
            stream_pe(pe, "k", NT=T2)
            stream_pe(pe, "q", NT=S1, off=META)
            pe.wait_ge(acc_free, ST["z3"].p0 + SEED)

            def n_scores(it, h):
                e, H = h % 2, Lin(it, 8, h)
                pe.wait_ge(S("n_staged"), H + 1)
                pe.wait_ge(S("bias_used"), H + SEED)
                for qt in range(2):
                    mm = T.matmul(ps[:, 4 + qt, 0:T2], QS[0:HD, e, P * qt:P * qt + P], KS[0:HD, e, :], start=True, stop=True)
                mm.then_inc(S("n_scores"), 1)

            def n_transposes(it, h):
                e, H = h % 2, Lin(it, 8, h)
                pe.wait_ge(S("n_exp"), H + 1)
                pe.wait_ge(S("n_pt"), H + SEED)
                pe.wait_ge(S("n_acc"), H + SEED)
                for qt in range(2):
                    for kt in range(3):
                        n = P if kt < 2 else META
                        o = ps[0:n, 6, S1 * kt + P * qt:S1 * kt + P * qt + P] if kt < 2 else ps[0:n, 7, P * qt:P * qt + P]
                        mm = T.transpose(o, SO[:, e, qt, P * kt:P * kt + n], ident[:, :])
                mm.then_inc(S("n_ptpsum"), 1)

            def n_sums(it, h):
                e, H, G = h % 2, Lin(it, 8, h), Lin(it, 4, h // 2)
                pe.wait_ge(S("n_pt"), H + (1 + SEED))
                for qt in range(2):
                    for kt in range(3):
                        n = P if kt < 2 else META
                        w = PT1[:, kt, P * qt:P * qt + P] if kt < 2 else PT2[0:META, P * qt:P * qt + P]
                        at = S1 + 128 * e + HD * qt
                        mm = T.matmul(ps[:, 7, at:at + HD], w, VO[0:n, kt, ds(G * P + HD * e, HD)],
                                      start=(kt == 0), stop=(kt == 2))
                mm.then_inc(S("n_pv"), 1)

            with pe.Fori(0, ST["z3"].its) as it:
                n_scores(it, 0)
                for h in range(8):
                    if h < 7:
                        n_scores(it, h + 1)
                    n_transposes(it, h)
                    multiply(pe, ST["z3"], it, h // 2, h % 2, S1, off=META)
                    n_sums(it, h)
            pe.wait_ge(S("n_acc"), SH + SEED)
            for i in range(8):
                if i >= 4:
                    pe.wait_ge(S("oT3_ready"), i - 3)
                for k in range(2):
                    for qt in range(2):
                        mm = T.transpose(ps[:, 4 + i % 4, 256 * k + P * qt:256 * k + P * qt + P], QO[:, 2 * i + k, P * qt:P * qt + P], ident[:, :])
                mm.then_inc(S("oT3_psum"), 1)
            stream_pe(pe, "o3", NT=S1, need="o3")
            norm_pe(pe, "fin2", S1)
            for i in range(8):
                pe.wait_ge(S("xf_ready"), 4 * (i // 2) + 4)
                if i >= 4:
                    pe.wait_ge(S("out_ready"), i - 3)
                for k in range(4):
                    mm = T.transpose(ps[:, 4 + i % 4, P * k:P * k + P], XF[:, 4 * (i // 2) + k, P * (i % 2):P * (i % 2) + P], ident[:, :])
                mm.then_inc(S("out_psum"), 1)


_INS = ["x", "p", "norm_g", "w_in", "cmp_pe_k", "cmp_w1_k", "cmp_w2_k", "cmp_pe_v", "cmp_w1_v", "cmp_w2_v", "ln_v_g",
        "ln_v_b", "sgu_w", "sgu_b", "w_up_a", "w_up_b", "w_out", "w_ple", "w_ple_gate", "final_g", "meta_tokens_2",
        "e_norm_g_2", "e_w_in_2", "e_conv_w_2", "e_conv_b_2", "e_dt_bias_2", "e_A_log_2", "e_D_2", "e_ssd_norm_g_2",
        "e_dw_w_2", "e_dw_b_2", "e_ln_g_2", "e_ln_b_2", "e_w_out_2", "o_norm_g_2", "o_w_in_2", "o_rpb_2", "o_w_out_2",
        "final_norm_g_2"]


def kernel(**inputs):
    import numpy as np
    import concourse.bacc as bacc
    from concourse.bass_utils import run_bass_kernel_spmd

    nc = bacc.Bacc("TRN2", target_bir_lowering=False, num_devices=1)
    arrays, aps = {}, {}
    for name in _INS:
        a = np.ascontiguousarray(inputs[name])
        arrays[f"in_{name}_dram"] = a
        aps[name] = nc.dram_tensor(f"in_{name}_dram", a.shape, mybir.dt.from_np(a.dtype), kind="ExternalInput").ap()
    out = nc.dram_tensor("out_0_dram", (1, S1, D), F, kind="ExternalOutput").ap()
    build(nc, aps, out)
    r = run_bass_kernel_spmd(nc, [arrays], core_ids=[0])
    return r.results[0]["out_0_dram"]
```
